# Optimizing a Trainium2 kernel written in Bass

```python
import jax
import jax.numpy as jnp
from jax import lax
import numpy as np
import math
import jax, jax.numpy as jnp

D_MODEL = 1024
BATCH = 1
SEQ = 256
DEPTH = 2

D_MIX = 1024
M_HEADS = 4
M_HEAD_DIM = 96
M_WIDTH = M_HEADS * M_HEAD_DIM
M_CHUNK = 128
CONV_WIDTH = 4
A_HEADS = 6
A_NOPE = 64
A_ROPE = 32
A_QK_DIM = A_NOPE + A_ROPE
A_V_DIM = 64
A_WIDTH = A_HEADS * A_V_DIM
A_Q_RANK = 256
A_KV_RANK = 128
ROPE_THETA = 10000.0
Q_BLOCK = 128
C_GROUPS = 4
C_GROUP_DIM = 64
C_WIDTH = C_GROUPS * C_GROUP_DIM
C_CHUNK = 128
IN_SIZES = (M_WIDTH, M_WIDTH, M_WIDTH, M_WIDTH, M_HEADS, M_HEADS,
            A_Q_RANK, A_KV_RANK, A_ROPE, C_WIDTH, C_WIDTH)
D_IN = 4 * M_WIDTH + 2 * M_HEADS + A_Q_RANK + A_KV_RANK + A_ROPE + 2 * C_WIDTH
N_GROUPS = 4
EXPERTS_PER_GROUP = 8
N_EXPERTS = N_GROUPS * EXPERTS_PER_GROUP
TOP_K = 2
D_EXPERT = 256
MOE_BLOCK = 256
EPS = 1e-6


def rms_norm(x, gain):
    xf = x.astype(jnp.float32)
    y = xf * lax.rsqrt(jnp.mean(xf * xf, axis=-1, keepdims=True) + EPS)
    return (y * gain.astype(jnp.float32)).astype(x.dtype)

def head_rms_norm(x, gain, n_heads):
    b, s, w = x.shape
    y = rms_norm(x.reshape(b, s, n_heads, w // n_heads), gain.reshape(n_heads, w // n_heads))
    return y.reshape(b, s, w)

def split_cols(t, sizes):
    out, off = [], 0
    for size in sizes:
        out.append(t[..., off:off + size])
        off += size
    return out

def causal_depthwise_conv(x, w, b):
    width, seq = w.shape[0], x.shape[1]
    xp = jnp.pad(x, ((0, 0), (width - 1, 0), (0, 0)))
    y = b
    for j in range(width):
        y = y + xp[:, j:j + seq] * w[j]
    return y

def mlstm_chunkwise(q, k, v, i_pre, f_pre):
    B, S, H, Dh = q.shape
    L = M_CHUNK
    N = S // L
    f32 = jnp.float32
    def to_chunks(t):
        return t.astype(f32).reshape(B, N, L, H, -1).transpose(1, 0, 3, 2, 4)
    qc = to_chunks(q)
    kc = to_chunks(k) * (Dh ** -0.5)
    vc = to_chunks(v)
    log_f = jax.nn.log_sigmoid(f_pre.astype(f32)).reshape(B, N, L, H).transpose(1, 0, 3, 2)
    log_i = i_pre.astype(f32).reshape(B, N, L, H).transpose(1, 0, 3, 2)
    bcum = jnp.cumsum(log_f, axis=-1)
    causal = jnp.tril(jnp.ones((L, L), dtype=bool))

    def step(carry, inp):
        C, n, m = carry
        qt, kt, vt, bt, it = inp
        d = bt[..., :, None] - bt[..., None, :] + it[..., None, :]
        d = jnp.where(causal, d, -jnp.inf)
        inter = bt + m[..., None]
        m_row = jnp.maximum(inter, jnp.max(d, axis=-1))
        w_intra = jnp.exp(d - m_row[..., None])
        w_inter = jnp.exp(inter - m_row)
        s = jnp.einsum('bhld,bhsd->bhls', qt, kt) * w_intra
        num = (jnp.einsum('bhls,bhsd->bhld', s, vt)
               + w_inter[..., None] * jnp.einsum('bhvk,bhlk->bhlv', C, qt))
        den = jnp.sum(s, axis=-1) + w_inter * jnp.einsum('bhk,bhlk->bhl', n, qt)
        h = num / jnp.maximum(jnp.abs(den), jnp.exp(-m_row))[..., None]
        b_last = bt[..., -1]
        g = b_last[..., None] - bt + it
        m_new = jnp.maximum(b_last + m, jnp.max(g, axis=-1))
        a = jnp.exp(b_last + m - m_new)
        wg = jnp.exp(g - m_new[..., None])
        C_new = a[..., None, None] * C + jnp.einsum('bhs,bhsv,bhsk->bhvk', wg, vt, kt)
        n_new = a[..., None] * n + jnp.einsum('bhs,bhsk->bhk', wg, kt)
        return (C_new, n_new, m_new), h

    init = (jnp.zeros((B, H, Dh, Dh), f32), jnp.zeros((B, H, Dh), f32), jnp.zeros((B, H), f32))
    _, h = lax.scan(step, init, (qc, kc, vc, bcum, log_i))
    return h.transpose(1, 0, 3, 2, 4).reshape(B, S, H, Dh).astype(v.dtype)

def rope_tables(positions):
    inv_freq = 1.0 / (ROPE_THETA ** (jnp.arange(0, A_ROPE, 2, dtype=jnp.float32) / A_ROPE))
    ang = positions.astype(jnp.float32)[..., None] * inv_freq
    return jnp.cos(ang), jnp.sin(ang)

def apply_rope(x, cos, sin):
    half = x.shape[-1] // 2
    xf = x.astype(jnp.float32)
    c, s = cos[:, :, None, :], sin[:, :, None, :]
    x1, x2 = xf[..., :half], xf[..., half:]
    return jnp.concatenate([x1 * c - x2 * s, x1 * s + x2 * c], axis=-1).astype(x.dtype)

def causal_block_attention(q, k, v):
    B, S, H, Dq = q.shape
    nb = S // Q_BLOCK
    scale = Dq ** -0.5
    qb = q.reshape(B, nb, Q_BLOCK, H, Dq).transpose(1, 0, 2, 3, 4)
    kpos = jnp.arange(S)

    def one_block(args):
        qi, idx = args
        s = jnp.einsum('blhd,bshd->bhls', qi, k, preferred_element_type=jnp.float32) * scale
        qpos = idx * Q_BLOCK + jnp.arange(Q_BLOCK)
        s = jnp.where(kpos[None, :] <= qpos[:, None], s, -jnp.inf)
        p = jax.nn.softmax(s, axis=-1).astype(v.dtype)
        return jnp.einsum('bhls,bshd->blhd', p, v)

    o = lax.map(one_block, (qb, jnp.arange(nb)))
    return o.transpose(1, 0, 2, 3, 4).reshape(B, S, H, v.shape[-1])

def mla_mixer(c_q, c_kv, k_rope, cos, sin, q_gain, kv_gain, w_uq, w_ukv, qh_gain, kh_gain):
    B, S, _ = c_q.shape
    q = (rms_norm(c_q, q_gain) @ w_uq).reshape(B, S, A_HEADS, A_QK_DIM)
    kv = (rms_norm(c_kv, kv_gain) @ w_ukv).reshape(B, S, A_HEADS, A_NOPE + A_V_DIM)
    k_nope, v = kv[..., :A_NOPE], kv[..., A_NOPE:]
    k = jnp.concatenate([k_nope, jnp.broadcast_to(k_rope[:, :, None, :], (B, S, A_HEADS, A_ROPE))], axis=-1)
    q = rms_norm(q, qh_gain)
    k = rms_norm(k, kh_gain)
    q = jnp.concatenate([q[..., :A_NOPE], apply_rope(q[..., A_NOPE:], cos, sin)], axis=-1)
    k = jnp.concatenate([k[..., :A_NOPE], apply_rope(k[..., A_NOPE:], cos, sin)], axis=-1)
    o = causal_block_attention(q, k, v)
    return o.reshape(B, S, A_WIDTH)

def chunk_spatial_gating(u, v, v_gain, w_s, b_s):
    B, S, _ = u.shape
    n = S // C_CHUNK
    v = rms_norm(v.reshape(B, S, C_GROUPS, C_GROUP_DIM), v_gain.reshape(C_GROUPS, C_GROUP_DIM))
    vc = v.reshape(B, n, C_CHUNK, C_GROUPS, C_GROUP_DIM)
    w = w_s * jnp.tril(jnp.ones((C_CHUNK, C_CHUNK), dtype=w_s.dtype))
    mixed = jnp.einsum('gts,bnsgd->bntgd', w, vc) + b_s.T[None, None, :, :, None]
    return u * mixed.reshape(B, S, C_WIDTH)

def hier_moe(x, w_group, b_group, w_expert, b_expert, w1, w3, w2):
    B, S, D = x.shape
    T = B * S
    xt = x.reshape(T, D)
    f32 = jnp.float32
    g_logits = (xt @ w_group).astype(f32)
    g_prob = jax.nn.softmax(g_logits, axis=-1)
    _, g_sel = lax.top_k(g_logits + b_group.astype(f32), 1)
    g_sel = g_sel[:, 0]
    tok = jnp.arange(T)
    g_gate = g_prob[tok, g_sel]
    e_logits = (xt @ w_expert).astype(f32).reshape(T, N_GROUPS, EXPERTS_PER_GROUP)
    e_logits = e_logits[tok, g_sel]
    e_bias = b_expert.astype(f32).reshape(N_GROUPS, EXPERTS_PER_GROUP)[g_sel]
    e_prob = jax.nn.softmax(e_logits, axis=-1)
    _, e_local = lax.top_k(e_logits + e_bias, TOP_K)
    e_w = jnp.take_along_axis(e_prob, e_local, axis=1)
    e_w = e_w / jnp.sum(e_w, axis=-1, keepdims=True)
    weights = g_gate[:, None] * e_w
    expert_id = g_sel[:, None] * EXPERTS_PER_GROUP + e_local

    A = T * TOP_K
    flat_e = expert_id.reshape(A)
    flat_tok = jnp.arange(A, dtype=jnp.int32) // TOP_K
    flat_w = weights.reshape(A)
    order = jnp.argsort(flat_e)
    se, stok, sw = flat_e[order], flat_tok[order], flat_w[order]
    counts = jnp.bincount(flat_e, length=N_EXPERTS)
    starts = jnp.cumsum(counts) - counts
    padded = ((counts + MOE_BLOCK - 1) // MOE_BLOCK) * MOE_BLOCK
    pad_ends = jnp.cumsum(padded)
    pad_starts = pad_ends - padded
    dest = pad_starts[se] + jnp.arange(A) - starts[se]
    n_blocks = -(-A // MOE_BLOCK) + N_EXPERTS
    P = n_blocks * MOE_BLOCK
    row_tok = jnp.full((P,), T, dtype=jnp.int32).at[dest].set(stok)
    row_w = jnp.zeros((P,), dtype=x.dtype).at[dest].set(sw.astype(x.dtype))
    block_start = jnp.arange(n_blocks) * MOE_BLOCK
    block_e = jnp.minimum(jnp.sum(pad_ends[None, :] <= block_start[:, None], axis=1), N_EXPERTS - 1)
    x_pad = jnp.concatenate([xt, jnp.zeros((1, D), dtype=x.dtype)], axis=0)

    def expert_block(args):
        rows, rw, e = args
        xi = x_pad[rows]
        h = jax.nn.silu(xi @ w1[e]) * (xi @ w3[e])
        return (h @ w2[e]) * rw[:, None]

    yb = lax.map(expert_block, (row_tok.reshape(n_blocks, MOE_BLOCK), row_w.reshape(n_blocks, MOE_BLOCK), block_e))
    out = jnp.zeros((T + 1, D), dtype=x.dtype).at[row_tok].add(yb.reshape(P, D))[:T]
    return out.reshape(B, S, D)

def first_inputs(seed: int = 0) -> dict:
    key = jax.random.key(seed)
    ks = jax.random.split(key, 32)
    nrm = jax.random.normal
    def gain(k, n):
        return 1.0 + 0.02 * nrm(k, (DEPTH, n), jnp.float32)
    x = nrm(ks[0], (BATCH, SEQ, D_MODEL), jnp.float32)
    offsets = jax.random.randint(ks[1], (BATCH, 1), 0, 4096, dtype=jnp.int32)
    positions = offsets + jnp.arange(SEQ, dtype=jnp.int32)[None, :]
    f_bias = jnp.linspace(3.0, 6.0, M_HEADS, dtype=jnp.float32)[None, :]
    m_gate_bias = jnp.concatenate([0.1 * nrm(ks[6], (DEPTH, M_HEADS), jnp.float32),
                                   f_bias + 0.1 * nrm(ks[7], (DEPTH, M_HEADS), jnp.float32)], axis=-1)
    return {
        'x': x,
        'positions': positions,
        'attn_norm': gain(ks[2], D_MODEL),
        'w_in': nrm(ks[3], (DEPTH, D_MODEL, D_IN), jnp.float32) * D_MODEL ** -0.5,
        'm_conv_w': nrm(ks[4], (DEPTH, CONV_WIDTH, 2 * M_WIDTH), jnp.float32) * CONV_WIDTH ** -0.5,
        'm_conv_b': 0.02 * nrm(ks[5], (DEPTH, 2 * M_WIDTH), jnp.float32),
        'm_gate_bias': m_gate_bias,
        'a_q_norm': gain(ks[8], A_Q_RANK),
        'a_kv_norm': gain(ks[9], A_KV_RANK),
        'a_w_uq': nrm(ks[10], (DEPTH, A_Q_RANK, A_HEADS * A_QK_DIM), jnp.float32) * A_Q_RANK ** -0.5,
        'a_w_ukv': nrm(ks[11], (DEPTH, A_KV_RANK, A_HEADS * (A_NOPE + A_V_DIM)), jnp.float32) * A_KV_RANK ** -0.5,
        'a_q_head_norm': gain(ks[12], A_QK_DIM),
        'a_k_head_norm': gain(ks[13], A_QK_DIM),
        'c_v_norm': gain(ks[14], C_WIDTH),
        'c_w_s': nrm(ks[15], (DEPTH, C_GROUPS, C_CHUNK, C_CHUNK), jnp.float32) * C_CHUNK ** -0.5,
        'c_b_s': 1.0 + 0.1 * nrm(ks[16], (DEPTH, C_GROUPS, C_CHUNK), jnp.float32),
        'mix_out_norm': gain(ks[17], D_MIX),
        'w_out': nrm(ks[18], (DEPTH, D_MIX, D_MODEL), jnp.float32) * (D_MIX ** -0.5) * ((2 * DEPTH) ** -0.5),
        'ffn_norm': gain(ks[19], D_MODEL),
        'w_group': nrm(ks[20], (DEPTH, D_MODEL, N_GROUPS), jnp.float32) * D_MODEL ** -0.5,
        'b_group': 0.01 * nrm(ks[21], (DEPTH, N_GROUPS), jnp.float32),
        'w_expert': nrm(ks[22], (DEPTH, D_MODEL, N_EXPERTS), jnp.float32) * D_MODEL ** -0.5,
        'b_expert': 0.01 * nrm(ks[23], (DEPTH, N_EXPERTS), jnp.float32),
        'w1': nrm(ks[24], (DEPTH, N_EXPERTS, D_MODEL, D_EXPERT), jnp.float32) * D_MODEL ** -0.5,
        'w3': nrm(ks[25], (DEPTH, N_EXPERTS, D_MODEL, D_EXPERT), jnp.float32) * D_MODEL ** -0.5,
        'w2': nrm(ks[26], (DEPTH, N_EXPERTS, D_EXPERT, D_MODEL), jnp.float32) * D_EXPERT ** -0.5 * ((2 * DEPTH) ** -0.5),
    }

def first_block(x, positions, attn_norm, w_in, m_conv_w, m_conv_b, m_gate_bias, a_q_norm, a_kv_norm,
              a_w_uq, a_w_ukv, a_q_head_norm, a_k_head_norm, c_v_norm, c_w_s, c_b_s, mix_out_norm,
              w_out, ffn_norm, w_group, b_group, w_expert, b_expert, w1, w3, w2):
    B, S, _ = x.shape
    cos, sin = rope_tables(positions)
    for l in range(DEPTH):
        h = rms_norm(x, attn_norm[l])
        proj = h @ w_in[l]
        mq, mk, mv, mo, mi, mf, cq, ckv, krope, cu, cv = split_cols(proj, IN_SIZES)
        qk = jax.nn.silu(causal_depthwise_conv(jnp.concatenate([mq, mk], axis=-1), m_conv_w[l], m_conv_b[l]))
        mq, mk = qk[..., :M_WIDTH], qk[..., M_WIDTH:]
        gb = m_gate_bias[l]
        hm = mlstm_chunkwise(mq.reshape(B, S, M_HEADS, M_HEAD_DIM),
                             mk.reshape(B, S, M_HEADS, M_HEAD_DIM),
                             mv.reshape(B, S, M_HEADS, M_HEAD_DIM),
                             mi + gb[:M_HEADS], mf + gb[M_HEADS:])
        hm = jax.nn.sigmoid(mo) * hm.reshape(B, S, M_WIDTH)
        ha = mla_mixer(cq, ckv, krope, cos, sin, a_q_norm[l], a_kv_norm[l], a_w_uq[l], a_w_ukv[l],
                       a_q_head_norm[l], a_k_head_norm[l])
        hc = chunk_spatial_gating(jax.nn.gelu(cu), jax.nn.gelu(cv), c_v_norm[l], c_w_s[l], c_b_s[l])
        g = mix_out_norm[l]
        y = jnp.concatenate([head_rms_norm(hm, g[:M_WIDTH], M_HEADS),
                             head_rms_norm(ha, g[M_WIDTH:M_WIDTH + A_WIDTH], A_HEADS),
                             head_rms_norm(hc, g[M_WIDTH + A_WIDTH:], C_GROUPS)], axis=-1)
        x = x + y @ w_out[l]
        x = x + hier_moe(rms_norm(x, ffn_norm[l]), w_group[l], b_group[l], w_expert[l], b_expert[l],
                         w1[l], w3[l], w2[l])
    return x


DEPTH_2 = 1

HEAD_DIM = 64
N_HEADS_MOBA = 8
N_HEADS_SB = 8
WIDTH_MOBA = N_HEADS_MOBA * HEAD_DIM
WIDTH_SB = N_HEADS_SB * HEAD_DIM
MOBA_BLOCK = 256
MOBA_TOPK = 3
MOBA_Q_CHUNK = 16
SB_Q_BLOCK = 128
REL_BUCKETS = 32
REL_MAX_DIST = 128
NORM_EPS = 1e-6
NEG_INF = -1e30
PROJ_SPLITS = [WIDTH_MOBA] * 4 + [WIDTH_SB] * 4 + [D_MODEL] * 2
IN_WIDTH = sum(PROJ_SPLITS)
SPLIT_POINTS = [int(c) for c in np.cumsum(PROJ_SPLITS)[:-1]]


def rms_norm_2(x, w):
    xf = x.astype(jnp.float32)
    y = xf * lax.rsqrt(jnp.mean(xf * xf, axis=-1, keepdims=True) + NORM_EPS)
    return (y * w.astype(jnp.float32)).astype(x.dtype)

def split_heads(t, n_heads):
    b, s, _ = t.shape
    return t.reshape(b, s, n_heads, HEAD_DIM).transpose(0, 2, 1, 3)

def merge_heads(t):
    b, h, s, dh = t.shape
    return t.transpose(0, 2, 1, 3).reshape(b, s, h * dh)

def t5_bucket(dist):
    n = jnp.maximum(dist, 0)
    max_exact = REL_BUCKETS // 2
    nf = jnp.maximum(n, 1).astype(jnp.float32)
    large = max_exact + (jnp.log(nf / max_exact) / math.log(REL_MAX_DIST / max_exact)
                         * (REL_BUCKETS - max_exact)).astype(jnp.int32)
    large = jnp.minimum(large, REL_BUCKETS - 1)
    return jnp.where(n < max_exact, n, large)

def moba_attention(q, k, v, rel_bias):
    b, h, s, dh = q.shape
    nb = -(-s // MOBA_BLOCK)
    s_pad = nb * MOBA_BLOCK
    top = min(MOBA_TOPK, nb)
    scale = dh ** -0.5
    pad = ((0, 0), (0, 0), (0, s_pad - s), (0, 0))
    q, k, v = jnp.pad(q, pad), jnp.pad(k, pad), jnp.pad(v, pad)
    k_blk = k.reshape(b, h, nb, MOBA_BLOCK, dh)
    v_blk = v.reshape(b, h, nb, MOBA_BLOCK, dh)
    k_mean = jnp.mean(k_blk.astype(jnp.float32), axis=3)
    n_chunks = s_pad // MOBA_Q_CHUNK
    q_chunks = q.reshape(b, h, n_chunks, MOBA_Q_CHUNK, dh).transpose(2, 0, 1, 3, 4)
    bi = jnp.arange(b)[:, None, None, None]
    hi = jnp.arange(h)[None, :, None, None]
    offs = jnp.arange(MOBA_BLOCK)
    blk_ids = jnp.arange(nb)

    def one_chunk(args):
        qc, ci = args
        t = ci * MOBA_Q_CHUNK + jnp.arange(MOBA_Q_CHUNK)
        cur = (ci * MOBA_Q_CHUNK) // MOBA_BLOCK
        gate = jnp.einsum('bhqd,bhnd->bhqn', qc.astype(jnp.float32), k_mean)
        gate = jnp.where(blk_ids < cur, gate, NEG_INF)
        _, idx = lax.top_k(gate, top)
        valid = idx < cur
        k_sel = k_blk[bi, hi, idx]
        v_sel = v_blk[bi, hi, idx]
        pos_sel = idx[..., None] * MOBA_BLOCK + offs
        bias_sel = rel_bias[hi[..., None], t5_bucket(t[:, None, None] - pos_sel)]
        logit_sel = jnp.einsum('bhqd,bhqjkd->bhqjk', qc, k_sel).astype(jnp.float32) * scale + bias_sel
        logit_sel = jnp.where(valid[..., None], logit_sel, NEG_INF).reshape(b, h, MOBA_Q_CHUNK, top * MOBA_BLOCK)
        k_own = lax.dynamic_index_in_dim(k_blk, cur, axis=2, keepdims=False)
        v_own = lax.dynamic_index_in_dim(v_blk, cur, axis=2, keepdims=False)
        dist_own = t[:, None] - (cur * MOBA_BLOCK + offs)[None, :]
        bias_own = rel_bias[:, t5_bucket(dist_own)]
        logit_own = jnp.einsum('bhqd,bhkd->bhqk', qc, k_own).astype(jnp.float32) * scale + bias_own
        logit_own = jnp.where(dist_own >= 0, logit_own, NEG_INF)
        p = jax.nn.softmax(jnp.concatenate([logit_sel, logit_own], axis=-1), axis=-1).astype(v.dtype)
        p_sel = p[..., :top * MOBA_BLOCK].reshape(b, h, MOBA_Q_CHUNK, top, MOBA_BLOCK)
        p_own = p[..., top * MOBA_BLOCK:]
        return (jnp.einsum('bhqjk,bhqjkd->bhqd', p_sel, v_sel)
                + jnp.einsum('bhqk,bhkd->bhqd', p_own, v_own))

    out = lax.map(one_chunk, (q_chunks, jnp.arange(n_chunks)))
    out = out.transpose(1, 2, 0, 3, 4).reshape(b, h, s_pad, dh)
    return out[:, :, :s]

def stick_breaking_attention(q, k, v):
    s_len = q.shape[2]
    scale = q.shape[-1] ** -0.5
    outs = []
    for i in range(s_len // SB_Q_BLOCK):
        t0, t1 = i * SB_Q_BLOCK, (i + 1) * SB_Q_BLOCK
        z = jnp.einsum('bhqd,bhkd->bhqk', q[:, :, t0:t1], k[:, :, :t1]).astype(jnp.float32) * scale
        past = jnp.arange(t1)[None, :] < (t0 + jnp.arange(SB_Q_BLOCK))[:, None]
        log_1m = jnp.where(past, jax.nn.log_sigmoid(-z), 0.0)
        shifted = jnp.concatenate([log_1m[..., 1:], jnp.zeros_like(log_1m[..., :1])], axis=-1)
        suffix = lax.cumsum(shifted, axis=3, reverse=True)
        w = jnp.where(past, jnp.exp(jax.nn.log_sigmoid(z) + suffix), 0.0).astype(v.dtype)
        outs.append(jnp.einsum('bhqk,bhkd->bhqd', w, v[:, :, :t1]))
    return jnp.concatenate(outs, axis=2)

def second_inputs(seed: int = 0) -> dict:
    key = jax.random.key(seed)
    ks = jax.random.split(key, 10)
    f32 = jnp.float32
    x = jax.random.normal(ks[0], (BATCH, SEQ, D_MODEL), f32)
    norm_w = 1.0 + 0.02 * jax.random.normal(ks[1], (DEPTH_2, D_MODEL), f32)
    w_in = jax.random.normal(ks[2], (DEPTH_2, D_MODEL, IN_WIDTH), f32) * D_MODEL ** -0.5
    merge_gate_b = 0.01 * jax.random.normal(ks[3], (DEPTH_2, 2 * D_MODEL), f32)
    q_norm_w = 1.0 + 0.02 * jax.random.normal(ks[4], (DEPTH_2, HEAD_DIM), f32)
    k_norm_w = 1.0 + 0.02 * jax.random.normal(ks[5], (DEPTH_2, HEAD_DIM), f32)
    rel_bias = 0.2 * jax.random.normal(ks[6], (N_HEADS_MOBA, REL_BUCKETS), f32)
    w_up_moba = jax.random.normal(ks[7], (DEPTH_2, WIDTH_MOBA, D_MODEL), f32) * WIDTH_MOBA ** -0.5
    w_up_sb = jax.random.normal(ks[8], (DEPTH_2, WIDTH_SB, D_MODEL), f32) * WIDTH_SB ** -0.5
    w_out = jax.random.normal(ks[9], (DEPTH_2, D_MODEL, D_MODEL), f32) * D_MODEL ** -0.5
    return {"x": x, "norm_w": norm_w, "w_in": w_in, "merge_gate_b": merge_gate_b,
            "q_norm_w": q_norm_w, "k_norm_w": k_norm_w, "rel_bias": rel_bias,
            "w_up_moba": w_up_moba, "w_up_sb": w_up_sb, "w_out": w_out}

def second_block(x, norm_w, w_in, merge_gate_b, q_norm_w, k_norm_w, rel_bias, w_up_moba, w_up_sb, w_out):
    for l in range(DEPTH_2):
        h = rms_norm_2(x, norm_w[l])
        proj = h @ w_in[l]
        qa, ka, va, za, qb, kb, vb, zb, gl_a, gl_b = jnp.split(proj, SPLIT_POINTS, axis=-1)
        qa = rms_norm_2(split_heads(qa, N_HEADS_MOBA), q_norm_w[l])
        ka = rms_norm_2(split_heads(ka, N_HEADS_MOBA), k_norm_w[l])
        oa = moba_attention(qa, ka, split_heads(va, N_HEADS_MOBA), rel_bias)
        ob = stick_breaking_attention(split_heads(qb, N_HEADS_SB), split_heads(kb, N_HEADS_SB),
                                      split_heads(vb, N_HEADS_SB))
        ya = (merge_heads(oa) * jax.nn.silu(za)) @ w_up_moba[l]
        yb = (merge_heads(ob) * jax.nn.silu(zb)) @ w_up_sb[l]
        gb = merge_gate_b[l]
        y = jax.nn.sigmoid(gl_a + gb[:D_MODEL]) * ya + jax.nn.sigmoid(gl_b + gb[D_MODEL:]) * yb
        x = x + y @ w_out[l]
    return x


def setup_inputs(seed=0):
    out = dict(first_inputs(seed))
    for name, value in second_inputs(seed + 1).items():
        if name != "x":
            out[name + "_2"] = value
    return out


def reference(
    x, positions, attn_norm, w_in, m_conv_w, m_conv_b, m_gate_bias, a_q_norm, a_kv_norm, a_w_uq,
    a_w_ukv, a_q_head_norm, a_k_head_norm, c_v_norm, c_w_s, c_b_s, mix_out_norm, w_out,
    ffn_norm, w_group, b_group, w_expert, b_expert, w1, w3, w2, norm_w_2, w_in_2,
    merge_gate_b_2, q_norm_w_2, k_norm_w_2, rel_bias_2, w_up_moba_2, w_up_sb_2, w_out_2,
):
    x = first_block(
        x, positions, attn_norm, w_in, m_conv_w, m_conv_b, m_gate_bias, a_q_norm, a_kv_norm,
        a_w_uq, a_w_ukv, a_q_head_norm, a_k_head_norm, c_v_norm, c_w_s, c_b_s, mix_out_norm,
        w_out, ffn_norm, w_group, b_group, w_expert, b_expert, w1, w3, w2,
    )
    return second_block(
        x, norm_w_2, w_in_2, merge_gate_b_2, q_norm_w_2, k_norm_w_2, rel_bias_2, w_up_moba_2,
        w_up_sb_2, w_out_2,
    )


_drawn_inputs = setup_inputs


def setup_inputs(seed=0):
    import zlib

    import numpy as np

    out = dict(_drawn_inputs(seed))
    spreads = {}
    factors = {'m_conv_b': 3.403,
     'a_q_norm': 4.251,
     'a_q_head_norm': 4.554,
     'a_k_head_norm': 3.703,
     'c_v_norm': 8.0,
     'mix_out_norm': 3.014,
     'ffn_norm': 2.776,
     'b_group': 7.808,
     'b_expert': 4.423,
     'norm_w_2': 8.0,
     'merge_gate_b_2': 41.656,
     'q_norm_w_2': 8.0,
     'k_norm_w_2': 8.0,
     'rel_bias_2': 5.98}
    for name, (base, spread) in spreads.items():
        noise = np.random.default_rng([zlib.crc32(name.encode()), seed]).standard_normal(out[name].shape)
        drawn = base * np.exp(spread * noise) if base else spread * noise
        out[name] = jnp.asarray(drawn.astype(out[name].dtype))
    for name, factor in factors.items():
        out[name] = (out[name] * factor).astype(out[name].dtype)
    return out
```

```python
from contextlib import ExitStack

import concourse.bass as bass
import numpy as np
from concourse import mybir

F32 = mybir.dt.float32
BF16 = mybir.dt.bfloat16
I32 = mybir.dt.int32
ALU = mybir.AluOpType
ACT = mybir.ActivationFunctionType
AX = mybir.AxisListType

P = 128
SEQ = 256
NT = SEQ // P
D = 1024
KD = D // P
DEPTH = 2
EPS = 1e-6
NEG = -1e30

N_GROUPS, PER_GROUP = 4, 8
NE = N_GROUPS * PER_GROUP
DE = 256
CELL = 64
PAIRS = NE // 2
ARENA = 19200
CELLS_OVER = 8

M_HEADS, M_DIM = 4, 96
M_WIDTH = M_HEADS * M_DIM
A_HEADS, NOPE, ROPE, V_DIM = 6, 64, 32, 64
QK_DIM = NOPE + ROPE
A_WIDTH = A_HEADS * V_DIM
Q_RANK, KV_RANK = 256, 128
C_GROUPS, C_DIM = 4, 64
C_WIDTH = C_GROUPS * C_DIM
MIX_GAIN_A = M_WIDTH
UNIT_COLS = [(0, 384), (384, 768), (768, 1280), (1280, 1792), (1792, 2304), (2304, 2472)]
A_COLS = 2 * M_WIDTH
B_COLS = 2472 - 4 * M_WIDTH
GATE_AT, CQ_AT, CKV_AT, KR_AT, CU_AT, CV_AT = 0, 8, 264, 392, 424, 680

SLOT = 4096
RING = 6
HALF = 512

CONST_WIDTHS = [("ident", P), ("upto", P), ("before", P), ("fromon", P), ("ones", P), ("iota", P),
                ("causal", 2 * P), ("causal_t", P), ("inv_freq", 16), ("rev", NE), ("cell64", NE),
                ("zeros", 2 * P), ("neg_half", 1)]
LATE_WIDTHS = [("past_neg", 2 * P), ("past_add", 2 * P), ("buckets", 384)]


S_HEADS, S_DIM = 8, 64
S_WIDTH = S_HEADS * S_DIM
COLUMNS = ("qa", "ka", "va", "za", "qb", "kb", "vb", "zb", "ga0", "ga1", "gb0", "gb1")
SECOND_UNITS = ("qa", "ka", "qb", "kb", "va", "vb", "za", "zb", "ga0", "ga1", "gb0", "gb1", "upa", "upb",
                "out0", "out1")
TILES = [f"{u}{t}" for u in ("za", "zb", "ga0", "ga1", "gb0", "gb1") for t in range(2)]


def step_tiles(h):
    before = {0: [0], 1: [1], 2: [3], 3: [5], 4: [7], 5: [8], 6: [9], 7: [10], 8: [11]}[h]
    after = {1: [2], 2: [4], 3: [6]}.get(h, [])
    return [TILES[i] for i in before], [TILES[i] for i in after]


def second_banks():
    uses = [("rel", 4), ("f", 5)]
    uses += [(n, b) for names in (("qa0", "qa1", "ka0", "ka1"), ("qbA", "qbB", "kbA", "kbB"),
                                  ("va0", "va1", "vb0", "vb1")) for b, n in enumerate(names)]
    uses += [("qT0", 4), ("qT1", 5), ("kT0", 6), ("kT1", 7)]
    tile = 0
    for h in range(S_HEADS + 1):
        if h < S_HEADS:
            uses += [(f"z{h}", 4 + h % 2), (f"sc{h}", 6 + h % 2)]
        front, behind = step_tiles(h)
        for n in front:
            uses.append((n, tile % 4))
            tile += 1
        if h:
            uses += [(f"r{h - 1}", 4 + (h - 1) % 2), (f"pT{h - 1}", 6 + (h - 1) % 2)]
        for n in behind:
            uses.append((n, tile % 4))
            tile += 1
        if h:
            uses += [(f"ob{h - 1}", 4 + (h - 1) % 2), (f"oa{h - 1}", 6 + (h - 1) % 2)]
    uses += [(f"oT{i}", 4 + i) for i in range(4)]
    uses += [(f"y{a}{t}{n}", 2 * (n % 2) + (a == "b")) for t in range(2) for n in range(2) for a in "ab"]
    uses += [(f"yT{u}", 4 + u) for u in range(4)] + [(f"out{b}", b) for b in range(4)]
    return uses


def constant_table():
    p = np.arange(P)[:, None]
    c = np.arange(P)[None, :]
    c2 = np.arange(2 * P)[None, :]
    dist = 255 - np.arange(384)
    n = np.maximum(dist, 1).astype(np.float64)
    bucket = np.where(dist < 16, dist, np.minimum(16 + (np.log(n / 16) / np.log(8.0) * 16).astype(np.int64), 31))
    bucket = np.where(dist < 0, 32, bucket)
    freq = 1.0 / (np.float32(10000.0) ** (np.arange(0, 32, 2, dtype=np.float32) / np.float32(32)))
    full = np.ones((P, 1), np.float32)
    parts = {
        "ident": p == c, "upto": p <= c, "before": p < c, "fromon": p >= c, "ones": full * np.ones((1, P)),
        "iota": full * c, "causal": np.where(p + P - c2 >= 0, 0.0, NEG), "causal_t": np.where(p <= c, 0.0, NEG),
        "past_neg": -(p < c2).astype(np.float32), "past_add": np.where(p < c2, 0.0, NEG),
        "inv_freq": full * freq[None, :], "rev": full * (NE - np.arange(NE))[None, :],
        "cell64": full * (CELL * np.arange(NE))[None, :], "zeros": full * np.zeros((1, 2 * P)),
        "buckets": p == bucket[None, :], "neg_half": -0.5 * full,
    }
    return [np.concatenate([np.asarray(parts[k], np.float32) for k, _ in widths], axis=1)
            for widths in (CONST_WIDTHS, LATE_WIDTHS)]


def bank_plan(uses, base):
    plan, total = {}, list(base)
    for name, b in uses:
        total[b] += 1
        plan[name] = (b, total[b])
    return plan, total


MIXER_BANKS = ([("conv_rows", 6), ("gate_w", 7), ("u3t0", 0), ("u3t1", 1), ("u4t0", 2), ("u4t1", 3), ("u5t0", 0),
                ("u5t1", 1), ("q01", 2), ("cqT", 4), ("ckvT", 5), ("cum", 6), ("q23", 3), ("rrow0", 7), ("rrow1", 6),
                ("q0a", 4), ("q0b", 5), ("k01", 0), ("q1a", 4), ("q1b", 5), ("mrow0", 7), ("kv0a", 4), ("kv0b", 5),
                ("k23", 1), ("mrow1", 6), ("kv1a", 4), ("kv1b", 5), ("gated", 7), ("u2t0", 2), ("u2t1", 3),
                ("st0", 4), ("st1", 5), ("ktok", 6), ("state", 7), ("num0", 4), ("num1", 5), ("inter", 6)]
               + [(f"qkT{i}", i % 4) for i in range(6)] + [("o0", 4), ("o1", 5)]
               + [x for h in range(6) for x in ((f"sc{h}", 2 + h % 2), (f"pT{h}", h % 2))]
               + [(f"yT{u}", 6 + u % 2) for u in range(4)] + [(f"out{b}", b) for b in range(4)])


class Chain:

    def __init__(self, eng, sem, base=0):
        self.eng, self.sem, self.n = eng, sem, base

    def __call__(self, ins):
        self.n = self.n + 1
        ins.then_inc(self.sem, 1)
        self.eng.wait_ge(self.sem, self.n)


def program(nc, io, out, mixer=True, second=True):
    with ExitStack() as ctx:
        def sb(name, shape, dt=F32):
            return ctx.enter_context(nc.sbuf_tensor(name, shape, dt))

        def sem(name):
            return ctx.enter_context(nc.semaphore(name))

        bank = [ctx.enter_context(nc.psum_tensor(f"bank{b}", [P, HALF], F32)) for b in range(8)]
        ring = [sb(f"ring{s}", [P, SLOT]) for s in range(RING)]
        x = sb("x", [P, NT, D])
        consts = sb("consts", [P, sum(w for _, w in CONST_WIDTHS)])
        const = {}
        at = 0
        for name, w in CONST_WIDTHS:
            const[name] = consts[:, at:at + w]
            at += w
        ident, ones = const["ident"], const["ones"]

        late = ctx.enter_context(nc.sbuf_tensor("arena", [P, ARENA], F32))

        def place(at, *shape):
            n = 1
            for w in shape:
                n *= w
            assert at + n <= ARENA, (at, shape)
            v = late[:, at:at + n]
            if len(shape) == 2:
                return v.rearrange("p (a b) -> p a b", b=shape[1])
            if len(shape) == 3:
                return v.rearrange("p (a b c) -> p a b c", b=shape[1], c=shape[2])
            return v

        gain = sb("gain", [P, D])
        w_router = sb("w_router", [P, KD, N_GROUPS + NE])
        router_bias = sb("router_bias", [P, N_GROUPS + NE])
        xf = sb("xf", [P, NT, KD, P])
        xfT = sb("xfT", [P, KD, SEQ])
        stats = sb("stats", [P, 16])
        positions = sb("positions", [P, NT], I32)
        overint = sb("overint", [1, DEPTH, CELLS_OVER + 1], I32)
        cos_sin = sb("cos_sin", [P, 2, NT, ROPE // 2])
        square = place(0, D)

        at = [D]

        def nxt(*shape):
            n = 1
            for w in shape:
                n *= w
            at[0] += n
            return place(at[0] - n, *shape)

        logits = nxt(NT, N_GROUPS + NE)
        groupwork = nxt(NT, 3, N_GROUPS)
        scores = nxt(NT, NE)
        work = nxt(NT, NE)
        pick = nxt(NT, 2, NE)
        rowmax = nxt(NT)
        expin = nxt(NT, 8)
        expout = nxt(NT, 8)
        gates = nxt(2, NT)
        slot_of = nxt(2, NT)
        position = nxt(NT + 1, NE)
        over = nxt(3, NE)
        overlist = nxt(CELLS_OVER, NE)
        oversum = nxt(CELLS_OVER + 1)
        slotrow = nxt(P)
        onehot = nxt(2, NT, P)
        onehot_w = nxt(2, NT, P)
        hotwork = nxt(P)
        xg = nxt(2, KD, P)
        silu = nxt(2, DE)
        hidden = nxt(2, DE)
        turned = nxt(2, 4, P)
        y = nxt(2, 2, HALF)

        conv_raw = place(0, 2 * M_HEADS, 3 + SEQ)
        prob = place(0, 2, 3 * P)
        probT = place(6 * P, 2, 3 * P)
        at[0] = 2 * M_HEADS * (3 + SEQ)
        turned_at = at[0]
        conv_out = nxt(2 * M_HEADS, SEQ)
        decay = nxt(NT, M_HEADS, P)
        qkT = place(turned_at, 2 * A_HEADS, SEQ)
        gate_raw = place(turned_at + 2 * M_HEADS * SEQ, C_GROUPS, P)
        proj_a = nxt(NT, A_COLS)
        b_at = at[0]
        proj_b = nxt(NT, B_COLS)
        kv = place(b_at, NT, A_HEADS, NOPE + V_DIM)
        qk = nxt(NT, 2 * A_HEADS, QK_DIM)
        diag_at = at[0]
        qk_square = nxt(2 * A_HEADS, QK_DIM)
        diag = place(diag_at, M_HEADS, P)
        masked = place(diag_at + M_HEADS * P, M_HEADS, P)
        conv_rows = place(diag_at, 2 * M_WIDTH)
        cb_rows = place(diag_at + 2 * M_WIDTH, P)
        gelu = nxt(NT, 2 * C_WIDTH)
        small_at = at[0]
        k_weighted = nxt(M_HEADS, M_DIM)
        state = nxt(M_HEADS, M_DIM + 1)
        total = nxt(NT, M_HEADS, M_DIM + 1)
        latent = place(small_at, NT, Q_RANK + KV_RANK)
        latentT = nxt(3, SEQ)
        gate_wT = nxt(C_GROUPS, P)
        w_uq = nxt(2, A_HEADS * QK_DIM)
        w_ukv = nxt(A_HEADS * (NOPE + V_DIM))
        latent_gain = nxt(Q_RANK + KV_RANK)
        cv_gain = nxt(C_WIDTH)
        qk_gain = nxt(2, QK_DIM)
        conv_w = nxt(2 * M_HEADS, 5)
        cb = nxt(C_GROUPS)
        gate_bias = nxt(2 * M_HEADS)
        gate_in = nxt(NT, 3, 2 * M_HEADS)
        log_f = nxt(NT, M_HEADS)
        cum = nxt(NT, 2, M_HEADS)
        rel = nxt(NT, M_HEADS)
        run_max = nxt(NT, M_HEADS)
        carry = nxt(M_HEADS)
        small_exp = nxt(3, M_HEADS)
        den = nxt(NT, 2, M_HEADS)
        head_sums = nxt(48)
        head_rstd = nxt(48)
        soft = nxt(A_HEADS, 2, NT)
        second_end = at[0]
        at[0] = 0
        s_v = nxt(2, NT * S_WIDTH).rearrange("p a (t n) -> p a t n", t=NT)
        s_z = nxt(2, NT * S_WIDTH).rearrange("p a (t n) -> p a t n", t=NT)
        s_qk = nxt(NT, 2 * S_WIDTH)
        s_o = place(at[0] - 2 * NT * S_WIDTH, 2, NT * S_WIDTH).rearrange("p a (t n) -> p a t n", t=NT)
        s_qkbT = nxt(2, S_HEADS // 2 * SEQ).rearrange("p a (i s) -> p a i s", s=SEQ)
        s_qkaT = nxt(2, S_HEADS // 2 * SEQ).rearrange("p a (i s) -> p a i s", s=SEQ)
        s_oT = s_qkaT
        gl_at = at[0]
        s_gates = nxt(NT, 2 * D)
        s_square = place(gl_at, 2 * S_WIDTH)
        s_rel = place(gl_at + 2 * S_WIDTH, 33)
        s_relT = place(gl_at + 2 * S_WIDTH + 64, S_HEADS)
        s_f = place(gl_at + 2 * S_WIDTH + 128, 384)
        s_bias = nxt(S_HEADS, SEQ)
        late_at = at[0]
        late_words = nxt(sum(w for _, w in LATE_WIDTHS))
        past_neg, past_add = place(late_at, SEQ), place(late_at + SEQ, SEQ)
        buckets = place(late_at + 2 * SEQ, 384)
        s_log = nxt(2, 3 * P)
        s_probT = nxt(2, 3 * P)
        s_prob = gain[:, 0:6 * P].rearrange("p (a n) -> p a n", a=2)
        s_gain = nxt(2, S_DIM)
        s_sums = nxt(NT * 2 * S_HEADS)
        s_rstd = nxt(NT * 2 * S_HEADS)
        s_soft = nxt(S_HEADS, 2, NT)
        s_work = nxt(S_DIM)
        at[0] = second_end

        rope_work = place(diag_at, 4, 2 * A_HEADS, ROPE // 2)

        loaded_x, loaded_consts, loaded_ffn = sem("loaded_x"), sem("loaded_consts"), sem("loaded_ffn")
        ROUTER_LOADS = 4 * 16
        MIXER_LOADS = 12 * 16
        loaded_mixer = sem("loaded_mixer")
        loaded_gain = sem("loaded_gain")
        loaded_positions = sem("loaded_positions")
        filled = [sem(f"filled{b}") for b in range(8)]
        drained = [sem(f"drained{b}") for b in range(8)]
        angles = sem("angles")
        rope_ready = sem("rope_ready")
        latent_sums = sem("latent_sums")
        head_sums_ready = sem("head_sums_ready")
        head_rstd_ready = sem("head_rstd_ready")
        gate_abs = sem("gate_abs")
        gate_exp = sem("gate_exp")
        gate_ln = sem("gate_ln")
        log_f_ready = sem("log_f_ready")
        latent_ready = sem("latent_ready")
        gelu_ready = sem("gelu_ready")
        gate_v_ready = sem("gate_v_ready")
        diag_ready = sem("diag_ready")
        decay_wanted = sem("decay_wanted")
        decay_done = sem("decay_done")
        conv_ready = sem("conv_ready")
        conv_act = sem("conv_act")
        out_gate = sem("out_gate")
        pt_ready = sem("pt_ready")
        kw_ready = sem("kw_ready")
        qk_ready = sem("qk_ready")
        logits_ready = sem("logits_ready")
        prob_ready = sem("prob_ready")
        y_rows = sem("y_rows")
        loaded_second = sem("loaded_second")
        loaded_merge_bias = sem("loaded_merge_bias")
        rel_ready = sem("rel_ready")
        f_ready = sem("f_ready")
        f_stored = sem("f_stored")
        bias_loaded = sem("bias_loaded")
        s_sums_ready = sem("s_sums_ready")
        s_rstd_ready = sem("s_rstd_ready")
        s_qk_ready = sem("s_qk_ready")
        s_ln_ready = sem("s_ln_ready")
        s_act = sem("s_act")
        s_log_ready = sem("s_log_ready")
        s_logits_ready = sem("s_logits_ready")
        s_prob_ready = sem("s_prob_ready")
        s_weight_ready = sem("s_weight_ready")
        s_silu_ready = sem("s_silu_ready")
        s_gate_ready = sem("s_gate_ready")
        s_o_ready = sem("s_o_ready")
        s_gates_in = sem("s_gates_in")
        s_rows = sem("s_rows")
        landed = [sem(f"landed{s}") for s in range(RING)]
        freed = [sem(f"freed{s}") for s in range(RING)]
        PER = 2 if mixer else 1
        plans, totals = [], [0] * 8
        for _ in range(DEPTH):
            plan, totals = bank_plan(MIXER_BANKS, totals)
            plans.append(plan)
        plan2, _ = bank_plan(second_banks(), totals)
        unit2, used2 = {}, [0] * RING
        for i, name in enumerate(SECOND_UNITS):
            used2[i % RING] += 1
            unit2[name] = (i % RING, used2[i % RING])

        def full(eng, plan, name):
            b, n = plan[name]
            eng.wait_ge(filled[b], n)
            return bank[b]

        def copied(eng, plan, *names):
            for name in names:
                b, n = plan[name]
                eng.wait_ge(drained[b], n)

        def left(plan, name):
            return drained[plan[name][0]]

        def unit_view(s, w):
            return ring[s][:, 0:KD * w].rearrange("p (k n) -> p k n", n=w)

        x_ready = sem("x_ready")
        vec_step = sem("vec_step")
        act_step = sem("act_step")
        squares = sem("squares")
        pool_step = sem("pool_step")
        rstd_ready = sem("rstd_ready")
        xf_ready = sem("xf_ready")
        xf_turned = sem("xf_turned")
        xfT_ready = sem("xfT_ready")
        logits_done = sem("logits_done")
        exp_wanted = sem("exp_wanted")
        exp_done = sem("exp_done")
        picked = sem("picked")
        counted = sem("counted")
        over_ready = sem("over_ready")
        acc_done = sem("acc_done")
        stored = sem("stored")
        over_back = sem("over_back")

        PAIR_SEMS = ("hot_ready", "turn_done", "gathered", "xg_ready", "up_done", "silu_ready",
                     "hidden_ready", "turned_ready", "down_done", "y_ready", "vec")

        def pair_sems(tag):
            return {n: sem(f"{tag}_{n}") for n in PAIR_SEMS}

        main = pair_sems("main")
        extra = [pair_sems(f"over{l}") for l in range(DEPTH)]
        extra_landed = [[sem(f"over{l}_landed{s}") for s in range(RING)] for l in range(DEPTH)]
        extra_freed = [[sem(f"over{l}_freed{s}") for s in range(RING)] for l in range(DEPTH)]

        UP_LO, UP_HI, DOWN = (2, 5), (3, 0), (4, 1)
        mixer_uses = [2 if s < 2 else 1 for s in range(RING)] if mixer else [0] * RING
        layer_uses = [b + PAIRS // 2 for b in mixer_uses]
        pair_bytes = [32 if s in DOWN else 64 for s in range(RING)]
        layer_lands = [16 * b + PAIRS // 2 * n for b, n in zip(mixer_uses, pair_bytes)]

        def up_view(s):
            return ring[s][:, :].rearrange("p (e w k f) -> p e w k f", e=2, w=2, k=KD // 2)

        def down_view(s):
            return ring[s][:, :].rearrange("p (e c n) -> p e c n", e=2, c=2)

        if second:
            skew = nc.dram_tensor("skew", [P, S_HEADS, 384], F32, kind="Internal").ap()

        block = ctx.enter_context(nc.Block())

        @block.sync
        def _(sp):
            sp.dma_start(x[:, :, :], io["x"][0].rearrange("(t p) d -> p t d", p=P)).then_inc(loaded_x, 16)

            def load_pair(l, par, experts, lands, frees, used):
                for h, s in ((0, UP_LO[par]), (1, UP_HI[par])):
                    sp.wait_ge(frees[s], used(s))
                    for w, name in ((0, "w1"), (1, "w3")):
                        for i, e in enumerate(experts):
                            src = io[name][l, bass.ds(e, 1)].rearrange(
                                "o (p k) f -> p (o k f)", p=P)[:, h * 1024:(h + 1) * 1024]
                            sp.dma_start(up_view(s)[:, i, w].rearrange("p k f -> p (k f)"), src)\
                              .then_inc(lands[s], 16)
                s = DOWN[par]
                sp.wait_ge(frees[s], used(s))
                for i, e in enumerate(experts):
                    src = io["w2"][l, bass.ds(e, 1)].rearrange("o (p c) n -> p (o c n)", p=P)
                    sp.dma_start(down_view(s)[:, i].rearrange("p c n -> p (c n)"), src).then_inc(lands[s], 16)

            def mixer_loads(l):
                def small(dst, src):
                    sp.dma_start(dst, src).then_inc(loaded_mixer, 16)

                small(gate_raw, io["c_w_s"][l].rearrange("g t s -> t g s"))
                small(conv_rows[0:4, :], io["m_conv_w"][l])
                small(conv_rows[4:5, :], io["m_conv_b"][l:l + 1, :])
                small(cb_rows[0:4, :], io["c_b_s"][l])
                small(gate_bias, io["m_gate_bias"][l:l + 1, :].broadcast_to([P, 2 * M_HEADS]))
                small(latent_gain[:, 0:Q_RANK], io["a_q_norm"][l:l + 1, :].broadcast_to([P, Q_RANK]))
                small(latent_gain[:, Q_RANK:], io["a_kv_norm"][l:l + 1, :].broadcast_to([P, KV_RANK]))
                small(cv_gain, io["c_v_norm"][l:l + 1, :].broadcast_to([P, C_WIDTH]))
                small(qk_gain[:, 0, :], io["a_q_head_norm"][l:l + 1, :].broadcast_to([P, QK_DIM]))
                small(qk_gain[:, 1, :], io["a_k_head_norm"][l:l + 1, :].broadcast_to([P, QK_DIM]))
                small(w_uq, io["a_w_uq"][l].rearrange("(k p) n -> p k n", p=P))
                small(w_ukv, io["a_w_ukv"][l])

            for l in range(DEPTH):
                if mixer:
                    if l == 0:
                        mixer_loads(l)
                    for s in (3, 4, 5, 0, 1, 2):
                        c0, c1 = UNIT_COLS[s]
                        sp.wait_ge(freed[s], l * layer_uses[s] + 1)
                        sp.dma_start(unit_view(s, c1 - c0),
                                     io["w_in"][l, :, c0:c1].rearrange("(k p) n -> p k n", p=P))\
                          .then_inc(landed[s], 16)
                    if l:
                        sp.wait_ge(x_ready, PER * l)
                        mixer_loads(l)
                    for s in range(2):
                        sp.wait_ge(freed[s], l * layer_uses[s] + 2)
                        sp.dma_start(unit_view(s, HALF), io["w_out"][l, :, s * HALF:(s + 1) * HALF].rearrange(
                            "(k p) n -> p k n", p=P)).then_inc(landed[s], 16)
                with sp.Fori(0, PAIRS // 2) as j:
                    for par in range(2):
                        load_pair(l, par, [4 * j + 2 * par, 4 * j + (2 * par + 1)], landed, freed,
                                  lambda s: j + (l * layer_uses[s] + mixer_uses[s] + 1))
                sp.wait_ge(over_ready, l + 1)
                n_over = sp.value_load(overint[0:1, l, CELLS_OVER:CELLS_OVER + 1], min_val=0, max_val=2)
                with sp.If(n_over > 0):
                    for s in range(RING):
                        sp.wait_ge(freed[s], (l + 1) * layer_uses[s] + 1)
                    with sp.Fori(0, n_over) as j:
                        for par in range(2):
                            experts = [sp.value_load(overint[0:1, l, bass.ds(4 * j + (2 * par + i), 1)],
                                                     min_val=0, max_val=NE - 1) for i in range(2)]
                            load_pair(l, par, experts, extra_landed[l], extra_freed[l], lambda s: j + 1)
                    sp.wait_ge(acc_done, l + 1)
                with sp.Else():
                    sp.nop()
            if second:
                def unit(name, src):
                    s, n = unit2[name]
                    sp.wait_ge(freed[s], DEPTH * layer_uses[s] + n)
                    k = src.shape[0] // P
                    sp.dma_start(ring[s][:, :].rearrange("p (k n) -> p k n", k=k),
                                 src.rearrange("(k p) n -> p k n", p=P)).then_inc(landed[s], 16)

                def columns(name):
                    c = COLUMNS.index(name) * HALF
                    unit(name, io["w_in_2"][0, :, c:c + HALF])

                for name in SECOND_UNITS[0:RING]:
                    columns(name)
                sp.wait_ge(x_ready, PER * DEPTH)
                for dst, src in ((late_words, io["late_consts"]), (s_rel[0:S_HEADS, 0:32], io["rel_bias_2"]),
                                 (s_gain[:, 0, :], io["q_norm_w_2"].broadcast_to([P, S_DIM])),
                                 (s_gain[:, 1, :], io["k_norm_w_2"].broadcast_to([P, S_DIM]))):
                    sp.dma_start(dst, src).then_inc(loaded_second, 16)
                sp.wait_ge(xfT_ready, 4 * (PER * DEPTH + 1))
                sp.dma_start(xf[:, :, :, :].rearrange("p t k i -> p (t k i)"),
                             io["merge_gate_b_2"].broadcast_to([P, 2 * D])).then_inc(loaded_merge_bias, 16)
                sp.wait_ge(f_ready, 1)
                sp.dma_start(skew.rearrange("p h j -> h p j"),
                             s_f[0:S_HEADS, :].unsqueeze(1).broadcast_to([S_HEADS, P, 384])).then_inc(f_stored, 16)
                sp.wait_ge(f_stored, 16)
                pitch = S_HEADS * 384 - 1
                sp.dma_start(s_bias, bass.AP(skew.tensor, P - 1, [[pitch, P], [384, S_HEADS], [1, SEQ]]))\
                  .then_inc(bias_loaded, 16)
                for name in SECOND_UNITS[RING:]:
                    if name in COLUMNS:
                        columns(name)
                    elif name in ("upa", "upb"):
                        unit(name, io["w_up_moba_2" if name == "upa" else "w_up_sb_2"][0])
                    else:
                        n = int(name[-1])
                        unit(name, io["w_out_2"][0, :, n * HALF:(n + 1) * HALF])
                sp.wait_ge(x_ready, PER * DEPTH + 1)
            else:
                sp.wait_ge(x_ready, PER * DEPTH)
            sp.dma_start(out[0].rearrange("(t p) d -> p t d", p=P), x[:, :, :]).then_inc(stored, 16)
            sp.wait_ge(stored, 16)

        @block.gpsimd
        def _(pool):
            step = Chain(pool, pool_step)

            def power(dst, signal):
                pool.tensor_tensor(dst, dst, const["neg_half"].broadcast_to(list(dst.shape)), ALU.pow)\
                    .then_inc(signal, 1)

            def rstd_of(dst, sums, n, signal):
                step(pool.tensor_scalar(dst, sums, 1.0 / n, EPS, ALU.mult, ALU.add))
                power(dst, signal)

            pool.dma_start(consts[:, :], io["consts"]).then_inc(loaded_consts, 16)
            pool.dma_start(positions[:, :], io["positions"][0].rearrange("(t p) -> p t", p=P),
                           allow_slow_non_contiguous=True)\
                .then_inc(loaded_positions, 16)

            def norm(m):
                for t in range(NT):
                    pool.wait_ge(squares, NT * m + t + 1)
                    rstd_of(stats[:, 8 + t:9 + t], stats[:, t:t + 1], D, rstd_ready)

            def load_gain(name, l):
                pool.dma_start(gain[:, :], io[name][l:l + 1, :].broadcast_to([P, D])).then_inc(loaded_gain, 16)

            for l in range(DEPTH):
                m = PER * l
                if mixer:
                    if l:
                        pool.wait_ge(xf_ready, NT * m)
                    load_gain("attn_norm", l)
                    if l == 0:
                        pool.wait_ge(loaded_consts, 16)
                    norm(m)
                    pool.wait_ge(latent_sums, 4 * l + 4)
                    step(pool.tensor_scalar(head_rstd[:, 0:2], head_sums[:, 0:2], 1.0 / Q_RANK, EPS, ALU.mult, ALU.add))
                    step(pool.tensor_scalar(head_rstd[:, 2:4], head_sums[:, 2:4], 1.0 / KV_RANK, EPS, ALU.mult, ALU.add))
                    power(head_rstd[:, 0:4], head_rstd_ready)
                    pool.wait_ge(xf_ready, NT * (m + 1))
                    load_gain("mix_out_norm", l)
                    pool.wait_ge(head_sums_ready, 3 * l + 1)
                    rstd_of(head_rstd[:, 4:12], head_sums[:, 4:12], C_DIM, head_rstd_ready)
                    pool.wait_ge(head_sums_ready, 3 * l + 2)
                    rstd_of(head_rstd[:, 12:36], head_sums[:, 12:36], QK_DIM, head_rstd_ready)
                    pool.wait_ge(head_sums_ready, 3 * l + 3)
                    step(pool.tensor_scalar(head_rstd[:, 0:8], head_sums[:, 0:8], 1.0 / M_DIM, EPS, ALU.mult, ALU.add))
                    step(pool.tensor_scalar(head_rstd[:, 8:28], head_sums[:, 8:28], 1.0 / C_DIM, EPS, ALU.mult, ALU.add))
                    power(head_rstd[:, 0:28], head_rstd_ready)
                if l:
                    pool.wait_ge(over_ready, l)
                pool.dma_start(w_router[:, :, 0:N_GROUPS], io["w_group"][l].rearrange("(p k) g -> p k g", p=P))\
                    .then_inc(loaded_ffn, 16)
                pool.dma_start(w_router[:, :, N_GROUPS:], io["w_expert"][l].rearrange("(p k) g -> p k g", p=P))\
                    .then_inc(loaded_ffn, 16)
                pool.dma_start(router_bias[:, 0:N_GROUPS], io["b_group"][l:l + 1, :].broadcast_to([P, N_GROUPS]))\
                    .then_inc(loaded_ffn, 16)
                pool.dma_start(router_bias[:, N_GROUPS:], io["b_expert"][l:l + 1, :].broadcast_to([P, NE]))\
                    .then_inc(loaded_ffn, 16)
                if mixer:
                    pool.wait_ge(y_rows, NT * (l + 1))
                elif l:
                    pool.wait_ge(xf_ready, NT * l)
                else:
                    pool.wait_ge(loaded_consts, 16)
                load_gain("ffn_norm", l)
                norm(m + PER - 1)

            if second:
                pool.wait_ge(xf_ready, NT * PER * DEPTH)
                load_gain("norm_w_2", 0)
                norm(PER * DEPTH)
                pool.wait_ge(s_sums_ready, 1)
                rstd_of(s_rstd, s_sums, S_DIM, s_rstd_ready)

        @block.tensor
        def _(pe):
            def gather(half, par, g, S, free_slot=None):
                if half == 0:
                    pe.wait_ge(S["hot_ready"], g + 1)
                for k in range(4):
                    for t in range(NT):
                        ins = pe.matmul(bank[4][:, k * P:(k + 1) * P], xf[:, t, 4 * half + k, :],
                                        onehot[:, par, t, :], start=(t == 0), stop=(t == NT - 1))
                        if free_slot is not None and k == 0 and t == 0:
                            ins.then_inc(free_slot, 1)
                ins.then_inc(S["gathered"], 1)

            def expert_pair(par, q, g, S, land, free, lands):
                pe.wait_ge(S["y_ready"], 2 * q + 1)
                for h, s in ((0, UP_LO[par]), (1, UP_HI[par])):
                    pe.wait_ge(land[s], lands(s))
                    pe.wait_ge(S["xg_ready"], 2 * g + (1 + h))
                    view = up_view(s)
                    for k in range(4):
                        for e in range(2):
                            ins = pe.matmul(bank[5][CELL * e:CELL * (e + 1), :],
                                            xg[:, par, 4 * h + k, CELL * e:CELL * (e + 1)], view[:, e, :, k, :],
                                            start=(h == 0 and k == 0), stop=(h == 1 and k == 3))
                            if h == 1 and k == 0 and e == 0:
                                ins.then_inc(free[UP_LO[par]], 1)
                ins.then_inc(S["up_done"], 1)
                gather(0, 1 - par, g + 1, S, free[UP_HI[par]])
                pe.wait_ge(S["hidden_ready"], q + 1)
                for c in range(2):
                    pe.transpose(bank[7][:, c * P:(c + 1) * P],
                                 hidden[:, par, :].rearrange("p (f c) -> p c f", c=2)[:, c, :], ident)
                for t in range(NT):
                    ins = pe.transpose(bank[7][:, (2 + t) * P:(3 + t) * P], onehot_w[:, par, t, :], ident)
                ins.then_inc(S["turn_done"], 1)
                pe.wait_ge(S["xg_ready"], 2 * g + 3)
                gather(1, 1 - par, g + 1, S)
                s = DOWN[par]
                pe.wait_ge(land[s], lands(s))
                pe.wait_ge(S["turned_ready"], q + 1)
                for n in range(2):
                    for c in range(2):
                        for e in range(2):
                            ins = pe.matmul(bank[6 - n][CELL * e:CELL * (e + 1), :],
                                            turned[:, par, c, CELL * e:CELL * (e + 1)],
                                            down_view(s)[:, e, c, n * HALF:(n + 1) * HALF],
                                            start=(c == 0), stop=(c == 1))
                    ins.then_inc(S["down_done"], 1)
                for n in range(2):
                    pe.wait_ge(S["y_ready"], 2 * q + (2 + n))
                    for t in range(NT):
                        ins = pe.matmul(bank[2 * t + n][:, :], turned[:, par, 2 + t, :], y[:, par, n, :],
                                        start=False, stop=False, skip_group_check=True)
                        if n == 0 and t == 0:
                            ins.then_inc(free[s], 1)

            zeros = const["zeros"].bitcast(BF16)

            def zero_acc(first):
                for b in range(4):
                    ins = pe.matmul(bank[b][:, :], zeros[:, 0:P], zeros, start=first, stop=not first,
                                    skip_group_check=True)
                return ins

            pe.wait_ge(loaded_consts, 16)
            for s in range(RING):
                pe.nop().then_inc(freed[s], 1)
            def turn(m):
                for t in range(NT):
                    pe.wait_ge(xf_ready, NT * m + t + 1)
                    for half in range(2):
                        u = 4 * m + 2 * t + half
                        if u >= 2:
                            pe.wait_ge(xfT_ready, u - 1)
                        for i in range(4):
                            ins = pe.transpose(bank[4 + u % 2][:, i * P:(i + 1) * P], xf[:, t, 4 * half + i, :], ident)
                        ins.then_inc(xf_turned, 1)
                pe.wait_ge(xfT_ready, 4 * m + 4)

            def mix(l):
                plan = plans[l]
                hd = slice(0, M_DIM)

                def open_bank(name):
                    b, n = plan[name]
                    if n > 1:
                        pe.wait_ge(drained[b], n - 1)
                    return bank[b]

                def done(ins, name):
                    ins.then_inc(filled[plan[name][0]], 1)

                def lands(s, n):
                    pe.wait_ge(landed[s], l * layer_lands[s] + 16 * n)

                def token_unit(u, t, release=None):
                    name = f"u{u}t{t}"
                    dst = open_bank(name)
                    w = UNIT_COLS[u][1] - UNIT_COLS[u][0]
                    lands(u, 1)
                    for k in range(KD):
                        ins = pe.matmul(dst[:, 0:w], xfT[:, k, t * P:(t + 1) * P], unit_view(u, w)[:, k, :],
                                        start=(k == 0), stop=(k == KD - 1))
                        if release is not None and k == 0:
                            ins.then_inc(freed[release], 1)
                    done(ins, name)

                def head_unit(u, i, name, release=None):
                    dst = open_bank(name)
                    lands(u, 1)
                    for h in range(2):
                        for k in range(KD):
                            ins = pe.matmul(dst[hd, h * SEQ:(h + 1) * SEQ],
                                            unit_view(u, M_WIDTH)[:, k, (2 * i + h) * M_DIM:(2 * i + h + 1) * M_DIM],
                                            xfT[:, k, :], start=(k == 0), stop=(k == KD - 1))
                            if release is not None and h == 0 and k == 0:
                                ins.then_inc(freed[release], 1)
                    done(ins, name)

                def turn_latent():
                    pe.wait_ge(latent_ready, NT * (l + 1))
                    for name, ks in (("cqT", (0, 1)), ("ckvT", (2,))):
                        dst = open_bank(name)
                        for i, k in enumerate(ks):
                            for t in range(NT):
                                ins = pe.transpose(dst[:, i * SEQ + t * P:i * SEQ + (t + 1) * P],
                                                   latent[:, t, k * P:(k + 1) * P], ident)
                        done(ins, name)

                def latent_q(t):
                    copied(pe, plan, "cqT")
                    for i, half in enumerate("ab"):
                        dst = open_bank(f"q{t}{half}")
                        w = 3 * QK_DIM
                        for k in range(2):
                            ins = pe.matmul(dst[:, 0:w], latentT[:, k, t * P:(t + 1) * P], w_uq[:, k, i * w:(i + 1) * w],
                                            start=(k == 0), stop=(k == 1))
                        done(ins, f"q{t}{half}")

                def latent_kv(t):
                    copied(pe, plan, "ckvT")
                    for i, half in enumerate("ab"):
                        dst = open_bank(f"kv{t}{half}")
                        w = 3 * (NOPE + V_DIM)
                        done(pe.matmul(dst[:, 0:w], latentT[:, 2, t * P:(t + 1) * P], w_ukv[:, i * w:(i + 1) * w],
                                       start=True, stop=True), f"kv{t}{half}")

                def spread(name, n):
                    dst = open_bank(name)
                    pe.wait_ge(diag_ready, 4 * l + n)
                    done(pe.matmul(dst[:, :], ones, diag[:, :, :].rearrange("p h s -> p (h s)"),
                                   start=True, stop=True), name)

                pe.wait_ge(loaded_mixer, MIXER_LOADS * (l + 1))
                dst = open_bank("conv_rows")
                for h in range(2 * M_HEADS):
                    pe.transpose(dst[hd, 5 * h:5 * h + 5], conv_rows[0:5, h * M_DIM:(h + 1) * M_DIM], ident[0:5, 0:5])
                done(pe.transpose(dst[:, 40:44], cb_rows[0:4, :], ident[0:4, 0:4]), "conv_rows")
                dst = open_bank("gate_w")
                for g in range(C_GROUPS):
                    ins = pe.transpose(dst[:, g * P:(g + 1) * P], gate_raw[:, g, :], ident)
                done(ins, "gate_w")

                token_unit(3, 0)
                token_unit(3, 1)
                token_unit(4, 0, 3)
                token_unit(4, 1)
                token_unit(5, 0, 4)
                token_unit(5, 1)
                head_unit(0, 0, "q01", 5)
                turn_latent()
                dst = open_bank("cum")
                pe.wait_ge(log_f_ready, l + 1)
                for t in range(NT):
                    pe.matmul(dst[:, 8 * t:8 * t + 4], const["upto"], log_f[:, t, :], start=True, stop=True)
                    ins = pe.matmul(dst[:, 8 * t + 4:8 * t + 8], ones, log_f[:, t, :], start=True, stop=True)
                done(ins, "cum")
                head_unit(0, 1, "q23")
                spread("rrow0", 1)
                spread("rrow1", 2)
                latent_q(0)
                head_unit(1, 0, "k01", 0)
                latent_q(1)
                spread("mrow0", 3)
                latent_kv(0)
                head_unit(1, 1, "k23")
                spread("mrow1", 4)
                latent_kv(1)
                copied(pe, plan, "gate_w")
                pe.wait_ge(gate_v_ready, l + 1)
                dst = open_bank("gated")
                for t in range(NT):
                    for g in range(C_GROUPS):
                        at = (t * C_GROUPS + g) * C_DIM
                        ins = pe.matmul(dst[:, at:at + C_DIM], gate_wT[:, g, :],
                                        gelu[:, t, C_WIDTH + g * C_DIM:C_WIDTH + (g + 1) * C_DIM], start=True, stop=True)
                done(ins, "gated")
                token_unit(2, 0, 1)
                token_unit(2, 1)

                for t in range(NT):
                    dst = open_bank(f"st{t}")
                    if t == 0:
                        pe.wait_ge(conv_act, 2 * (l + 1))
                    for h in range(M_HEADS):
                        ins = pe.matmul(dst[:, h * P:(h + 1) * P], conv_out[hd, M_HEADS + h, t * P:(t + 1) * P],
                                        conv_out[hd, h, t * P:(t + 1) * P], start=True, stop=True)
                        if t == 0 and h == 0:
                            ins.then_inc(freed[2], 1)
                    done(ins, f"st{t}")
                dst = open_bank("ktok")
                for h in range(M_HEADS):
                    ins = pe.transpose(dst[:, h * M_DIM:(h + 1) * M_DIM], conv_out[hd, M_HEADS + h, 0:P],
                                       ident[hd, 0:M_DIM])
                done(ins, "ktok")
                copied(pe, plan, "u2t0", "u2t1")
                dst = open_bank("state")
                pe.wait_ge(kw_ready, l + 1)
                for h in range(M_HEADS):
                    at = h * (M_DIM + 1)
                    pe.matmul(dst[hd, at:at + M_DIM], k_weighted[:, h, :], proj_a[:, 0, h * M_DIM:(h + 1) * M_DIM],
                              start=True, stop=True)
                    ins = pe.matmul(dst[hd, at + M_DIM:at + M_DIM + 1], k_weighted[:, h, :], ones[:, 0:1],
                                    start=True, stop=True)
                done(ins, "state")
                for t in range(NT):
                    dst = open_bank(f"num{t}")
                    pe.wait_ge(pt_ready, NT * l + t + 1)
                    for h in range(M_HEADS):
                        at = h * (M_DIM + 1)
                        pe.matmul(dst[:, at:at + M_DIM], decay[:, t, h, :], proj_a[:, t, h * M_DIM:(h + 1) * M_DIM],
                                  start=True, stop=True)
                        ins = pe.matmul(dst[:, at + M_DIM:at + M_DIM + 1], decay[:, t, h, :], ones[:, 0:1],
                                        start=True, stop=True)
                    done(ins, f"num{t}")
                copied(pe, plan, "state")
                dst = open_bank("inter")
                for h in range(M_HEADS):
                    at = h * (M_DIM + 1)
                    ins = pe.matmul(dst[:, at:at + M_DIM + 1], conv_out[hd, h, P:SEQ], state[hd, h, :],
                                    start=True, stop=True)
                done(ins, "inter")

                pe.wait_ge(qk_ready, NT * (l + 1))
                for i in range(6):
                    dst = open_bank(f"qkT{i}")
                    for j in range(2):
                        for t in range(NT):
                            ins = pe.transpose(dst[0:QK_DIM, j * SEQ + t * P:j * SEQ + (t + 1) * P],
                                               qk[:, t, 2 * i + j, :], ident)
                    done(ins, f"qkT{i}")
                copied(pe, plan, *[f"qkT{i}" for i in range(6)])

                def attend_scores(h):
                    dst = open_bank(f"sc{h}")
                    pe.matmul(dst[:, 0:P], qkT[0:QK_DIM, h, 0:P], qkT[0:QK_DIM, A_HEADS + h, 0:P], start=True, stop=True)
                    done(pe.matmul(dst[:, P:3 * P], qkT[0:QK_DIM, h, P:SEQ], qkT[0:QK_DIM, A_HEADS + h, :],
                                   start=True, stop=True), f"sc{h}")

                def attend_turn(h):
                    dst = open_bank(f"pT{h}")
                    pe.wait_ge(prob_ready, NT * (A_HEADS * l + h + 1))
                    for i in range(3):
                        ins = pe.transpose(dst[:, i * P:(i + 1) * P], prob[:, h % 2, i * P:(i + 1) * P], ident)
                    done(ins, f"pT{h}")

                o = [open_bank(f"o{t}") for t in range(NT)]

                def attend_values(h):
                    copied(pe, plan, f"pT{h}")
                    c = slice(h * V_DIM, (h + 1) * V_DIM)
                    pt = probT[:, h % 2, :]
                    ins = pe.matmul(o[0][:, c], pt[:, 0:P], kv[:, 0, h, NOPE:], start=True, stop=True)
                    if h == A_HEADS - 1:
                        done(ins, "o0")
                    pe.matmul(o[1][:, c], pt[:, P:2 * P], kv[:, 0, h, NOPE:], start=True, stop=False)
                    ins = pe.matmul(o[1][:, c], pt[:, 2 * P:3 * P], kv[:, 1, h, NOPE:], start=False, stop=True)
                    if h == A_HEADS - 1:
                        done(ins, "o1")

                attend_scores(0)
                for h in range(A_HEADS):
                    if h + 1 < A_HEADS:
                        attend_scores(h + 1)
                    attend_turn(h)
                    attend_values(h)

                for u in range(4):
                    t, half = u // 2, u % 2
                    dst = open_bank(f"yT{u}")
                    pe.wait_ge(y_rows, NT * l + t + 1)
                    for i in range(4):
                        ins = pe.transpose(dst[:, i * P:(i + 1) * P], xf[:, t, 4 * half + i, :], ident)
                    done(ins, f"yT{u}")
                copied(pe, plan, *[f"yT{u}" for u in range(4)])
                for n in range(2):
                    lands(n, 2)
                    for t in range(NT):
                        name = f"out{2 * t + n}"
                        dst = open_bank(name)
                        for k in range(KD):
                            ins = pe.matmul(dst[:, :], xfT[:, k, t * P:(t + 1) * P], unit_view(n, HALF)[:, k, :],
                                            start=(k == 0), stop=(k == KD - 1))
                            if n == 1 and t == 0 and k == 0:
                                ins.then_inc(freed[0], 1)
                        done(ins, name)

            for l in range(DEPTH):
                if mixer:
                    turn(PER * l)
                    mix(l)
                turn(PER * (l + 1) - 1)
                pe.wait_ge(loaded_ffn, ROUTER_LOADS * (l + 1))
                for t in range(NT):
                    for k in range(KD):
                        ins = pe.matmul(bank[6][:, t * 36:(t + 1) * 36], xfT[:, k, t * P:(t + 1) * P],
                                        w_router[:, k, :], start=(k == 0), stop=(k == KD - 1))
                        if mixer and t == 0 and k == 0:
                            ins.then_inc(freed[1], 1)
                ins.then_inc(logits_done, 1)
                if PER * (l + 1) > 1:
                    pe.wait_ge(x_ready, PER * (l + 1) - 1)
                zero_acc(True)
                pe.wait_ge(picked, l + 1)
                pe.matmul(bank[7][:, 0:NE], const["before"], work[:, 0, :], start=True, stop=True)
                pe.matmul(bank[7][:, NE:2 * NE], const["before"], work[:, 1, :], start=True, stop=False)
                pe.matmul(bank[7][:, NE:2 * NE], ones, work[:, 0, :], start=False, stop=True)
                pe.matmul(bank[7][:, 2 * NE:3 * NE], ones, work[:, 0, :], start=True, stop=False)
                pe.matmul(bank[7][:, 2 * NE:3 * NE], ones, work[:, 1, :], start=False, stop=True)\
                    .then_inc(counted, 1)
                g0 = l * (PAIRS + 1)
                gather(0, 0, g0, main)
                pe.wait_ge(main["xg_ready"], 2 * g0 + 1)
                gather(1, 0, g0, main)
                pe.wait_ge(main["xg_ready"], 2 * g0 + 2)
                with pe.Fori(0, PAIRS // 2) as j:
                    for par in range(2):
                        expert_pair(par, 2 * j + (l * PAIRS + par), 2 * j + (g0 + par), main, landed, freed,
                                    lambda s: j * pair_bytes[s]
                                    + (l * layer_lands[s] + 16 * mixer_uses[s] + pair_bytes[s]))
                        
                pe.wait_ge(over_ready, l + 1)
                n_over = pe.value_load(overint[0:1, l, CELLS_OVER:CELLS_OVER + 1], min_val=0, max_val=2)
                with pe.If(n_over > 0):
                    S = extra[l]
                    for s in range(RING):
                        pe.nop().then_inc(extra_freed[l][s], 1)
                    pe.wait_ge(main["xg_ready"], 2 * (g0 + PAIRS + 1))
                    gather(0, 0, 0, S)
                    pe.wait_ge(S["xg_ready"], 1)
                    gather(1, 0, 0, S)
                    pe.wait_ge(S["xg_ready"], 2)
                    with pe.Fori(0, n_over) as j:
                        for par in range(2):
                            expert_pair(par, 2 * j + par, 2 * j + par, S, extra_landed[l], extra_freed[l],
                                        lambda s: j * pair_bytes[s] + pair_bytes[s])
                with pe.Else():
                    pe.nop()
                zero_acc(False).then_inc(acc_done, 1)

            def last_block():
                plan = plan2
                step_no = PER * DEPTH

                def open_bank(name):
                    b, n = plan[name]
                    pe.wait_ge(drained[b], n - 1)
                    return bank[b]

                def done(ins, name):
                    ins.then_inc(filled[plan[name][0]], 1)

                def unit(name, cols):
                    s, n = unit2[name]
                    pe.wait_ge(landed[s], DEPTH * layer_lands[s] + 16 * n)
                    return ring[s][:, :].rearrange("p (k n) -> p k n", n=cols)

                behind = []

                def give_back(ins):
                    if behind:
                        ins.then_inc(freed[unit2[behind.pop()][0]], 1)

                def token_tile(u, t):
                    dst = open_bank(f"{u}{t}")
                    w = unit(u, HALF)
                    for k in range(KD):
                        ins = pe.matmul(dst[:, :], xfT[:, k, t * P:(t + 1) * P], w[:, k, :],
                                        start=(k == 0), stop=(k == KD - 1))
                        if k == 0:
                            give_back(ins)
                    done(ins, f"{u}{t}")
                    if t == 1:
                        behind.append(u)

                def pair_unit(u):
                    w = unit(u, HALF)
                    for half in range(2):
                        name = u + "AB"[half]
                        dst = open_bank(name)
                        for i in range(2):
                            at = (2 * half + i) * P
                            for k in range(KD):
                                ins = pe.matmul(dst[:, i * SEQ:(i + 1) * SEQ], w[:, k, at:at + P], xfT[:, k, :],
                                                start=(k == 0), stop=(k == KD - 1))
                                if k == 0:
                                    give_back(ins)
                        done(ins, name)
                    behind.append(u)

                pe.wait_ge(loaded_second, 4 * 16)
                pe.wait_ge(rel_ready, 1)
                dst = open_bank("rel")
                done(pe.transpose(dst[0:33, 0:S_HEADS], s_rel[0:S_HEADS, :], ident[0:S_HEADS, 0:S_HEADS]), "rel")
                copied(pe, plan, "rel")
                dst = open_bank("f")
                done(pe.matmul(dst[0:S_HEADS, 0:384], s_relT[0:33, :], buckets[0:33, :], start=True, stop=True), "f")

                for u in ("qa", "ka"):
                    for t in range(NT):
                        token_tile(u, t)
                pair_unit("qb")
                pair_unit("kb")
                for u in ("va", "vb"):
                    for t in range(NT):
                        token_tile(u, t)
                pe.wait_ge(s_qk_ready, 1)
                for a, kind in enumerate("qk"):
                    for t in range(NT):
                        dst = open_bank(f"{kind}T{t}")
                        for i in range(S_HEADS // 2):
                            ins = pe.transpose(dst[:, i * P:(i + 1) * P],
                                               s_qk[:, t, a * S_WIDTH + i * P:a * S_WIDTH + (i + 1) * P], ident)
                        done(ins, f"{kind}T{t}")
                copied(pe, plan, "qbA", "qbB", "kbA", "kbB", "va0", "va1", "vb0", "vb1", "qT0", "qT1", "kT0", "kT1")

                def first_stage(h):
                    rows_h = slice(S_DIM * (h % 2), S_DIM * (h % 2 + 1))
                    q, k = s_qkbT[rows_h, 0, h // 2, :], s_qkbT[rows_h, 1, h // 2, :]
                    dst = open_bank(f"z{h}")
                    pe.matmul(dst[:, 0:SEQ], k[:, 0:P], q, start=True, stop=False, skip_group_check=True)
                    done(pe.matmul(dst[:, SEQ:3 * P], k[:, P:], q[:, P:], start=False, stop=False,
                                   skip_group_check=True), f"z{h}")
                    q, k = s_qkaT[rows_h, 0, h // 2, :], s_qkaT[rows_h, 1, h // 2, :]
                    dst = open_bank(f"sc{h}")
                    pe.matmul(dst[:, 0:P], q[:, 0:P], k[:, 0:P], start=True, stop=True)
                    done(pe.matmul(dst[:, P:3 * P], q[:, P:], k, start=True, stop=True), f"sc{h}")

                def second_stage(h):
                    dst = open_bank(f"r{h}")
                    pe.wait_ge(s_log_ready, h + 1)
                    log = s_log[:, h % 2, :]
                    pe.matmul(dst[:, 0:SEQ], const["fromon"], log[:, 0:SEQ], start=False, stop=False,
                              skip_group_check=True)
                    pe.matmul(dst[:, P:SEQ], ones, log[:, SEQ:], start=False, stop=False, skip_group_check=True)
                    done(pe.matmul(dst[:, SEQ:3 * P], const["fromon"], log[:, SEQ:], start=False, stop=True,
                                   skip_group_check=True), f"r{h}")
                    dst = open_bank(f"pT{h}")
                    pe.wait_ge(s_prob_ready, NT * (h + 1))
                    for i in range(3):
                        ins = pe.transpose(dst[:, i * P:(i + 1) * P], s_prob[:, h % 2, i * P:(i + 1) * P], ident)
                    done(ins, f"pT{h}")

                def third_stage(h):
                    c = slice(h * S_DIM, (h + 1) * S_DIM)
                    for a, name, src in ((1, "ob", s_log), (0, "oa", s_probT)):
                        dst = open_bank(f"{name}{h}")
                        if a:
                            pe.wait_ge(s_weight_ready, h + 1)
                        w = src[:, h % 2, :]
                        pe.matmul(dst[:, 0:S_DIM], w[:, 0:P], s_v[:, a, 0, c], start=True, stop=True)
                        pe.matmul(dst[:, S_DIM:P], w[:, P:SEQ], s_v[:, a, 0, c], start=True, stop=False)
                        done(pe.matmul(dst[:, S_DIM:P], w[:, SEQ:], s_v[:, a, 1, c], start=False, stop=True),
                             f"{name}{h}")

                for h in range(S_HEADS + 1):
                    if h == 0:
                        pass
                    if h < S_HEADS:
                        first_stage(h)
                    front, back = step_tiles(h)
                    for n in front:
                        token_tile(n[:-1], int(n[-1]))
                    if h:
                        second_stage(h - 1)
                    for n in back:
                        token_tile(n[:-1], int(n[-1]))
                    if h:
                        third_stage(h - 1)

                pe.wait_ge(s_o_ready, 1)
                for i in range(4):
                    a, t = i // 2, i % 2
                    dst = open_bank(f"oT{i}")
                    for k in range(4):
                        ins = pe.transpose(dst[:, k * P:(k + 1) * P], s_o[:, a, t, k * P:(k + 1) * P], ident)
                        if k == 0:
                            give_back(ins)
                    done(ins, f"oT{i}")
                copied(pe, plan, *[f"oT{i}" for i in range(4)])
                for t in range(NT):
                    for n in range(2):
                        for a, u in enumerate(("upa", "upb")):
                            name = f"y{'ab'[a]}{t}{n}"
                            dst = open_bank(name)
                            w = unit(u, D)
                            for k in range(4):
                                ins = pe.matmul(dst[:, :], s_oT[:, a, k, t * P:(t + 1) * P],
                                                w[:, k, n * HALF:(n + 1) * HALF], start=(k == 0), stop=(k == 3))
                            done(ins, name)
                for u in range(4):
                    t, half = u // 2, u % 2
                    dst = open_bank(f"yT{u}")
                    pe.wait_ge(s_rows, t + 1)
                    for i in range(4):
                        ins = pe.transpose(dst[:, i * P:(i + 1) * P], xf[:, t, 4 * half + i, :], ident)
                    done(ins, f"yT{u}")
                copied(pe, plan, *[f"yT{u}" for u in range(4)])
                for n in range(2):
                    w = unit(f"out{n}", HALF)
                    for t in range(NT):
                        dst = open_bank(f"out{2 * t + n}")
                        for k in range(KD):
                            ins = pe.matmul(dst[:, :], xfT[:, k, t * P:(t + 1) * P], w[:, k, :],
                                            start=(k == 0), stop=(k == KD - 1))
                        done(ins, f"out{2 * t + n}")

            if second:
                turn(PER * DEPTH)
                last_block()

        @block.scalar
        def _(act):
            step = Chain(act, act_step)

            def copy_half(half, par, g, S):
                act.wait_ge(S["gathered"], 2 * g + (half + 1))
                act.activation(xg[:, par, 4 * half:4 * half + 4, :],
                               bank[4][:, :].rearrange("p (k s) -> p k s", k=4), ACT.Copy)\
                   .then_inc(S["xg_ready"], 1)

            def expert_pair(par, q, g, S):
                act.wait_ge(S["up_done"], q + 1)
                act.activation(silu[:, par, :], bank[5][:, 0:DE], ACT.Silu).then_inc(S["silu_ready"], 1)
                copy_half(0, 1 - par, g + 1, S)
                copy_half(1, 1 - par, g + 1, S)
                for n in range(2):
                    act.wait_ge(S["down_done"], 2 * q + (n + 1))
                    act.activation(y[:, par, n, :], bank[6 - n][:, :], ACT.Copy).then_inc(S["y_ready"], 1)

            def norm_turn(m):
                if m == 0:
                    act.wait_ge(loaded_x, 16)
                else:
                    act.wait_ge(x_ready, m)
                for t in range(NT):
                    if m or t:
                        act.wait_ge(squares, NT * m + t)
                    act.activation(square, x[:, t, :], ACT.Square, accum_out=stats[:, t:t + 1])\
                       .then_inc(squares, 1)
                for u in range(4 * m, 4 * m + 4):
                    act.wait_ge(xf_turned, u + 1)
                    t, half = u % 4 // 2, u % 2
                    act.activation(xfT[:, 4 * half:4 * half + 4, t * P:(t + 1) * P],
                                   bank[4 + u % 2][:, :].rearrange("p (k s) -> p k s", k=4), ACT.Copy)\
                       .then_inc(xfT_ready, 1)

            def mix(l):
                plan = plans[l]
                hd = slice(0, M_DIM)

                def copy_out(name, dst, src):
                    src_bank = full(act, plan, name)
                    act.activation(dst, src(src_bank), ACT.Copy).then_inc(left(plan, name), 1)

                def token_unit(u, t):
                    c0, c1 = UNIT_COLS[u][0] - A_COLS, UNIT_COLS[u][1] - A_COLS
                    src = full(act, plan, f"u{u}t{t}")
                    if c0 < A_COLS < c1:
                        w = A_COLS - c0
                        step(act.activation(proj_a[:, t, c0:], src[:, 0:w], ACT.Copy))
                        ins = act.activation(proj_b[:, t, 0:c1 - A_COLS], src[:, w:c1 - c0], ACT.Copy)
                    elif c0 < A_COLS:
                        ins = act.activation(proj_a[:, t, c0:c1], src[:, 0:c1 - c0], ACT.Copy)
                    else:
                        ins = act.activation(proj_b[:, t, c0 - A_COLS:c1 - A_COLS], src[:, 0:c1 - c0], ACT.Copy)
                    ins.then_inc(left(plan, f"u{u}t{t}"), 1)

                def heads(name, first):
                    copy_out(name, conv_raw[hd, first:first + 2, 3:],
                             lambda b: b[hd, :].rearrange("p (h s) -> p h s", h=2))

                def latent_q(t):
                    for i, half in enumerate("ab"):
                        copy_out(f"q{t}{half}", qk[:, t, 3 * i:3 * i + 3, :],
                                 lambda b: b[:, 0:3 * QK_DIM].rearrange("p (h d) -> p h d", h=3))

                def latent_kv(t):
                    for i, half in enumerate("ab"):
                        copy_out(f"kv{t}{half}", kv[:, t, 3 * i:3 * i + 3, :],
                                 lambda b: b[:, 0:3 * P].rearrange("p (h d) -> p h d", h=3))

                for t in range(NT):
                    token_unit(3, t)
                for t in range(NT):
                    token_unit(4, t)
                copied(act, plan, "u3t0", "u3t1", "u4t0", "u4t1")
                for i, (at, n) in enumerate(((CQ_AT, Q_RANK), (CKV_AT, KV_RANK))):
                    for t in range(NT):
                        if 4 * l + 2 * i + t:
                            act.wait_ge(latent_sums, 4 * l + 2 * i + t)
                        act.activation(square[:, 0:n], proj_b[:, t, at:at + n], ACT.Square,
                                       accum_out=head_sums[:, 2 * i + t:2 * i + t + 1]).then_inc(latent_sums, 1)
                act.wait_ge(gate_abs, l + 1)
                act.activation(gate_in[:, :, 2, 0:4], gate_in[:, :, 1, 4:8], ACT.Exp).then_inc(gate_exp, 1)
                act.wait_ge(gate_exp, l + 1)
                act.activation(gate_in[:, :, 2, 4:8], gate_in[:, :, 2, 0:4], ACT.Ln, bias=1.0).then_inc(gate_ln, 1)
                for t in range(NT):
                    token_unit(5, t)
                copied(act, plan, "u5t0", "u5t1")
                act.activation(gelu, proj_b[:, :, CU_AT:], ACT.Gelu_apprx_tanh).then_inc(gelu_ready, 1)
                act.wait_ge(latent_sums, 4 * l + 4)
                heads("q01", 0)
                copy_out("cqT", latentT[:, 0:2, :], lambda b: b[:, :].rearrange("p (k s) -> p k s", k=2))
                copy_out("ckvT", latentT[:, 2, :], lambda b: b[:, 0:SEQ])
                heads("q23", 2)
                latent_q(0)
                heads("k01", 4)
                latent_q(1)
                act.wait_ge(latent_ready, NT * (l + 1))
                act.wait_ge(gelu_ready, l + 1)
                latent_kv(0)
                heads("k23", 6)
                latent_kv(1)
                for t in range(NT):
                    token_unit(2, t)
                for t in range(NT):
                    act.wait_ge(decay_wanted, NT * l + t + 1)
                    act.activation(decay[:, t, :, :], decay[:, t, :, :], ACT.Exp).then_inc(decay_done, 1)
                act.activation(small_exp, small_exp, ACT.Exp).then_inc(decay_done, 1)
                for i in range(2):
                    act.wait_ge(conv_ready, 2 * l + i + 1)
                    part = conv_out[hd, M_HEADS * i:M_HEADS * (i + 1), :]
                    act.activation(part, part, ACT.Silu).then_inc(conv_act, 1)
                copied(act, plan, "u2t0", "u2t1")
                act.activation(proj_a[:, :, M_WIDTH:], proj_a[:, :, M_WIDTH:], ACT.Sigmoid).then_inc(out_gate, 1)
                copy_out("state", state[hd, :, :],
                         lambda b: b[hd, 0:M_HEADS * (M_DIM + 1)].rearrange("p (h d) -> p h d", h=M_HEADS))
                for i in range(6):
                    copy_out(f"qkT{i}", qkT[0:QK_DIM, 2 * i:2 * i + 2, :],
                             lambda b: b[0:QK_DIM, :].rearrange("p (h s) -> p h s", h=2))
                for h in range(A_HEADS):
                    act.wait_ge(logits_ready, A_HEADS * l + h + 1)
                    for t, c in ((0, slice(0, P)), (1, slice(P, 3 * P))):
                        act.activation(prob[:, h % 2, c], prob[:, h % 2, c], ACT.Exp, bias=soft[:, h, 0, t:t + 1],
                                       accum_out=soft[:, h, 1, t:t + 1]).then_inc(prob_ready, 1)
                    copy_out(f"pT{h}", probT[:, h % 2, :], lambda b: b[:, 0:3 * P])
                for u in range(4):
                    t, half = u // 2, u % 2
                    copy_out(f"yT{u}", xfT[:, 4 * half:4 * half + 4, t * P:(t + 1) * P],
                             lambda b: b[:, :].rearrange("p (k s) -> p k s", k=4))

            if mixer:
                act.wait_ge(angles, 1)
                act.activation(cos_sin[:, :, :, :], cos_sin[:, :, :, :], ACT.Sin).then_inc(rope_ready, 1)
            act.nop().then_inc(main["y_ready"], 1)
            for l in range(DEPTH):
                if mixer:
                    norm_turn(PER * l)
                    mix(l)
                norm_turn(PER * (l + 1) - 1)
                act.wait_ge(exp_wanted, l + 1)
                act.activation(expout[:, :, 0:7], expin[:, :, 0:7], ACT.Exp).then_inc(exp_done, 1)
                g0 = l * (PAIRS + 1)
                copy_half(0, 0, g0, main)
                copy_half(1, 0, g0, main)
                with act.Fori(0, PAIRS // 2) as j:
                    for par in range(2):
                        expert_pair(par, 2 * j + (l * PAIRS + par), 2 * j + (g0 + par), main)
                act.wait_ge(over_ready, l + 1)
                n_over = act.value_load(overint[0:1, l, CELLS_OVER:CELLS_OVER + 1], min_val=0, max_val=2)
                with act.If(n_over > 0):
                    S = extra[l]
                    act.nop().then_inc(S["y_ready"], 1)
                    copy_half(0, 0, 0, S)
                    copy_half(1, 0, 0, S)
                    with act.Fori(0, n_over) as j:
                        for par in range(2):
                            expert_pair(par, 2 * j + par, 2 * j + par, S)
                with act.Else():
                    act.nop()

            def last_block():
                plan = plan2

                def copy_out(name, dst, src, scale=1.0):
                    src_bank = full(act, plan, name)
                    act.activation(dst, src(src_bank), ACT.Copy, scale=scale).then_inc(left(plan, name), 1)

                whole = lambda b: b[:, :]
                for a, u in enumerate(("qa", "ka")):
                    for t in range(NT):
                        copy_out(f"{u}{t}", s_qk[:, t, a * S_WIDTH:(a + 1) * S_WIDTH], whole)
                for a, u in enumerate(("qb", "kb")):
                    for half in range(2):
                        copy_out(u + "AB"[half], s_qkbT[:, a, 2 * half:2 * half + 2, :],
                                 lambda b: b[:, :].rearrange("p (i s) -> p i s", i=2),
                                 scale=1.0 if a else float(S_DIM) ** -0.5)
                for a, u in enumerate(("va", "vb")):
                    for t in range(NT):
                        copy_out(f"{u}{t}", s_v[:, a, t, :], whole)
                for a, kind in enumerate("qk"):
                    for t in range(NT):
                        copy_out(f"{kind}T{t}", s_qkaT[:, a, :, t * P:(t + 1) * P],
                                 lambda b: b[:, :].rearrange("p (i s) -> p i s", i=4))
                steps = [0]

                def in_place(dst, src, func, **kw):
                    steps[0] += 1
                    act.activation(dst, src, func, **kw).then_inc(s_act, 1)
                    act.wait_ge(s_act, steps[0])

                def z_tile(n):
                    if n[0] == "z":
                        copy_out(n, s_z[:, "ab".index(n[1]), int(n[-1]), :], whole)

                for h in range(S_HEADS + 1):
                    front, back = step_tiles(h)
                    if h < S_HEADS:
                        log = s_log[:, h % 2, :]
                        src = full(act, plan, f"z{h}")[:, 0:3 * P]
                        if h >= 2:
                            copied(act, plan, f"ob{h - 2}")
                        in_place(log, src, ACT.Abs)
                        in_place(log, log, ACT.Exp, scale=-1.0)
                        act.activation(log, log, ACT.Ln, bias=1.0).then_inc(s_ln_ready, 1)
                    for n in front:
                        z_tile(n)
                    if h < S_HEADS:
                        act.wait_ge(s_logits_ready, h + 1)
                        for t, c in ((0, slice(0, P)), (1, slice(P, 3 * P))):
                            act.activation(s_prob[:, h % 2, c], s_prob[:, h % 2, c], ACT.Exp,
                                           bias=s_soft[:, h, 0, t:t + 1], accum_out=s_soft[:, h, 1, t:t + 1])\
                               .then_inc(s_prob_ready, 1)
                    if h:
                        g = h - 1
                        copy_out(f"pT{g}", s_probT[:, g % 2, :], lambda b: b[:, 0:3 * P])
                        copied(act, plan, f"r{g}")
                        act.activation(s_log[:, g % 2, :], s_log[:, g % 2, :], ACT.Exp).then_inc(s_weight_ready, 1)
                    for n in back:
                        z_tile(n)
                copied(act, plan, "za0", "za1", "zb0", "zb1")
                act.activation(s_z, s_z, ACT.Silu).then_inc(s_silu_ready, 1)
                act.wait_ge(s_gates_in, 1)
                act.activation(s_gates, s_gates, ACT.Sigmoid).then_inc(s_gate_ready, 1)
                for i in range(4):
                    a, t = i // 2, i % 2
                    copy_out(f"oT{i}", s_oT[:, a, :, t * P:(t + 1) * P],
                             lambda b: b[:, :].rearrange("p (k s) -> p k s", k=4))
                for u in range(4):
                    t, half = u // 2, u % 2
                    copy_out(f"yT{u}", xfT[:, 4 * half:4 * half + 4, t * P:(t + 1) * P],
                             lambda b: b[:, :].rearrange("p (k s) -> p k s", k=4))

            if second:
                norm_turn(PER * DEPTH)
                last_block()

        @block.vector
        def _(dve):
            step = Chain(dve, vec_step)

            def build_hot(par, S, link):
                for t in range(NT):
                    a, b = slot_of[:, 0, t:t + 1], slot_of[:, 1, t:t + 1]
                    wa, wb = gates[:, 0, t:t + 1], gates[:, 1, t:t + 1]
                    link(dve.tensor_scalar(hotwork[:, :], slotrow[:, :], a, None, ALU.is_equal))
                    link(dve.scalar_tensor_tensor(onehot[:, par, t, :], slotrow[:, :], b, hotwork[:, :],
                                                  ALU.is_equal, ALU.add))
                    link(dve.tensor_scalar(hotwork[:, :], slotrow[:, :], a, wa, ALU.is_equal, ALU.mult))
                    link(dve.tensor_scalar(onehot_w[:, par, t, :], slotrow[:, :], b, wb, ALU.is_equal, ALU.mult))
                    link(dve.tensor_tensor(onehot_w[:, par, t, :], onehot_w[:, par, t, :], hotwork[:, :], ALU.add))
                dve.tensor_scalar(slotrow[:, :], slotrow[:, :], float(P), None, ALU.add).then_inc(S["hot_ready"], 1)

            HOT_LINKS = 5 * NT

            def expert_pair(par, q, g, S):
                link = Chain(dve, S["vec"], HOT_LINKS * g + HOT_LINKS)
                dve.wait_ge(S["hot_ready"], g + 1)
                build_hot(1 - par, S, link)
                dve.wait_ge(S["silu_ready"], q + 1)
                dve.tensor_tensor(hidden[:, par, :], silu[:, par, :], bank[5][:, DE:2 * DE], ALU.mult)\
                   .then_inc(S["hidden_ready"], 1)
                dve.wait_ge(S["turn_done"], q + 1)
                dve.tensor_copy(turned[:, par, :, :], bank[7][:, :].rearrange("p (c s) -> p c s", c=4))\
                   .then_inc(S["turned_ready"], 1)

            def first_of(dst, src, n, link):
                m = rowmax[:, :]
                mb = rowmax[:, :].unsqueeze(2).broadcast_to([P, NT, n])
                rev = const["rev"][:, 0:n].unsqueeze(1).broadcast_to([P, NT, n])
                link(dve.tensor_reduce(m, src, AX.X, ALU.max))
                link(dve.tensor_tensor(dst, src, mb, ALU.is_equal))
                link(dve.tensor_tensor(dst, dst, rev, ALU.mult))
                link(dve.tensor_reduce(m, dst, AX.X, ALU.max))
                link(dve.tensor_tensor(dst, dst, mb, ALU.is_equal))

            def route(l):
                gl, el = logits[:, :, 0:N_GROUPS], logits[:, :, N_GROUPS:]
                bias = router_bias[:, :].unsqueeze(1).broadcast_to([P, NT, 36])
                gw = [groupwork[:, :, i, :] for i in range(3)]
                rb = lambda n: rowmax[:, :].unsqueeze(2).broadcast_to([P, NT, n])
                dve.wait_ge(logits_done, l + 1)
                step(dve.tensor_copy(logits[:, :, :], bank[6][:, 0:72].rearrange("p (t n) -> p t n", t=NT)))
                step(dve.tensor_tensor(gw[0], gl, bias[:, :, 0:N_GROUPS], ALU.add))
                first_of(gw[1], gw[0], N_GROUPS, step)
                step(dve.tensor_reduce(rowmax[:, :], gl, AX.X, ALU.max))
                step(dve.tensor_tensor(expin[:, :, 0:N_GROUPS], gl, rb(N_GROUPS), ALU.subtract))
                step(dve.tensor_tensor(gw[2], expin[:, :, 0:N_GROUPS], gw[1], ALU.mult))
                step(dve.tensor_reduce(expin[:, :, 4:5], gw[2], AX.X, ALU.add))
                step(dve.tensor_scalar(gw[2], gw[1], -1.0, -NEG, ALU.add, ALU.mult))
                out_of = gw[2].unsqueeze(3).broadcast_to([P, NT, N_GROUPS, PER_GROUP])
                four = "p t (g e) -> p t g e"
                step(dve.tensor_tensor(scores[:, :, :].rearrange(four, g=N_GROUPS), el.rearrange(four, g=N_GROUPS),
                                       out_of, ALU.add))
                step(dve.tensor_reduce(rowmax[:, :], scores[:, :, :], AX.X, ALU.max))
                step(dve.tensor_copy(expin[:, :, 7:8], rowmax[:, :].unsqueeze(2)))
                step(dve.tensor_tensor(scores[:, :, :], scores[:, :, :], bias[:, :, N_GROUPS:], ALU.add))
                first_of(pick[:, :, 0, :], scores[:, :, :], NE, step)
                step(dve.scalar_tensor_tensor(scores[:, :, :], pick[:, :, 0, :], 4 * NEG, scores[:, :, :],
                                              ALU.mult, ALU.add))
                first_of(pick[:, :, 1, :], scores[:, :, :], NE, step)
                for i in range(2):
                    step(dve.tensor_tensor(scores[:, :, :], pick[:, :, i, :], el, ALU.mult))
                    step(dve.tensor_reduce(expin[:, :, 5 + i:6 + i], scores[:, :, :], AX.X, ALU.add))
                step(dve.tensor_tensor(expin[:, :, 5:7], expin[:, :, 5:7],
                                       expin[:, :, 7:8].broadcast_to([P, NT, 2]), ALU.subtract))
                dve.nop().then_inc(exp_wanted, 1)
                dve.tensor_tensor(work[:, :, :], pick[:, :, 0, :], pick[:, :, 1, :], ALU.add).then_inc(picked, 1)
                dve.wait_ge(exp_done, l + 1)
                step(dve.tensor_reduce(expin[:, :, 0:1], expout[:, :, 0:N_GROUPS], AX.X, ALU.add))
                step(dve.tensor_tensor(expin[:, :, 1:2], expout[:, :, 5:6], expout[:, :, 6:7], ALU.add))
                step(dve.tensor_tensor(expin[:, :, 0:1], expin[:, :, 0:1], expin[:, :, 1:2], ALU.mult))
                step(dve.reciprocal(expin[:, :, 0:1], expin[:, :, 0:1]))
                step(dve.tensor_tensor(expin[:, :, 0:1], expin[:, :, 0:1], expout[:, :, 4:5], ALU.mult))
                for i in range(2):
                    step(dve.tensor_tensor(gates[:, i, :], expin[:, :, 0:1].rearrange("p t o -> p (t o)"),
                                           expout[:, :, 5 + i:6 + i].rearrange("p t o -> p (t o)"), ALU.mult))
                dve.wait_ge(counted, l + 1)
                step(dve.tensor_copy(position[:, :, :], bank[7][:, 0:3 * NE].rearrange("p (t e) -> p t e", e=NE)))
                count = position[:, NT, :]
                cells, ahead, total = over[:, 0, :], over[:, 1, :], over[:, 2, :]
                step(dve.tensor_scalar(cells, count, CELL + 0.5, None, ALU.is_gt))
                for lim in range(2 * CELL, SEQ, CELL):
                    step(dve.scalar_tensor_tensor(cells, count, lim + 0.5, cells, ALU.is_gt, ALU.add))
                step(dve.tensor_copy(total, cells))
                a, b = total, ahead
                for sh in (1, 2, 4, 8, 16):
                    step(dve.tensor_copy(b, a))
                    step(dve.tensor_tensor(b[:, sh:], a[:, sh:], a[:, 0:NE - sh], ALU.add))
                    a, b = b, a
                total = a
                cidx = const["iota"][:, 0:CELLS_OVER].unsqueeze(2).broadcast_to([P, CELLS_OVER, NE])
                step(dve.tensor_tensor(overlist[:, :, :], total.unsqueeze(1).broadcast_to([P, CELLS_OVER, NE]), cidx,
                                       ALU.is_le))
                step(dve.tensor_reduce(oversum[:, 0:CELLS_OVER], overlist[:, :, :], AX.X, ALU.add))
                step(dve.tensor_scalar(oversum[:, 0:CELLS_OVER], oversum[:, 0:CELLS_OVER], float(NE - 1), None, ALU.min))
                last = total[:, NE - 1:NE]
                step(dve.tensor_scalar(oversum[:, CELLS_OVER:], last, 4.5, None, ALU.is_gt))
                step(dve.scalar_tensor_tensor(oversum[:, CELLS_OVER:], last, 0.5, oversum[:, CELLS_OVER:],
                                              ALU.is_gt, ALU.add))
                dve.tensor_copy(overint[0:1, l, :], oversum[0:1, :]).then_inc(over_ready, 1)
                step(dve.tensor_tensor(b, total, cells, ALU.subtract))
                step(dve.tensor_scalar(b, b, float(CELL), float(CELL * (NE - 1)), ALU.mult, ALU.add))
                step(dve.tensor_tensor(b, b, const["cell64"], ALU.subtract))
                pos = position[:, 0:NT, :]
                step(dve.tensor_scalar(scores[:, :, :], pos, CELL - 0.5, None, ALU.is_gt))
                step(dve.tensor_tensor(scores[:, :, :], scores[:, :, :], b.unsqueeze(1).broadcast_to([P, NT, NE]),
                                       ALU.mult))
                step(dve.tensor_tensor(scores[:, :, :], scores[:, :, :], pos, ALU.add))
                step(dve.tensor_tensor(scores[:, :, :], scores[:, :, :],
                                       const["cell64"].unsqueeze(1).broadcast_to([P, NT, NE]), ALU.add))
                for i in range(2):
                    step(dve.tensor_tensor(pick[:, :, i, :], pick[:, :, i, :], scores[:, :, :], ALU.mult))
                    step(dve.tensor_reduce(slot_of[:, i, :], pick[:, :, i, :], AX.X, ALU.add))

            def norm(m, by_chunk, gains):
                dve.wait_ge(loaded_gain, 16 * gains)
                for t in range(NT):
                    dve.wait_ge(rstd_ready, NT * m + t + 1)
                    dve.scalar_tensor_tensor(xf[:, t, :, :], x[:, t, :].rearrange(by_chunk, k=KD),
                                             stats[:, 8 + t:9 + t], gain[:, :].rearrange(by_chunk, k=KD),
                                             ALU.mult, ALU.mult).then_inc(xf_ready, 1)

            def rope_tables():
                two_pi = 2.0 * np.pi
                c1 = 6.28125
                c2 = float(np.float32(np.round((two_pi - c1) * 2.0 ** 20) / 2.0 ** 20))
                c3 = two_pi - c1 - c2
                pos = gate_in[:, :, 0, 0:1]
                ang, turns, r = [place(turned_at + 32 * i, NT, 16) for i in range(3)]
                magic = 12582912.0
                dve.wait_ge(loaded_positions, 16)
                step(dve.tensor_copy(pos, positions[:, :].unsqueeze(2)))
                step(dve.tensor_tensor(ang, pos.broadcast_to([P, NT, 16]),
                                       const["inv_freq"].unsqueeze(1).broadcast_to([P, NT, 16]), ALU.mult))
                for i, quarter in ((0, 0.25), (1, 0.0)):
                    step(dve.tensor_scalar(turns, ang, 1.0 / two_pi, quarter, ALU.mult, ALU.add))
                    step(dve.tensor_scalar(turns, turns, magic, None, ALU.add))
                    step(dve.tensor_scalar(turns, turns, -magic, None, ALU.add))
                    step(dve.scalar_tensor_tensor(r, turns, -c1, ang, ALU.mult, ALU.add))
                    step(dve.scalar_tensor_tensor(r, turns, -c2, r, ALU.mult, ALU.add))
                    step(dve.scalar_tensor_tensor(r, turns, -c3, r, ALU.mult, ALU.add))
                    step(dve.tensor_scalar(r, r, quarter * two_pi, 3.1415925, ALU.add, ALU.min))
                    ins = dve.tensor_scalar(cos_sin[:, i, :, :], r, -3.1415925, None, ALU.max)
                    if i == 0:
                        step(ins)
                ins.then_inc(angles, 1)

            def mix(l):
                plan = plans[l]
                hd = slice(0, M_DIM)
                rows = xf[:, :, :, :].rearrange("p t k i -> p t (k i)")

                def spread(ap, *shape):
                    return ap.broadcast_to([P, *shape])

                def rstds(n):
                    dve.wait_ge(head_rstd_ready, 4 * l + n)

                src = full(dve, plan, "conv_rows")
                step(dve.tensor_copy(conv_w[hd, :, :], src[hd, 0:40].rearrange("p (h j) -> p h j", j=5)))
                dve.tensor_copy(cb, src[:, 40:44]).then_inc(left(plan, "conv_rows"), 1)
                src = full(dve, plan, "gate_w")
                dve.tensor_tensor(gate_wT, src[:, :].rearrange("p (g s) -> p g s", g=C_GROUPS),
                                  spread(const["upto"].unsqueeze(1), C_GROUPS, P), ALU.mult)\
                   .then_inc(left(plan, "gate_w"), 1)
                copied(dve, plan, "u3t0", "u3t1")
                z, na = gate_in[:, :, 0, :], gate_in[:, :, 1, :]
                step(dve.tensor_tensor(z, proj_b[:, :, GATE_AT:GATE_AT + 8], spread(gate_bias.unsqueeze(1), NT, 8),
                                       ALU.add))
                step(dve.tensor_scalar(na, z, -1.0, None, ALU.mult))
                dve.tensor_tensor(na, na, z, ALU.min).then_inc(gate_abs, 1)
                copied(dve, plan, "u4t0", "u4t1")
                for t in range(NT):
                    step(dve.tensor_copy(qk[:, t, A_HEADS:, NOPE:],
                                         spread(proj_b[:, t, KR_AT:KR_AT + ROPE].unsqueeze(1), A_HEADS, ROPE)))
                dve.wait_ge(gate_ln, l + 1)
                dve.scalar_tensor_tensor(log_f, z[:, :, 4:8], 0.0, gate_in[:, :, 2, 4:8], ALU.min, ALU.subtract)\
                   .then_inc(log_f_ready, 1)
                rstds(1)
                step(dve.memset(conv_raw[hd, :, 0:3], 0.0))
                for t in range(NT):
                    step(dve.scalar_tensor_tensor(latent[:, t, 0:Q_RANK], proj_b[:, t, CQ_AT:CQ_AT + Q_RANK],
                                                  head_rstd[:, t:t + 1], latent_gain[:, 0:Q_RANK], ALU.mult, ALU.mult))
                    dve.scalar_tensor_tensor(latent[:, t, Q_RANK:], proj_b[:, t, CKV_AT:CKV_AT + KV_RANK],
                                             head_rstd[:, 2 + t:3 + t], latent_gain[:, Q_RANK:], ALU.mult, ALU.mult)\
                       .then_inc(latent_ready, 1)

                def diagonal(v):
                    dve.tensor_tensor(diag, spread(ident.unsqueeze(1), M_HEADS, P), spread(v.unsqueeze(2), M_HEADS, P),
                                      ALU.mult).then_inc(diag_ready, 1)

                def causal_max(name, t):
                    src = full(dve, plan, name)
                    dve.tensor_tensor(masked, src[:, :].rearrange("p (h s) -> p h s", h=M_HEADS),
                                      spread(const["causal"][:, P:].unsqueeze(1), M_HEADS, P), ALU.add)\
                       .then_inc(left(plan, name), 1)
                    copied(dve, plan, name)
                    step(dve.tensor_reduce(run_max[:, t, :], masked, AX.X, ALU.max))

                def decays(t):
                    name = f"mrow{t}"
                    src = full(dve, plan, name)[:, :].rearrange("p (h s) -> p h s", h=M_HEADS)
                    if t == 0:
                        step(dve.tensor_tensor(carry, cum[:, 0, 1, :],
                                               src[:, :, P - 1:P].rearrange("p h o -> p (h o)"), ALU.add))
                    dve.tensor_tensor(decay[:, t, :, :], spread(const["causal_t"].unsqueeze(1), M_HEADS, P), src,
                                      ALU.subtract).then_inc(left(plan, name), 1)
                    copied(dve, plan, name)
                    return dve.tensor_tensor(decay[:, t, :, :], decay[:, t, :, :],
                                             spread(rel[:, t, :].unsqueeze(2), M_HEADS, P), ALU.add)

                src = full(dve, plan, "cum")
                dve.tensor_copy(cum, src[:, 0:16].rearrange("p (t n h) -> p t n h", t=NT, n=2))\
                   .then_inc(left(plan, "cum"), 1)
                copied(dve, plan, "cum")
                step(dve.tensor_tensor(rel, z[:, :, 0:4], cum[:, :, 0, :], ALU.subtract))
                diagonal(rel[:, 0, :])
                causal_max("rrow0", 0)
                step(dve.tensor_scalar(run_max[:, 0, :], run_max[:, 0, :], 0.0, None, ALU.max))
                diagonal(rel[:, 1, :])
                causal_max("rrow1", 1)
                diagonal(run_max[:, 0, :])
                dve.wait_ge(gelu_ready, l + 1)
                gv = gelu[:, :, C_WIDTH:]
                v_square = place(small_at + 772, NT, C_WIDTH)
                v_groups = [gv[:, t, :].rearrange("p (g d) -> p g d", g=C_GROUPS) for t in range(NT)]
                step(dve.tensor_tensor(v_square, gv, gv, ALU.mult))
                dve.tensor_reduce(head_sums[:, 4:12].rearrange("p (t g) -> p t g", t=NT),
                                  v_square.rearrange("p t (g d) -> p t g d", g=C_GROUPS), AX.X, ALU.add)\
                   .then_inc(head_sums_ready, 1)
                rstds(2)
                for t in range(NT):
                    step(dve.tensor_tensor(v_groups[t], v_groups[t],
                                           spread(head_rstd[:, 4 + 4 * t:8 + 4 * t].unsqueeze(2), C_GROUPS, C_DIM),
                                           ALU.mult))
                dve.tensor_tensor(gv, gv, spread(cv_gain.unsqueeze(1), NT, C_WIDTH), ALU.mult)\
                   .then_inc(gate_v_ready, 1)
                decays(0).then_inc(decay_wanted, 1)
                step(dve.tensor_tensor(run_max[:, 1, :], run_max[:, 1, :], carry, ALU.max))
                diagonal(run_max[:, 1, :])
                step(dve.tensor_tensor(small_exp[:, 0, :], carry, run_max[:, 1, :], ALU.subtract))
                step(dve.tensor_tensor(small_exp[:, 1:3, :], cum[:, :, 0, :], run_max, ALU.add))
                step(dve.tensor_scalar(small_exp[:, 1:3, :], small_exp[:, 1:3, :], -1.0, None, ALU.mult))
                decays(1).then_inc(decay_wanted, 1)
                for i, names in enumerate((("q01", "q23"), ("k01", "k23"))):
                    copied(dve, plan, *names)
                    for h in range(M_HEADS * i, M_HEADS * (i + 1)):
                        dst = conv_out[hd, h, :]
                        step(dve.tensor_scalar(dst, conv_raw[hd, h, 3:3 + SEQ], conv_w[hd, h, 3:4], conv_w[hd, h, 4:5],
                                               ALU.mult, ALU.add))
                        for j in range(3):
                            ins = dve.scalar_tensor_tensor(dst, conv_raw[hd, h, j:j + SEQ], conv_w[hd, h, j:j + 1],
                                                           dst, ALU.mult, ALU.add)
                            if j < 2 or h % M_HEADS < M_HEADS - 1:
                                step(ins)
                    ins.then_inc(conv_ready, 1)
                src = full(dve, plan, "gated")
                out_c = rows[:, :, M_WIDTH + A_WIDTH:]
                for t in range(NT):
                    o = out_c[:, t, :].rearrange("p (g d) -> p g d", g=C_GROUPS)
                    ins = dve.tensor_tensor(o, src[:, t * C_WIDTH:(t + 1) * C_WIDTH].rearrange("p (g d) -> p g d",
                                                                                              g=C_GROUPS),
                                            spread(cb.unsqueeze(2), C_GROUPS, C_DIM), ALU.add)
                    if t == 0:
                        step(ins)
                ins.then_inc(left(plan, "gated"), 1)
                copied(dve, plan, "gated")
                step(dve.tensor_tensor(out_c, out_c, gelu[:, :, 0:C_WIDTH], ALU.mult))
                for t in range(NT):
                    copied(dve, plan, f"q{t}a", f"q{t}b", f"kv{t}a", f"kv{t}b")
                    step(dve.tensor_copy(qk[:, t, A_HEADS:, 0:NOPE], kv[:, t, :, 0:NOPE]))
                    step(dve.tensor_tensor(qk_square, qk[:, t, :, :], qk[:, t, :, :], ALU.mult))
                    ins = dve.tensor_reduce(head_sums[:, 12 + 12 * t:24 + 12 * t], qk_square, AX.X, ALU.add)
                    if t == 0:
                        step(ins)
                ins.then_inc(head_sums_ready, 1)
                scale = float(M_DIM) ** -0.5
                dve.wait_ge(decay_done, 3 * (l + 1))
                keep = carry
                step(dve.tensor_copy(keep, decay[:, 0, :, P - 1:P].rearrange("p h o -> p (h o)")))
                for t in range(NT):
                    src = full(dve, plan, f"st{t}")
                    dve.scalar_tensor_tensor(decay[:, t, :, :], src[:, :].rearrange("p (h s) -> p h s", h=M_HEADS),
                                             scale, decay[:, t, :, :], ALU.mult, ALU.mult)\
                       .then_inc(left(plan, f"st{t}"), 1)
                    copied(dve, plan, f"st{t}")
                    dve.nop().then_inc(pt_ready, 1)
                src = full(dve, plan, "ktok")
                dve.scalar_tensor_tensor(k_weighted, src[:, 0:M_WIDTH].rearrange("p (h d) -> p h d", h=M_HEADS), scale,
                                         spread(keep.unsqueeze(2), M_HEADS, M_DIM), ALU.mult, ALU.mult)\
                   .then_inc(left(plan, "ktok"), 1)
                copied(dve, plan, "ktok")
                dve.nop().then_inc(kw_ready, 1)
                rstds(3)
                if l == 0:
                    dve.wait_ge(rope_ready, 1)
                n = 2 * A_HEADS
                half = ROPE // 2
                for t in range(NT):
                    heads = qk[:, t, :, :]
                    step(dve.tensor_tensor(heads, heads, spread(head_rstd[:, 12 + 12 * t:24 + 12 * t].unsqueeze(2), n,
                                                                QK_DIM), ALU.mult))
                    for i in range(2):
                        part = heads[:, A_HEADS * i:A_HEADS * (i + 1), :]
                        step(dve.tensor_tensor(part, part, spread(qk_gain[:, i, :].unsqueeze(1), A_HEADS, QK_DIM),
                                               ALU.mult))
                    a, b = heads[:, :, NOPE:NOPE + half], heads[:, :, NOPE + half:]
                    c = spread(cos_sin[:, 0, t, :].unsqueeze(1), n, half)
                    si = spread(cos_sin[:, 1, t, :].unsqueeze(1), n, half)
                    w = [rope_work[:, i, :, :] for i in range(4)]
                    step(dve.tensor_tensor(w[0], a, c, ALU.mult))
                    step(dve.tensor_tensor(w[1], b, si, ALU.mult))
                    step(dve.tensor_tensor(w[2], a, si, ALU.mult))
                    step(dve.tensor_tensor(w[3], b, c, ALU.mult))
                    step(dve.tensor_tensor(a, w[0], w[1], ALU.subtract))
                    dve.tensor_tensor(b, w[2], w[3], ALU.add).then_inc(qk_ready, 1)
                by_head = lambda b: b[:, 0:M_HEADS * (M_DIM + 1)].rearrange("p (h d) -> p h d", h=M_HEADS)
                src = by_head(full(dve, plan, "num0"))
                dve.tensor_copy(total[:, 0, :, :], src).then_inc(left(plan, "num0"), 1)
                copied(dve, plan, "num0")
                src = by_head(full(dve, plan, "inter"))
                dve.tensor_tensor(total[:, 1, :, :], src, spread(small_exp[:, 0, :].unsqueeze(2), M_HEADS, M_DIM + 1),
                                  ALU.mult).then_inc(left(plan, "inter"), 1)
                copied(dve, plan, "inter")
                src = by_head(full(dve, plan, "num1"))
                dve.tensor_tensor(total[:, 1, :, :], total[:, 1, :, :], src, ALU.add).then_inc(left(plan, "num1"), 1)
                copied(dve, plan, "num1")
                for t in range(NT):
                    n_q = total[:, t, :, M_DIM:].rearrange("p h o -> p (h o)")
                    d = den[:, t, 0, :]
                    step(dve.tensor_scalar(d, n_q, -1.0, None, ALU.mult))
                    step(dve.tensor_tensor(d, d, n_q, ALU.max))
                    step(dve.tensor_tensor(d, d, small_exp[:, 1 + t, :], ALU.max))
                    step(dve.reciprocal(den[:, t, 1, :], d))
                    step(dve.tensor_tensor(rows[:, t, 0:M_WIDTH].rearrange("p (h d) -> p h d", h=M_HEADS),
                                           total[:, t, :, 0:M_DIM], spread(den[:, t, 1, :].unsqueeze(2), M_HEADS, M_DIM),
                                           ALU.mult))
                dve.wait_ge(out_gate, l + 1)
                step(dve.tensor_tensor(rows[:, :, 0:M_WIDTH], rows[:, :, 0:M_WIDTH], proj_a[:, :, M_WIDTH:], ALU.mult))
                scale = float(QK_DIM) ** -0.5
                for h in range(A_HEADS):
                    src = full(dve, plan, f"sc{h}")
                    step(dve.scalar_tensor_tensor(prob[:, h % 2, 0:P], src[:, 0:P], scale, const["causal"][:, P:],
                                                  ALU.mult, ALU.add))
                    dve.scalar_tensor_tensor(prob[:, h % 2, P:], src[:, P:3 * P], scale, const["causal"],
                                             ALU.mult, ALU.add).then_inc(left(plan, f"sc{h}"), 1)
                    copied(dve, plan, f"sc{h}")
                    step(dve.tensor_reduce(soft[:, h, 0, 0:1], prob[:, h % 2, 0:P], AX.X, ALU.max))
                    step(dve.tensor_reduce(soft[:, h, 0, 1:2], prob[:, h % 2, P:], AX.X, ALU.max))
                    dve.tensor_scalar(soft[:, h, 0, :], soft[:, h, 0, :], -1.0, None, ALU.mult)\
                       .then_inc(logits_ready, 1)
                dve.wait_ge(prob_ready, NT * A_HEADS * (l + 1))
                step(dve.reciprocal(soft[:, :, 1, :], soft[:, :, 1, :]))
                for t in range(NT):
                    src = full(dve, plan, f"o{t}")
                    dve.tensor_tensor(rows[:, t, M_WIDTH:M_WIDTH + A_WIDTH].rearrange("p (h d) -> p h d", h=A_HEADS),
                                      src[:, 0:A_WIDTH].rearrange("p (h d) -> p h d", h=A_HEADS),
                                      spread(soft[:, :, 1, t:t + 1], A_HEADS, V_DIM), ALU.mult)\
                       .then_inc(left(plan, f"o{t}"), 1)
                    copied(dve, plan, f"o{t}")
                y_square = place(diag_at, D)
                for t in range(NT):
                    step(dve.tensor_tensor(y_square, rows[:, t, :], rows[:, t, :], ALU.mult))
                    step(dve.tensor_reduce(head_sums[:, 4 * t:4 * t + 4],
                                           y_square[:, 0:M_WIDTH].rearrange("p (h d) -> p h d", d=M_DIM), AX.X, ALU.add))
                    ins = dve.tensor_reduce(head_sums[:, 8 + 10 * t:18 + 10 * t],
                                            y_square[:, M_WIDTH:].rearrange("p (h d) -> p h d", d=V_DIM), AX.X, ALU.add)
                    if t == 0:
                        step(ins)
                ins.then_inc(head_sums_ready, 1)
                rstds(4)
                dve.wait_ge(loaded_gain, 16 * (3 * l + 2))
                for t in range(NT):
                    a = rows[:, t, 0:M_WIDTH].rearrange("p (h d) -> p h d", d=M_DIM)
                    b = rows[:, t, M_WIDTH:].rearrange("p (h d) -> p h d", d=V_DIM)
                    step(dve.tensor_tensor(a, a, spread(head_rstd[:, 4 * t:4 * t + 4].unsqueeze(2), M_HEADS, M_DIM),
                                           ALU.mult))
                    step(dve.tensor_tensor(b, b, spread(head_rstd[:, 8 + 10 * t:18 + 10 * t].unsqueeze(2), 10, V_DIM),
                                           ALU.mult))
                    dve.tensor_tensor(rows[:, t, :], rows[:, t, :], gain[:, :], ALU.mult).then_inc(y_rows, 1)
                for n in range(2):
                    for t in range(NT):
                        name = f"out{2 * t + n}"
                        src = full(dve, plan, name)
                        xs = x[:, t, n * HALF:(n + 1) * HALF]
                        dve.tensor_tensor(xs, xs, src[:, :], ALU.add).then_inc(left(plan, name), 1)
                        copied(dve, plan, name)
                dve.nop().then_inc(x_ready, 1)

            dve.wait_ge(loaded_consts, 16)
            dve.wait_ge(loaded_x, 16)
            for l in range(DEPTH):
                if mixer:
                    if l == 0:
                        rope_tables()
                    norm(PER * l, "p (k i) -> p k i", 3 * l + 1)
                    mix(l)
                norm(PER * (l + 1) - 1, "p (i k) -> p k i", 3 * (l + 1) if mixer else l + 1)
                dve.wait_ge(loaded_ffn, ROUTER_LOADS * (l + 1))
                route(l)
                g0 = l * (PAIRS + 1)
                step(dve.tensor_copy(slotrow[:, :], const["iota"]))
                build_hot(0, main, Chain(dve, main["vec"], HOT_LINKS * g0))
                with dve.Fori(0, PAIRS // 2) as j:
                    for par in range(2):
                        expert_pair(par, 2 * j + (l * PAIRS + par), 2 * j + (g0 + par), main)
                n_over = dve.value_load(overint[0:1, l, CELLS_OVER:CELLS_OVER + 1], min_val=0, max_val=2)
                with dve.If(n_over > 0):
                    S = extra[l]
                    dve.wait_ge(main["hot_ready"], g0 + PAIRS + 1)
                    dve.wait_ge(main["gathered"], 2 * (g0 + PAIRS + 1))
                    dve.tensor_scalar(slotrow[:, :], slotrow[:, :], -float(P), None, ALU.add)\
                       .then_inc(over_back, 1)
                    dve.wait_ge(over_back, 1)
                    build_hot(0, S, Chain(dve, S["vec"]))
                    with dve.Fori(0, n_over) as j:
                        for par in range(2):
                            expert_pair(par, 2 * j + par, 2 * j + par, S)
                with dve.Else():
                    dve.nop()
                dve.wait_ge(acc_done, l + 1)
                for t in range(NT):
                    for n in range(2):
                        xs = x[:, t, n * HALF:(n + 1) * HALF]
                        ins = dve.tensor_tensor(xs, xs, bank[2 * t + n][:, :], ALU.add)
                        if (t, n) != (NT - 1, 1):
                            step(ins)
                ins.then_inc(x_ready, 1)

            def last_block():
                plan = plan2
                rows = xf[:, :, :, :].rearrange("p t k i -> p t (k i)")

                def spread(ap, *shape):
                    return ap.broadcast_to([P, *shape])

                dve.wait_ge(loaded_second, 4 * 16)
                dve.memset(s_rel[0:S_HEADS, 32:33], NEG).then_inc(rel_ready, 1)
                src = full(dve, plan, "rel")
                dve.tensor_copy(s_relT[0:33, :], src[0:33, 0:S_HEADS]).then_inc(left(plan, "rel"), 1)
                src = full(dve, plan, "f")
                dve.tensor_copy(s_f[0:S_HEADS, :], src[0:S_HEADS, 0:384]).then_inc(left(plan, "f"), 1)
                copied(dve, plan, "f")
                dve.nop().then_inc(f_ready, 1)
                n = 2 * S_HEADS
                for t in range(NT):
                    copied(dve, plan, f"qa{t}", f"ka{t}")
                    step(dve.tensor_tensor(s_square, s_qk[:, t, :], s_qk[:, t, :], ALU.mult))
                    ins = dve.tensor_reduce(s_sums[:, n * t:n * (t + 1)],
                                            s_square.rearrange("p (h d) -> p h d", h=n), AX.X, ALU.add)
                    if t == 0:
                        step(ins)
                ins.then_inc(s_sums_ready, 1)
                dve.wait_ge(s_rstd_ready, 1)
                for t in range(NT):
                    heads = s_qk[:, t, :].rearrange("p (h d) -> p h d", h=n)
                    step(dve.tensor_tensor(heads, heads, spread(s_rstd[:, n * t:n * (t + 1)].unsqueeze(2), n, S_DIM),
                                           ALU.mult))
                    for a in range(2):
                        part = heads[:, a * S_HEADS:(a + 1) * S_HEADS, :]
                        step(dve.tensor_tensor(part, part, spread(s_gain[:, a, :].unsqueeze(1), S_HEADS, S_DIM),
                                               ALU.mult))
                dve.nop().then_inc(s_qk_ready, 1)

                def merge_tile(name):
                    if name[0] != "g":
                        return
                    t = int(name[-1])
                    at = "ab".index(name[1]) * D + int(name[2]) * HALF
                    src = full(dve, plan, name)
                    dve.tensor_tensor(s_gates[:, t, at:at + HALF], src[:, :],
                                      xf[:, :, :, :].rearrange("p t k i -> p (t k i)")[:, at:at + HALF], ALU.add)\
                       .then_inc(left(plan, name), 1)

                scale = float(S_DIM) ** -0.5
                dve.wait_ge(bias_loaded, 16)
                dve.wait_ge(loaded_merge_bias, 16)
                for h in range(S_HEADS + 1):
                    front, back = step_tiles(h)
                    if h < S_HEADS:
                        src = full(dve, plan, f"sc{h}")
                        if h >= 2:
                            full(dve, plan, f"pT{h - 2}")
                        p = s_prob[:, h % 2, :]
                        step(dve.scalar_tensor_tensor(p[:, 0:P], src[:, 0:P], scale, s_bias[:, h, P:],
                                                      ALU.mult, ALU.add))
                        dve.scalar_tensor_tensor(p[:, P:], src[:, P:3 * P], scale, s_bias[:, h, :],
                                                 ALU.mult, ALU.add).then_inc(left(plan, f"sc{h}"), 1)
                        copied(dve, plan, f"sc{h}")
                        step(dve.tensor_reduce(s_soft[:, h, 0, 0:1], p[:, 0:P], AX.X, ALU.max))
                        step(dve.tensor_reduce(s_soft[:, h, 0, 1:2], p[:, P:], AX.X, ALU.max))
                        dve.tensor_scalar(s_soft[:, h, 0, :], s_soft[:, h, 0, :], -1.0, None, ALU.mult)\
                           .then_inc(s_logits_ready, 1)
                        dve.wait_ge(s_ln_ready, h + 1)
                        log = s_log[:, h % 2, :]
                        src = full(dve, plan, f"z{h}")
                        dve.scalar_tensor_tensor(log, src[:, 0:3 * P], 0.0, log, ALU.max, ALU.add)\
                           .then_inc(left(plan, f"z{h}"), 1)
                        copied(dve, plan, f"z{h}")
                        step(dve.tensor_tensor(log[:, 0:SEQ], log[:, 0:SEQ], past_neg, ALU.mult))
                        dve.tensor_tensor(log[:, SEQ:], log[:, SEQ:], past_neg[:, 0:P], ALU.mult)\
                           .then_inc(s_log_ready, 1)
                    for name in front:
                        merge_tile(name)
                    if h:
                        g = h - 1
                        log = s_log[:, g % 2, :]
                        src = full(dve, plan, f"r{g}")
                        step(dve.tensor_tensor(log[:, 0:SEQ], src[:, 0:SEQ], past_add, ALU.add))
                        dve.tensor_tensor(log[:, SEQ:], src[:, SEQ:3 * P], past_add[:, 0:P], ALU.add)\
                           .then_inc(left(plan, f"r{g}"), 1)
                    for name in back:
                        merge_tile(name)
                    if h:
                        c = slice(g * S_DIM, (g + 1) * S_DIM)
                        src = full(dve, plan, f"ob{g}")
                        dve.tensor_copy(s_o[:, 1, :, c], src[:, 0:P].rearrange("p (t d) -> p t d", t=NT))\
                           .then_inc(left(plan, f"ob{g}"), 1)
                        step(dve.reciprocal(s_soft[:, g, 1, :], s_soft[:, g, 1, :]))
                        src = full(dve, plan, f"oa{g}")
                        dve.tensor_tensor(s_o[:, 0, :, c], src[:, 0:P].rearrange("p (t d) -> p t d", t=NT),
                                          spread(s_soft[:, g, 1, :].unsqueeze(2), NT, S_DIM), ALU.mult)\
                           .then_inc(left(plan, f"oa{g}"), 1)
                        copied(dve, plan, f"ob{g}", f"oa{g}")
                for name in TILES[4:]:
                    copied(dve, plan, name)
                dve.nop().then_inc(s_gates_in, 1)
                dve.wait_ge(s_silu_ready, 1)
                dve.tensor_tensor(s_o, s_o, s_z, ALU.mult).then_inc(s_o_ready, 1)
                dve.wait_ge(s_gate_ready, 1)
                for t in range(NT):
                    for n in range(2):
                        at = n * HALF
                        dst = rows[:, t, at:at + HALF]
                        src = full(dve, plan, f"ya{t}{n}")
                        dve.tensor_tensor(dst, s_gates[:, t, at:at + HALF], src[:, :], ALU.mult)\
                           .then_inc(left(plan, f"ya{t}{n}"), 1)
                        src = full(dve, plan, f"yb{t}{n}")
                        g = s_gates[:, t, D + at:D + at + HALF]
                        dve.tensor_tensor(g, g, src[:, :], ALU.mult).then_inc(left(plan, f"yb{t}{n}"), 1)
                        copied(dve, plan, f"ya{t}{n}", f"yb{t}{n}")
                        ins = dve.tensor_tensor(dst, dst, g, ALU.add)
                        if n == 0:
                            step(ins)
                    ins.then_inc(s_rows, 1)
                for n in range(2):
                    for t in range(NT):
                        name = f"out{2 * t + n}"
                        src = full(dve, plan, name)
                        xs = x[:, t, n * HALF:(n + 1) * HALF]
                        dve.tensor_tensor(xs, xs, src[:, :], ALU.add).then_inc(left(plan, name), 1)
                        copied(dve, plan, name)
                dve.nop().then_inc(x_ready, 1)

            if second:
                norm(PER * DEPTH, "p (k i) -> p k i", 3 * DEPTH + 1)
                last_block()


_INS = ["x", "positions", "attn_norm", "w_in", "m_conv_w", "m_conv_b", "m_gate_bias", "a_q_norm", "a_kv_norm",
        "a_w_uq", "a_w_ukv", "a_q_head_norm", "a_k_head_norm", "c_v_norm", "c_w_s", "c_b_s", "mix_out_norm",
        "w_out", "ffn_norm", "w_group", "b_group", "w_expert", "b_expert", "w1", "w3", "w2",
        "norm_w_2", "w_in_2", "merge_gate_b_2", "q_norm_w_2", "k_norm_w_2", "rel_bias_2", "w_up_moba_2",
        "w_up_sb_2", "w_out_2"]
_OUTS = [((1, SEQ, D), "float32")]


def kernel(**inputs):
    import concourse.bacc as _bacc
    from concourse.bass_utils import run_bass_kernel_spmd as _run

    nc = _bacc.Bacc("TRN2", target_bir_lowering=False, num_devices=1)
    arrays = {name: np.ascontiguousarray(inputs[name]) for name in _INS}
    arrays["consts"], arrays["late_consts"] = constant_table()
    io = {name: nc.dram_tensor(f"in_{name}", a.shape, mybir.dt.from_np(a.dtype), kind="ExternalInput").ap()
          for name, a in arrays.items()}
    shape, dtype = _OUTS[0]
    out = nc.dram_tensor("out_0", shape, mybir.dt.from_np(np.dtype(dtype)), kind="ExternalOutput").ap()
    program(nc, io, out)
    r = _run(nc, [{f"in_{name}": a for name, a in arrays.items()}], core_ids=[0])
    return r.results[0]["out_0"]
```

```python
from contextlib import ExitStack

import concourse.bass as bass
import numpy as np
from concourse import mybir

F32 = mybir.dt.float32
BF16 = mybir.dt.bfloat16
I32 = mybir.dt.int32
ALU = mybir.AluOpType
ACT = mybir.ActivationFunctionType
AX = mybir.AxisListType

P = 128
SEQ = 256
NT = SEQ // P
D = 1024
KD = D // P
DEPTH = 2
EPS = 1e-6
NEG = -1e30

N_GROUPS, PER_GROUP = 4, 8
NE = N_GROUPS * PER_GROUP
DE = 256
CELL = 64
PAIRS = NE // 2
ARENA = 19200
CELLS_OVER = 8

M_HEADS, M_DIM = 4, 96
M_WIDTH = M_HEADS * M_DIM
A_HEADS, NOPE, ROPE, V_DIM = 6, 64, 32, 64
QK_DIM = NOPE + ROPE
A_WIDTH = A_HEADS * V_DIM
Q_RANK, KV_RANK = 256, 128
C_GROUPS, C_DIM = 4, 64
C_WIDTH = C_GROUPS * C_DIM
UNIT_COLS = [(0, 384), (384, 768), (768, 1280), (1280, 1792), (1792, 2304), (2304, 2472)]
A_COLS = 2 * M_WIDTH
B_COLS = 2472 - 4 * M_WIDTH
GATE_AT, CQ_AT, CKV_AT, KR_AT, CU_AT, CV_AT = 0, 8, 264, 392, 424, 680

SLOT = 4096
RING = 6
HALF = 512

CONST_WIDTHS = [("ident", P), ("upto", P), ("before", P), ("fromon", P), ("ones", P), ("iota", P),
                ("causal", 2 * P), ("causal_t", P), ("inv_freq", 16), ("rev", NE), ("cell64", NE),
                ("zeros", 2 * P), ("neg_half", 1)]
LATE_WIDTHS = [("past_neg", 2 * P), ("past_add", 2 * P), ("buckets", 384)]


S_HEADS, S_DIM = 8, 64
S_WIDTH = S_HEADS * S_DIM
COLUMNS = ("qa", "ka", "va", "za", "qb", "kb", "vb", "zb", "ga0", "ga1", "gb0", "gb1")
SECOND_UNITS = ("qa", "ka", "qb", "kb", "va", "vb", "za", "zb", "ga0", "ga1", "gb0", "gb1", "upa", "upb",
                "out0", "out1")
TILES = [f"{u}{t}" for u in ("za", "zb", "ga0", "ga1", "gb0", "gb1") for t in range(2)]


def step_tiles(h):
    before = {0: [0], 1: [1], 2: [3], 3: [5], 4: [7], 5: [8], 6: [9], 7: [10], 8: [11]}[h]
    after = {1: [2], 2: [4], 3: [6]}.get(h, [])
    return [TILES[i] for i in before], [TILES[i] for i in after]


def second_banks():
    uses = [("rel", 4), ("f", 5)]
    uses += [(n, b) for names in (("qa0", "qa1", "ka0", "ka1"), ("qbA", "qbB", "kbA", "kbB"),
                                  ("va0", "va1", "vb0", "vb1")) for b, n in enumerate(names)]
    uses += [("qT0", 4), ("qT1", 5), ("kT0", 6), ("kT1", 7)]
    tile = 0
    for h in range(S_HEADS + 1):
        if h < S_HEADS:
            uses += [(f"z{h}", 4 + h % 2), (f"sc{h}", 6 + h % 2)]
        front, behind = step_tiles(h)
        for n in front:
            uses.append((n, tile % 4))
            tile += 1
        if h:
            uses += [(f"r{h - 1}", 4 + (h - 1) % 2), (f"pT{h - 1}", 6 + (h - 1) % 2)]
        for n in behind:
            uses.append((n, tile % 4))
            tile += 1
        if h:
            uses += [(f"ob{h - 1}", 4 + (h - 1) % 2), (f"oa{h - 1}", 6 + (h - 1) % 2)]
    uses += [(f"oT{i}", 4 + i) for i in range(4)]
    uses += [(f"y{a}{t}{n}", 2 * (n % 2) + (a == "b")) for t in range(2) for n in range(2) for a in "ab"]
    uses += [(f"yT{u}", 4 + u) for u in range(4)] + [(f"out{b}", b) for b in range(4)]
    return uses


def constant_table():
    p = np.arange(P)[:, None]
    c = np.arange(P)[None, :]
    c2 = np.arange(2 * P)[None, :]
    dist = 255 - np.arange(384)
    n = np.maximum(dist, 1).astype(np.float64)
    bucket = np.where(dist < 16, dist, np.minimum(16 + (np.log(n / 16) / np.log(8.0) * 16).astype(np.int64), 31))
    bucket = np.where(dist < 0, 32, bucket)
    freq = 1.0 / (np.float32(10000.0) ** (np.arange(0, 32, 2, dtype=np.float32) / np.float32(32)))
    full = np.ones((P, 1), np.float32)
    parts = {
        "ident": p == c, "upto": p <= c, "before": p < c, "fromon": p >= c, "ones": full * np.ones((1, P)),
        "iota": full * c, "causal": np.where(p + P - c2 >= 0, 0.0, NEG), "causal_t": np.where(p <= c, 0.0, NEG),
        "past_neg": -(p < c2).astype(np.float32), "past_add": np.where(p < c2, 0.0, NEG),
        "inv_freq": full * freq[None, :], "rev": full * (NE - np.arange(NE))[None, :],
        "cell64": full * (CELL * np.arange(NE))[None, :], "zeros": full * np.zeros((1, 2 * P)),
        "buckets": p == bucket[None, :], "neg_half": -0.5 * full,
    }
    return [np.concatenate([np.asarray(parts[k], np.float32) for k, _ in widths], axis=1)
            for widths in (CONST_WIDTHS, LATE_WIDTHS)]


def bank_plan(uses, base):
    plan, total = {}, list(base)
    for name, b in uses:
        total[b] += 1
        plan[name] = (b, total[b])
    return plan, total


MIXER_BANKS = ([("conv_rows", 6), ("gate_w", 7), ("u3t0", 0), ("u3t1", 1), ("u4t0", 2), ("u4t1", 3), ("u5t0", 0),
                ("u5t1", 1), ("q01", 2), ("cqT", 4), ("ckvT", 5), ("cum", 6), ("q23", 3), ("rrow0", 7), ("rrow1", 6),
                ("q0a", 4), ("q0b", 5), ("k01", 0), ("q1a", 4), ("q1b", 5), ("mrow0", 7), ("kv0a", 4), ("kv0b", 5),
                ("k23", 1), ("mrow1", 6), ("kv1a", 4), ("kv1b", 5), ("gated", 7), ("u2t0", 2), ("u2t1", 3),
                ("st0", 4), ("st1", 5), ("ktok", 6), ("state", 7), ("num0", 4), ("num1", 5), ("inter", 6)]
               + [(f"qkT{i}", i % 4) for i in range(6)] + [("o0", 4), ("o1", 5)]
               + [x for h in range(6) for x in ((f"sc{h}", 2 + h % 2), (f"pT{h}", h % 2))]
               + [(f"yT{u}", 6 + u % 2) for u in range(4)] + [(f"out{b}", b) for b in range(4)])


class Chain:

    def __init__(self, eng, sem, base=0):
        self.eng, self.sem, self.n = eng, sem, base

    def __call__(self, ins):
        self.n = self.n + 1
        ins.then_inc(self.sem, 1)
        self.eng.wait_ge(self.sem, self.n)


def program(nc, io, out, mixer=True, second=True):
    with ExitStack() as ctx:
        def sb(name, shape, dt=F32):
            return ctx.enter_context(nc.sbuf_tensor(name, shape, dt))

        def sem(name):
            return ctx.enter_context(nc.semaphore(name))

        bank = [ctx.enter_context(nc.psum_tensor(f"bank{b}", [P, HALF], F32)) for b in range(8)]
        ring = [sb(f"ring{s}", [P, SLOT]) for s in range(RING)]
        x = sb("x", [P, NT, D])
        consts = sb("consts", [P, sum(w for _, w in CONST_WIDTHS)])
        const = {}
        at = 0
        for name, w in CONST_WIDTHS:
            const[name] = consts[:, at:at + w]
            at += w
        ident, ones = const["ident"], const["ones"]

        late = ctx.enter_context(nc.sbuf_tensor("arena", [P, ARENA], F32))

        def place(at, *shape):
            n = 1
            for w in shape:
                n *= w
            assert at + n <= ARENA, (at, shape)
            v = late[:, at:at + n]
            if len(shape) == 2:
                return v.rearrange("p (a b) -> p a b", b=shape[1])
            if len(shape) == 3:
                return v.rearrange("p (a b c) -> p a b c", b=shape[1], c=shape[2])
            return v

        gain = sb("gain", [P, D])
        w_router = sb("w_router", [P, KD, N_GROUPS + NE])
        router_bias = sb("router_bias", [P, N_GROUPS + NE])
        xf = sb("xf", [P, NT, KD, P])
        xfT = sb("xfT", [P, KD, SEQ])
        stats = sb("stats", [P, 16])
        positions = sb("positions", [P, NT], I32)
        overint = sb("overint", [1, DEPTH, CELLS_OVER + 1], I32)
        cos_sin = sb("cos_sin", [P, 2, NT, ROPE // 2])
        square = place(0, D)

        at = [D]

        def nxt(*shape):
            n = 1
            for w in shape:
                n *= w
            at[0] += n
            return place(at[0] - n, *shape)

        logits = nxt(NT, N_GROUPS + NE)
        groupwork = nxt(NT, 3, N_GROUPS)
        scores = nxt(NT, NE)
        work = nxt(NT, NE)
        pick = nxt(NT, 2, NE)
        rowmax = nxt(NT)
        expin = nxt(NT, 8)
        expout = nxt(NT, 8)
        gates = nxt(2, NT)
        slot_of = nxt(2, NT)
        position = nxt(NT + 1, NE)
        over = nxt(3, NE)
        overlist = nxt(CELLS_OVER, NE)
        oversum = nxt(CELLS_OVER + 1)
        slots_gathered = nxt(2 * P)
        slots_weighted = nxt(P)
        onehot = nxt(NT * P).bitcast(BF16).rearrange("p (t s) -> p t s", t=NT)
        onehot_w = nxt(2, NT, P)
        hotwork = nxt(2 * P)
        xg = nxt(KD, 2 * P)
        silu = nxt(2, DE)
        hidden = nxt(2, DE)
        turned = nxt(2, 4, P)
        y = nxt(2, 2, HALF)
        biased = nxt(NT, NE)
        xf_parts = [nxt(NT * D // 2).bitcast(BF16).rearrange("p (t k i) -> p t k i", t=NT, k=KD) for _ in range(3)]
        xf_rest = nxt(NT, KD, P)

        conv_raw = place(0, 2 * M_HEADS, 3 + SEQ)
        prob = place(0, 2, 3 * P)
        probT = place(6 * P, 2, 3 * P)
        at[0] = 2 * M_HEADS * (3 + SEQ)
        turned_at = at[0]
        conv_out = nxt(2 * M_HEADS, SEQ)
        decay = nxt(NT, M_HEADS, P)
        qkT = place(turned_at, 2 * A_HEADS, SEQ)
        gate_raw = place(turned_at + 2 * M_HEADS * SEQ, C_GROUPS, P)
        proj_a = nxt(NT, A_COLS)
        b_at = at[0]
        proj_b = nxt(NT, B_COLS)
        kv = place(b_at, NT, A_HEADS, NOPE + V_DIM)
        qk = nxt(NT, 2 * A_HEADS, QK_DIM)
        diag_at = at[0]
        qk_square = nxt(2 * A_HEADS, QK_DIM)
        diag = place(diag_at, M_HEADS, P)
        masked = place(diag_at + M_HEADS * P, M_HEADS, P)
        conv_rows = place(diag_at, 2 * M_WIDTH)
        cb_rows = place(diag_at + 2 * M_WIDTH, P)
        gelu = nxt(NT, 2 * C_WIDTH)
        small_at = at[0]
        k_weighted = nxt(M_HEADS, M_DIM)
        state = nxt(M_HEADS, M_DIM + 1)
        total = nxt(NT, M_HEADS, M_DIM + 1)
        latent = place(small_at, NT, Q_RANK + KV_RANK)
        latentT = nxt(3, SEQ)
        gate_wT = nxt(C_GROUPS, P)
        w_uq = nxt(2, A_HEADS * QK_DIM)
        w_ukv = nxt(A_HEADS * (NOPE + V_DIM))
        latent_gain = nxt(Q_RANK + KV_RANK)
        cv_gain = nxt(C_WIDTH)
        qk_gain = nxt(2, QK_DIM)
        conv_w = nxt(2 * M_HEADS, 5)
        cb = nxt(C_GROUPS)
        gate_bias = nxt(2 * M_HEADS)
        gate_in = nxt(NT, 3, 2 * M_HEADS)
        log_f = nxt(NT, M_HEADS)
        cum = nxt(NT, 2, M_HEADS)
        rel = nxt(NT, M_HEADS)
        run_max = nxt(NT, M_HEADS)
        carry = nxt(M_HEADS)
        small_exp = nxt(3, M_HEADS)
        den = nxt(NT, 2, M_HEADS)
        head_sums = nxt(48)
        head_rstd = nxt(48)
        soft = nxt(A_HEADS, 2, NT)
        second_end = at[0]
        at[0] = 0
        s_v = nxt(2, NT * S_WIDTH).rearrange("p a (t n) -> p a t n", t=NT)
        s_z = nxt(2, NT * S_WIDTH).rearrange("p a (t n) -> p a t n", t=NT)
        s_qk = nxt(NT, 2 * S_WIDTH)
        s_o = place(at[0] - 2 * NT * S_WIDTH, 2, NT * S_WIDTH).rearrange("p a (t n) -> p a t n", t=NT)
        s_qkbT = nxt(2, S_HEADS // 2 * SEQ).rearrange("p a (i s) -> p a i s", s=SEQ)
        s_qkaT = nxt(2, S_HEADS // 2 * SEQ).rearrange("p a (i s) -> p a i s", s=SEQ)
        s_oT = s_qkaT
        gl_at = at[0]
        s_gates = nxt(NT, 2 * D)
        s_square = place(gl_at, 2 * S_WIDTH)
        s_rel = place(gl_at + 2 * S_WIDTH, 33)
        s_relT = place(gl_at + 2 * S_WIDTH + 64, S_HEADS)
        s_f = place(gl_at + 2 * S_WIDTH + 128, 384)
        s_bias = nxt(S_HEADS, SEQ)
        late_at = at[0]
        late_words = nxt(sum(w for _, w in LATE_WIDTHS))
        past_neg, past_add = place(late_at, SEQ), place(late_at + SEQ, SEQ)
        buckets = place(late_at + 2 * SEQ, 384)
        s_log = nxt(2, 3 * P)
        s_probT = nxt(2, 3 * P)
        s_prob = gain[:, 0:6 * P].rearrange("p (a n) -> p a n", a=2)
        s_gain = nxt(2, S_DIM)
        s_sums = nxt(NT * 2 * S_HEADS)
        s_rstd = nxt(NT * 2 * S_HEADS)
        s_soft = nxt(S_HEADS, 2, NT)
        at[0] = second_end

        rope_work = place(diag_at, 4, 2 * A_HEADS, ROPE // 2)

        loaded_x = [sem(f"loaded_x{t}") for t in range(NT)]
        loaded_consts, loaded_ffn = sem("loaded_consts"), sem("loaded_ffn")
        ROUTER_LOADS = 4 * 16
        MIXER_LOADS = 12 * 16
        loaded_mixer = sem("loaded_mixer")
        loaded_gain = sem("loaded_gain")
        loaded_positions = sem("loaded_positions")
        filled = [sem(f"filled{b}") for b in range(8)]
        drained = [sem(f"drained{b}") for b in range(8)]
        angles = sem("angles")
        rope_ready = sem("rope_ready")
        latent_sums = sem("latent_sums")
        head_sums_ready = sem("head_sums_ready")
        head_rstd_ready = sem("head_rstd_ready")
        gate_abs = sem("gate_abs")
        gate_exp = sem("gate_exp")
        gate_ln = sem("gate_ln")
        log_f_ready = sem("log_f_ready")
        latent_ready = sem("latent_ready")
        gelu_ready = sem("gelu_ready")
        gate_v_ready = sem("gate_v_ready")
        diag_ready = sem("diag_ready")
        decay_wanted = sem("decay_wanted")
        decay_done = sem("decay_done")
        conv_ready = sem("conv_ready")
        conv_act = sem("conv_act")
        out_gate = sem("out_gate")
        pt_ready = sem("pt_ready")
        kw_ready = sem("kw_ready")
        qk_ready = sem("qk_ready")
        logits_ready = sem("logits_ready")
        prob_ready = sem("prob_ready")
        y_rows = sem("y_rows")
        loaded_second = sem("loaded_second")
        loaded_merge_bias = sem("loaded_merge_bias")
        rel_ready = sem("rel_ready")
        f_ready = sem("f_ready")
        f_stored = sem("f_stored")
        bias_loaded = sem("bias_loaded")
        s_sums_ready = sem("s_sums_ready")
        s_rstd_ready = sem("s_rstd_ready")
        s_qk_ready = sem("s_qk_ready")
        s_ln_ready = sem("s_ln_ready")
        s_act = sem("s_act")
        s_log_ready = sem("s_log_ready")
        s_logits_ready = sem("s_logits_ready")
        s_prob_ready = sem("s_prob_ready")
        s_weight_ready = sem("s_weight_ready")
        s_silu_ready = sem("s_silu_ready")
        s_gate_ready = sem("s_gate_ready")
        s_o_ready = sem("s_o_ready")
        s_gates_in = sem("s_gates_in")
        s_rows = sem("s_rows")
        landed = [sem(f"landed{s}") for s in range(RING)]
        freed = [sem(f"freed{s}") for s in range(RING)]
        PER = 2 if mixer else 1
        plans, totals = [], [0] * 8
        for _ in range(DEPTH):
            plan, totals = bank_plan(MIXER_BANKS, totals)
            plans.append(plan)
        plan2, _ = bank_plan(second_banks(), totals)
        unit2, used2 = {}, [0] * RING
        for i, name in enumerate(SECOND_UNITS):
            used2[i % RING] += 1
            unit2[name] = (i % RING, used2[i % RING])

        def full(eng, plan, name):
            b, n = plan[name]
            eng.wait_ge(filled[b], n)
            return bank[b]

        def copied(eng, plan, *names):
            for name in names:
                b, n = plan[name]
                eng.wait_ge(drained[b], n)

        def left(plan, name):
            return drained[plan[name][0]]

        def unit_view(s, w):
            return ring[s][:, 0:KD * w].rearrange("p (k n) -> p k n", n=w)

        x_tile_ready = sem("x_tile_ready")
        x_ready = sem("x_ready")
        vec_step = sem("vec_step")
        act_step = sem("act_step")
        squares = sem("squares")
        pool_step = sem("pool_step")
        rstd_ready = sem("rstd_ready")
        xf_ready = sem("xf_ready")
        xf_turned = sem("xf_turned")
        xfT_ready = sem("xfT_ready")
        logits_done = sem("logits_done")
        exp_wanted = sem("exp_wanted")
        exp_done = sem("exp_done")
        picked = sem("picked")
        rest_ready = sem("rest_ready")
        parts_ready = sem("parts_ready")
        counted = sem("counted")
        over_ready = sem("over_ready")
        acc_done = sem("acc_done")
        stored = sem("stored")

        PAIR_SEMS = ("hot_ready", "turn_done", "gathered", "xg_ready", "up_done", "silu_ready",
                     "hidden_ready", "turned_ready", "down_done", "y_ready", "vec")

        def pair_sems(tag):
            return {n: sem(f"{tag}_{n}") for n in PAIR_SEMS}

        main = pair_sems("main")
        extra = [pair_sems(f"over{l}") for l in range(DEPTH)]
        extra_landed = [[sem(f"over{l}_landed{s}") for s in range(RING)] for l in range(DEPTH)]
        extra_freed = [[sem(f"over{l}_freed{s}") for s in range(RING)] for l in range(DEPTH)]

        UP_LO, UP_HI, DOWN = (2, 5), (3, 0), (4, 1)
        START_BANKS = (4, 7, 6, 4)
        mixer_uses = [2 if s < 2 else 1 for s in range(RING)] if mixer else [0] * RING
        layer_uses = [b + PAIRS // 2 for b in mixer_uses]
        pair_bytes = [32 if s in DOWN else 64 for s in range(RING)]
        layer_lands = [16 * b + PAIRS // 2 * n for b, n in zip(mixer_uses, pair_bytes)]

        def up_view(s):
            return ring[s][:, :].rearrange("p (e w k f) -> p e w k f", e=2, w=2, k=KD // 2)

        def down_view(s):
            return ring[s][:, :].rearrange("p (e c n) -> p e c n", e=2, c=2)

        if second:
            skew = nc.dram_tensor("skew", [P, S_HEADS, 384], F32, kind="Internal").ap()

        block = ctx.enter_context(nc.Block())

        @block.sync
        def _(sp):
            for t in range(NT):
                sp.dma_start(x[:, t, :], io["x"][0, t * P:(t + 1) * P, :]).then_inc(loaded_x[t], 16)

            def load_pair(l, par, experts, lands, frees, used):
                for h, s in ((0, UP_LO[par]), (1, UP_HI[par])):
                    sp.wait_ge(frees[s], used(s))
                    for w, name in ((0, "w1"), (1, "w3")):
                        for i, e in enumerate(experts):
                            src = io[name][l, bass.ds(e, 1)].rearrange(
                                "o (p k) f -> p (o k f)", p=P)[:, h * 1024:(h + 1) * 1024]
                            sp.dma_start(up_view(s)[:, i, w].rearrange("p k f -> p (k f)"), src)\
                              .then_inc(lands[s], 16)
                s = DOWN[par]
                sp.wait_ge(frees[s], used(s))
                for i, e in enumerate(experts):
                    src = io["w2"][l, bass.ds(e, 1)].rearrange("o (p c) n -> p (o c n)", p=P)
                    sp.dma_start(down_view(s)[:, i].rearrange("p c n -> p (c n)"), src).then_inc(lands[s], 16)

            def mixer_loads(l):
                def small(dst, src):
                    sp.dma_start(dst, src).then_inc(loaded_mixer, 16)

                small(gate_raw, io["c_w_s"][l].rearrange("g t s -> t g s"))
                small(conv_rows[0:4, :], io["m_conv_w"][l])
                small(conv_rows[4:5, :], io["m_conv_b"][l:l + 1, :])
                small(cb_rows[0:4, :], io["c_b_s"][l])
                small(gate_bias, io["m_gate_bias"][l:l + 1, :].broadcast_to([P, 2 * M_HEADS]))
                small(latent_gain[:, 0:Q_RANK], io["a_q_norm"][l:l + 1, :].broadcast_to([P, Q_RANK]))
                small(latent_gain[:, Q_RANK:], io["a_kv_norm"][l:l + 1, :].broadcast_to([P, KV_RANK]))
                small(cv_gain, io["c_v_norm"][l:l + 1, :].broadcast_to([P, C_WIDTH]))
                small(qk_gain[:, 0, :], io["a_q_head_norm"][l:l + 1, :].broadcast_to([P, QK_DIM]))
                small(qk_gain[:, 1, :], io["a_k_head_norm"][l:l + 1, :].broadcast_to([P, QK_DIM]))
                small(w_uq, io["a_w_uq"][l].rearrange("(k p) n -> p k n", p=P))
                small(w_ukv, io["a_w_ukv"][l])

            for l in range(DEPTH):
                if mixer:
                    for s in (3, 4, 5, 0, 1, 2):
                        if l == 0 and s == 4:
                            mixer_loads(l)
                        c0, c1 = UNIT_COLS[s]
                        sp.wait_ge(freed[s], l * layer_uses[s] + 1)
                        sp.dma_start(unit_view(s, c1 - c0),
                                     io["w_in"][l, :, c0:c1].rearrange("(k p) n -> p k n", p=P))\
                          .then_inc(landed[s], 16)
                    if l:
                        sp.wait_ge(x_ready, PER * l)
                        mixer_loads(l)
                    for s in range(2):
                        sp.wait_ge(freed[s], l * layer_uses[s] + 2)
                        sp.dma_start(unit_view(s, HALF), io["w_out"][l, :, s * HALF:(s + 1) * HALF].rearrange(
                            "(k p) n -> p k n", p=P)).then_inc(landed[s], 16)
                with sp.Fori(0, PAIRS // 2) as j:
                    for par in range(2):
                        load_pair(l, par, [4 * j + 2 * par, 4 * j + (2 * par + 1)], landed, freed,
                                  lambda s: j + (l * layer_uses[s] + mixer_uses[s] + 1))
                sp.wait_ge(over_ready, l + 1)
                n_over = sp.value_load(overint[0:1, l, CELLS_OVER:CELLS_OVER + 1], min_val=0, max_val=2)
                with sp.If(n_over > 0):
                    for s in range(RING):
                        sp.wait_ge(freed[s], (l + 1) * layer_uses[s] + 1)
                    with sp.Fori(0, n_over) as j:
                        for par in range(2):
                            experts = [sp.value_load(overint[0:1, l, bass.ds(4 * j + (2 * par + i), 1)],
                                                     min_val=0, max_val=NE - 1) for i in range(2)]
                            load_pair(l, par, experts, extra_landed[l], extra_freed[l], lambda s: j + 1)
                    sp.wait_ge(acc_done, l + 1)
                with sp.Else():
                    sp.nop()
            if second:
                def unit(name, src):
                    s, n = unit2[name]
                    sp.wait_ge(freed[s], DEPTH * layer_uses[s] + n)
                    k = src.shape[0] // P
                    sp.dma_start(ring[s][:, :].rearrange("p (k n) -> p k n", k=k),
                                 src.rearrange("(k p) n -> p k n", p=P)).then_inc(landed[s], 16)

                def columns(name):
                    c = COLUMNS.index(name) * HALF
                    unit(name, io["w_in_2"][0, :, c:c + HALF])

                for name in SECOND_UNITS[0:RING]:
                    columns(name)
                sp.wait_ge(x_ready, PER * DEPTH)
                for dst, src in ((late_words, io["late_consts"]), (s_rel[0:S_HEADS, 0:32], io["rel_bias_2"]),
                                 (s_gain[:, 0, :], io["q_norm_w_2"].broadcast_to([P, S_DIM])),
                                 (s_gain[:, 1, :], io["k_norm_w_2"].broadcast_to([P, S_DIM]))):
                    sp.dma_start(dst, src).then_inc(loaded_second, 16)
                def expand_bias():
                    sp.wait_ge(f_ready, 1)
                    sp.dma_start(skew.rearrange("p h j -> h p j"),
                                 s_f[0:S_HEADS, :].unsqueeze(1).broadcast_to([S_HEADS, P, 384])).then_inc(f_stored, 16)
                    sp.wait_ge(f_stored, 16)
                    pitch = S_HEADS * 384 - 1
                    sp.dma_start(s_bias, bass.AP(skew.tensor, P - 1, [[pitch, P], [384, S_HEADS], [1, SEQ]]))\
                      .then_inc(bias_loaded, 16)
                sp.wait_ge(xfT_ready, 4 * (PER * DEPTH + 1))
                sp.dma_start(xf[:, :, :, :].rearrange("p t k i -> p (t k i)"),
                             io["merge_gate_b_2"].broadcast_to([P, 2 * D])).then_inc(loaded_merge_bias, 16)
                for name in SECOND_UNITS[RING:]:
                    if name == SECOND_UNITS[RING + 2]:
                        expand_bias()
                    if name in COLUMNS:
                        columns(name)
                    elif name in ("upa", "upb"):
                        unit(name, io["w_up_moba_2" if name == "upa" else "w_up_sb_2"][0])
                    else:
                        n = int(name[-1])
                        unit(name, io["w_out_2"][0, :, n * HALF:(n + 1) * HALF])
            last = PER * DEPTH + (1 if second else 0)
            for t in range(NT):
                sp.wait_ge(x_tile_ready if t == 0 else x_ready, last)
                sp.dma_start(out[0, t * P:(t + 1) * P, :], x[:, t, :]).then_inc(stored, 16)
            sp.wait_ge(stored, 16 * NT)

        @block.gpsimd
        def _(pool):
            step = Chain(pool, pool_step)

            def power(dst, signal):
                pool.tensor_tensor(dst, dst, const["neg_half"].broadcast_to(list(dst.shape)), ALU.pow)\
                    .then_inc(signal, 1)

            def rstd_of(dst, sums, n, signal):
                step(pool.tensor_scalar(dst, sums, 1.0 / n, EPS, ALU.mult, ALU.add))
                power(dst, signal)

            pool.dma_start(consts[:, :], io["consts"]).then_inc(loaded_consts, 16)
            pool.dma_start(positions[:, :], io["positions"][0].rearrange("(t p) -> p t", p=P),
                           allow_slow_non_contiguous=True)\
                .then_inc(loaded_positions, 16)

            def norm(m):
                for t in range(NT):
                    pool.wait_ge(squares, NT * m + t + 1)
                    rstd_of(stats[:, 8 + t:9 + t], stats[:, t:t + 1], D, rstd_ready)

            def load_gain(name, l):
                pool.dma_start(gain[:, :], io[name][l:l + 1, :].broadcast_to([P, D])).then_inc(loaded_gain, 16)

            for l in range(DEPTH):
                m = PER * l
                if mixer:
                    if l:
                        pool.wait_ge(xf_ready, NT * m)
                    load_gain("attn_norm", l)
                    if l == 0:
                        pool.wait_ge(loaded_consts, 16)
                    norm(m)
                    pool.wait_ge(latent_sums, 4 * l + 4)
                    step(pool.tensor_scalar(head_rstd[:, 0:2], head_sums[:, 0:2], 1.0 / Q_RANK, EPS, ALU.mult, ALU.add))
                    step(pool.tensor_scalar(head_rstd[:, 2:4], head_sums[:, 2:4], 1.0 / KV_RANK, EPS, ALU.mult, ALU.add))
                    power(head_rstd[:, 0:4], head_rstd_ready)
                    pool.wait_ge(xf_ready, NT * (m + 1))
                    load_gain("mix_out_norm", l)
                    pool.wait_ge(head_sums_ready, 5 * l + 1)
                    rstd_of(head_rstd[:, 4:12], head_sums[:, 4:12], C_DIM, head_rstd_ready)
                    pool.wait_ge(head_sums_ready, 5 * l + 2)
                    rstd_of(head_rstd[:, 12:36], head_sums[:, 12:36], QK_DIM, head_rstd_ready)
                    pool.wait_ge(head_sums_ready, 5 * l + 3)
                    step(pool.tensor_scalar(head_rstd[:, 0:8], head_sums[:, 0:8], 1.0 / M_DIM, EPS, ALU.mult, ALU.add))
                    step(pool.tensor_scalar(head_rstd[:, 8:16], head_sums[:, 8:16], 1.0 / C_DIM, EPS, ALU.mult, ALU.add))
                    power(head_rstd[:, 0:16], head_rstd_ready)
                    for t in range(NT):
                        pool.wait_ge(head_sums_ready, 5 * l + 4 + t)
                        rstd_of(head_rstd[:, 16 + 6 * t:22 + 6 * t], head_sums[:, 16 + 6 * t:22 + 6 * t], V_DIM,
                                head_rstd_ready)
                if l:
                    pool.wait_ge(over_ready, l)
                pool.dma_start(w_router[:, :, 0:N_GROUPS], io["w_group"][l].rearrange("(p k) g -> p k g", p=P))\
                    .then_inc(loaded_ffn, 16)
                pool.dma_start(w_router[:, :, N_GROUPS:], io["w_expert"][l].rearrange("(p k) g -> p k g", p=P))\
                    .then_inc(loaded_ffn, 16)
                pool.dma_start(router_bias[:, 0:N_GROUPS], io["b_group"][l:l + 1, :].broadcast_to([P, N_GROUPS]))\
                    .then_inc(loaded_ffn, 16)
                pool.dma_start(router_bias[:, N_GROUPS:], io["b_expert"][l:l + 1, :].broadcast_to([P, NE]))\
                    .then_inc(loaded_ffn, 16)
                if mixer:
                    pool.wait_ge(y_rows, NT * (l + 1))
                elif l:
                    pool.wait_ge(xf_ready, NT * l)
                else:
                    pool.wait_ge(loaded_consts, 16)
                load_gain("ffn_norm", l)
                norm(m + PER - 1)
                pool.memset(y[:, 1, :, :], 0.0)
                pool.memset(turned[:, 1, 2:4, :], 0.0)
                pool.wait_ge(rest_ready, l + 1)
                step(pool.tensor_copy(xf_parts[1], xf_rest))
                pool.tensor_tensor(xf_parts[2], xf_rest, xf_parts[1], ALU.subtract).then_inc(parts_ready, 1)

            if second:
                pool.wait_ge(xf_ready, NT * PER * DEPTH)
                load_gain("norm_w_2", 0)
                norm(PER * DEPTH)
                pool.wait_ge(s_sums_ready, 1)
                rstd_of(s_rstd, s_sums, S_DIM, s_rstd_ready)

        @block.tensor
        def _(pe):
            def gather(quarter, it, S, dst, release=None):
                pe.wait_ge(S["hot_ready"], it + 1)
                for k in range(2):
                    for t in range(NT):
                        for i in range(3):
                            ins = pe.matmul(dst[:, 2 * k * P:2 * (k + 1) * P], xf_parts[i][:, t, 2 * quarter + k, :],
                                            onehot[:, t, :], start=(t == 0 and i == 0), stop=(t == NT - 1 and i == 2))
                            if release is not None and k == 0 and t == 0 and i == 0:
                                ins.then_inc(release, 1)
                ins.then_inc(S["gathered"], 1)

            def combine(par, n, release=None):
                for t in range(NT):
                    ins = pe.matmul(bank[2 * t + n][:, :], turned[:, par, 2 + t, :], y[:, par, n, :],
                                    start=False, stop=False, skip_group_check=True)
                    if release is not None and t == 0:
                        ins.then_inc(release, 1)

            def expert_pair(par, it, q, S, land, free, lands):
                pe.wait_ge(S["y_ready"], 2 * q + 1)
                for h, s in ((0, UP_LO[par]), (1, UP_HI[par])):
                    pe.wait_ge(land[s], lands(s))
                    view = up_view(s)
                    for k in range(4):
                        if par == 0 and k % 2 == 0:
                            pe.wait_ge(S["xg_ready"], 4 * it + (2 * h + k // 2 + 1))
                        for e in range(2):
                            at = P * par + CELL * e
                            ins = pe.matmul(bank[5][CELL * e:CELL * (e + 1), :], xg[:, 4 * h + k, at:at + CELL],
                                            view[:, e, :, k, :],
                                            start=(h == 0 and k == 0), stop=(h == 1 and k == 3))
                            if par == 1 and h == 0 and k == 0 and e == 0:
                                ins.then_inc(free[DOWN[0]], 1)
                            if h == 1 and k == 0 and e == 0:
                                ins.then_inc(free[UP_LO[par]], 1)
                ins.then_inc(S["up_done"], 1)
                if par == 1:
                    pe.wait_ge(S["xg_ready"], 4 * it + 4)
                    gather(0, it + 1, S, bank[4], free[UP_HI[par]])
                pe.wait_ge(S["y_ready"], 2 * q + 1)
                combine(1 - par, 0, None if par else free[UP_HI[par]])
                pe.wait_ge(S["hidden_ready"], q + 1)
                for c in range(2):
                    pe.transpose(bank[7][:, c * P:(c + 1) * P],
                                 hidden[:, par, :].rearrange("p (f c) -> p c f", c=2)[:, c, :], ident)
                for t in range(NT):
                    ins = pe.transpose(bank[7][:, (2 + t) * P:(3 + t) * P], onehot_w[:, par, t, :], ident)
                ins.then_inc(S["turn_done"], 1)
                if par == 1:
                    pe.wait_ge(S["xg_ready"], 4 * it + 5)
                    gather(1, it + 1, S, bank[4])
                pe.wait_ge(S["y_ready"], 2 * q + 2)
                combine(1 - par, 1)
                if par == 1:
                    pe.wait_ge(S["xg_ready"], 4 * it + 6)
                    gather(2, it + 1, S, bank[4])
                s = DOWN[par]
                pe.wait_ge(land[s], lands(s))
                pe.wait_ge(S["turned_ready"], q + 1)
                for n in range(2):
                    for c in range(2):
                        for e in range(2):
                            ins = pe.matmul(bank[5 + n][CELL * e:CELL * (e + 1), :],
                                            turned[:, par, c, CELL * e:CELL * (e + 1)],
                                            down_view(s)[:, e, c, n * HALF:(n + 1) * HALF],
                                            start=(c == 0), stop=(c == 1))
                    ins.then_inc(S["down_done"], 1)
                if par == 1:
                    pe.wait_ge(S["xg_ready"], 4 * it + 7)
                    gather(3, it + 1, S, bank[4], free[s])

            zeros = const["zeros"].bitcast(BF16)

            def zero_acc(first):
                for b in range(4):
                    ins = pe.matmul(bank[b][:, :], zeros[:, 0:P], zeros, start=first, stop=not first,
                                    skip_group_check=True)
                return ins

            pe.wait_ge(loaded_consts, 16)
            for s in range(RING):
                pe.nop().then_inc(freed[s], 1)

            def turn(m):
                for t in range(NT):
                    pe.wait_ge(xf_ready, NT * m + t + 1)
                    for half in range(2):
                        u = 4 * m + 2 * t + half
                        if u >= 2:
                            pe.wait_ge(xfT_ready, u - 1)
                        for i in range(4):
                            ins = pe.transpose(bank[4 + u % 2][:, i * P:(i + 1) * P], xf[:, t, 4 * half + i, :], ident)
                        ins.then_inc(xf_turned, 1)
                pe.wait_ge(xfT_ready, 4 * m + 4)

            def mix(l):
                plan = plans[l]
                hd = slice(0, M_DIM)

                def open_bank(name):
                    b, n = plan[name]
                    if n > 1:
                        pe.wait_ge(drained[b], n - 1)
                    return bank[b]

                def done(ins, name):
                    ins.then_inc(filled[plan[name][0]], 1)

                def lands(s, n):
                    pe.wait_ge(landed[s], l * layer_lands[s] + 16 * n)

                def token_unit(u, t, release=None):
                    name = f"u{u}t{t}"
                    dst = open_bank(name)
                    w = UNIT_COLS[u][1] - UNIT_COLS[u][0]
                    lands(u, 1)
                    for k in range(KD):
                        ins = pe.matmul(dst[:, 0:w], xfT[:, k, t * P:(t + 1) * P], unit_view(u, w)[:, k, :],
                                        start=(k == 0), stop=(k == KD - 1))
                        if release is not None and k == 0:
                            ins.then_inc(freed[release], 1)
                    done(ins, name)

                def head_unit(u, i, name, release=None):
                    dst = open_bank(name)
                    lands(u, 1)
                    for h in range(2):
                        for k in range(KD):
                            ins = pe.matmul(dst[hd, h * SEQ:(h + 1) * SEQ],
                                            unit_view(u, M_WIDTH)[:, k, (2 * i + h) * M_DIM:(2 * i + h + 1) * M_DIM],
                                            xfT[:, k, :], start=(k == 0), stop=(k == KD - 1))
                            if release is not None and h == 0 and k == 0:
                                ins.then_inc(freed[release], 1)
                    done(ins, name)

                def turn_latent():
                    pe.wait_ge(latent_ready, NT * (l + 1))
                    for name, ks in (("cqT", (0, 1)), ("ckvT", (2,))):
                        dst = open_bank(name)
                        for i, k in enumerate(ks):
                            for t in range(NT):
                                ins = pe.transpose(dst[:, i * SEQ + t * P:i * SEQ + (t + 1) * P],
                                                   latent[:, t, k * P:(k + 1) * P], ident)
                        done(ins, name)

                def latent_q(t):
                    copied(pe, plan, "cqT")
                    for i, half in enumerate("ab"):
                        dst = open_bank(f"q{t}{half}")
                        w = 3 * QK_DIM
                        for k in range(2):
                            ins = pe.matmul(dst[:, 0:w], latentT[:, k, t * P:(t + 1) * P], w_uq[:, k, i * w:(i + 1) * w],
                                            start=(k == 0), stop=(k == 1))
                        done(ins, f"q{t}{half}")

                def latent_kv(t):
                    copied(pe, plan, "ckvT")
                    for i, half in enumerate("ab"):
                        dst = open_bank(f"kv{t}{half}")
                        w = 3 * (NOPE + V_DIM)
                        done(pe.matmul(dst[:, 0:w], latentT[:, 2, t * P:(t + 1) * P], w_ukv[:, i * w:(i + 1) * w],
                                       start=True, stop=True), f"kv{t}{half}")

                def spread(name, n):
                    dst = open_bank(name)
                    pe.wait_ge(diag_ready, 4 * l + n)
                    done(pe.matmul(dst[:, :], ones, diag[:, :, :].rearrange("p h s -> p (h s)"),
                                   start=True, stop=True), name)

                token_unit(3, 0)
                token_unit(3, 1)
                pe.wait_ge(loaded_mixer, MIXER_LOADS * (l + 1))
                dst = open_bank("conv_rows")
                for h in range(2 * M_HEADS):
                    pe.transpose(dst[hd, 5 * h:5 * h + 5], conv_rows[0:5, h * M_DIM:(h + 1) * M_DIM], ident[0:5, 0:5])
                done(pe.transpose(dst[:, 40:44], cb_rows[0:4, :], ident[0:4, 0:4]), "conv_rows")
                dst = open_bank("gate_w")
                for g in range(C_GROUPS):
                    ins = pe.transpose(dst[:, g * P:(g + 1) * P], gate_raw[:, g, :], ident)
                done(ins, "gate_w")

                token_unit(4, 0, 3)
                token_unit(4, 1)
                token_unit(5, 0, 4)
                token_unit(5, 1)
                head_unit(0, 0, "q01", 5)
                turn_latent()
                dst = open_bank("cum")
                pe.wait_ge(log_f_ready, l + 1)
                for t in range(NT):
                    pe.matmul(dst[:, 8 * t:8 * t + 4], const["upto"], log_f[:, t, :], start=True, stop=True)
                    ins = pe.matmul(dst[:, 8 * t + 4:8 * t + 8], ones, log_f[:, t, :], start=True, stop=True)
                done(ins, "cum")
                head_unit(0, 1, "q23")
                spread("rrow0", 1)
                spread("rrow1", 2)
                latent_q(0)
                head_unit(1, 0, "k01", 0)
                latent_q(1)
                spread("mrow0", 3)
                latent_kv(0)
                head_unit(1, 1, "k23")
                spread("mrow1", 4)
                latent_kv(1)
                copied(pe, plan, "gate_w")
                pe.wait_ge(gate_v_ready, l + 1)
                dst = open_bank("gated")
                for t in range(NT):
                    for g in range(C_GROUPS):
                        at = (t * C_GROUPS + g) * C_DIM
                        ins = pe.matmul(dst[:, at:at + C_DIM], gate_wT[:, g, :],
                                        gelu[:, t, C_WIDTH + g * C_DIM:C_WIDTH + (g + 1) * C_DIM], start=True, stop=True)
                done(ins, "gated")
                token_unit(2, 0, 1)
                token_unit(2, 1)

                for t in range(NT):
                    dst = open_bank(f"st{t}")
                    if t == 0:
                        pe.wait_ge(conv_act, 2 * (l + 1))
                    for h in range(M_HEADS):
                        ins = pe.matmul(dst[:, h * P:(h + 1) * P], conv_out[hd, M_HEADS + h, t * P:(t + 1) * P],
                                        conv_out[hd, h, t * P:(t + 1) * P], start=True, stop=True)
                        if t == 0 and h == 0:
                            ins.then_inc(freed[2], 1)
                    done(ins, f"st{t}")
                dst = open_bank("ktok")
                for h in range(M_HEADS):
                    ins = pe.transpose(dst[:, h * M_DIM:(h + 1) * M_DIM], conv_out[hd, M_HEADS + h, 0:P],
                                       ident[hd, 0:M_DIM])
                done(ins, "ktok")
                copied(pe, plan, "u2t0", "u2t1")
                dst = open_bank("state")
                pe.wait_ge(kw_ready, l + 1)
                for h in range(M_HEADS):
                    at = h * (M_DIM + 1)
                    pe.matmul(dst[hd, at:at + M_DIM], k_weighted[:, h, :], proj_a[:, 0, h * M_DIM:(h + 1) * M_DIM],
                              start=True, stop=True)
                    ins = pe.matmul(dst[hd, at + M_DIM:at + M_DIM + 1], k_weighted[:, h, :], ones[:, 0:1],
                                    start=True, stop=True)
                done(ins, "state")
                for t in range(NT):
                    dst = open_bank(f"num{t}")
                    pe.wait_ge(pt_ready, NT * l + t + 1)
                    for h in range(M_HEADS):
                        at = h * (M_DIM + 1)
                        pe.matmul(dst[:, at:at + M_DIM], decay[:, t, h, :], proj_a[:, t, h * M_DIM:(h + 1) * M_DIM],
                                  start=True, stop=True)
                        ins = pe.matmul(dst[:, at + M_DIM:at + M_DIM + 1], decay[:, t, h, :], ones[:, 0:1],
                                        start=True, stop=True)
                    done(ins, f"num{t}")
                copied(pe, plan, "state")
                dst = open_bank("inter")
                for h in range(M_HEADS):
                    at = h * (M_DIM + 1)
                    ins = pe.matmul(dst[:, at:at + M_DIM + 1], conv_out[hd, h, P:SEQ], state[hd, h, :],
                                    start=True, stop=True)
                done(ins, "inter")

                pe.wait_ge(qk_ready, NT * (l + 1))
                for i in range(6):
                    dst = open_bank(f"qkT{i}")
                    for j in range(2):
                        for t in range(NT):
                            ins = pe.transpose(dst[0:QK_DIM, j * SEQ + t * P:j * SEQ + (t + 1) * P],
                                               qk[:, t, 2 * i + j, :], ident)
                    done(ins, f"qkT{i}")
                copied(pe, plan, *[f"qkT{i}" for i in range(6)])

                def attend_scores(h):
                    dst = open_bank(f"sc{h}")
                    pe.matmul(dst[:, 0:P], qkT[0:QK_DIM, h, 0:P], qkT[0:QK_DIM, A_HEADS + h, 0:P], start=True, stop=True)
                    done(pe.matmul(dst[:, P:3 * P], qkT[0:QK_DIM, h, P:SEQ], qkT[0:QK_DIM, A_HEADS + h, :],
                                   start=True, stop=True), f"sc{h}")

                def attend_turn(h):
                    dst = open_bank(f"pT{h}")
                    pe.wait_ge(prob_ready, NT * (A_HEADS * l + h + 1))
                    for i in range(3):
                        ins = pe.transpose(dst[:, i * P:(i + 1) * P], prob[:, h % 2, i * P:(i + 1) * P], ident)
                    done(ins, f"pT{h}")

                o = [open_bank(f"o{t}") for t in range(NT)]

                def attend_values(h):
                    copied(pe, plan, f"pT{h}")
                    c = slice(h * V_DIM, (h + 1) * V_DIM)
                    pt = probT[:, h % 2, :]
                    ins = pe.matmul(o[0][:, c], pt[:, 0:P], kv[:, 0, h, NOPE:], start=True, stop=True)
                    if h == A_HEADS - 1:
                        done(ins, "o0")
                    pe.matmul(o[1][:, c], pt[:, P:2 * P], kv[:, 0, h, NOPE:], start=True, stop=False)
                    ins = pe.matmul(o[1][:, c], pt[:, 2 * P:3 * P], kv[:, 1, h, NOPE:], start=False, stop=True)
                    if h == A_HEADS - 1:
                        done(ins, "o1")

                attend_scores(0)
                for h in range(A_HEADS):
                    if h + 1 < A_HEADS:
                        attend_scores(h + 1)
                    attend_turn(h)
                    if h:
                        attend_values(h - 1)
                attend_values(A_HEADS - 1)

                for u in range(4):
                    t, half = u // 2, u % 2
                    dst = open_bank(f"yT{u}")
                    pe.wait_ge(y_rows, NT * l + t + 1)
                    for i in range(4):
                        ins = pe.transpose(dst[:, i * P:(i + 1) * P], xf[:, t, 4 * half + i, :], ident)
                    done(ins, f"yT{u}")
                copied(pe, plan, *[f"yT{u}" for u in range(4)])
                for n in range(2):
                    lands(n, 2)
                    for t in range(NT):
                        name = f"out{2 * t + n}"
                        dst = open_bank(name)
                        for k in range(KD):
                            ins = pe.matmul(dst[:, :], xfT[:, k, t * P:(t + 1) * P], unit_view(n, HALF)[:, k, :],
                                            start=(k == 0), stop=(k == KD - 1))
                            if n == 1 and t == 0 and k == 0:
                                ins.then_inc(freed[0], 1)
                        done(ins, name)

            for l in range(DEPTH):
                if mixer:
                    turn(PER * l)
                    mix(l)
                turn(PER * (l + 1) - 1)
                pe.wait_ge(loaded_ffn, ROUTER_LOADS * (l + 1))
                for t in range(NT):
                    for k in range(KD):
                        ins = pe.matmul(bank[6][:, t * 36:(t + 1) * 36], xfT[:, k, t * P:(t + 1) * P],
                                        w_router[:, k, :], start=(k == 0), stop=(k == KD - 1))
                        if mixer and t == 0 and k == 0:
                            ins.then_inc(freed[1], 1)
                ins.then_inc(logits_done, 1)
                if PER * (l + 1) > 1:
                    pe.wait_ge(x_ready, PER * (l + 1) - 1)
                zero_acc(True)
                pe.wait_ge(picked, l + 1)
                pe.matmul(bank[7][:, 0:NE], const["before"], work[:, 0, :], start=True, stop=True)
                pe.matmul(bank[7][:, NE:2 * NE], const["before"], work[:, 1, :], start=True, stop=False)
                pe.matmul(bank[7][:, NE:2 * NE], ones, work[:, 0, :], start=False, stop=True)
                pe.matmul(bank[7][:, 2 * NE:3 * NE], ones, work[:, 0, :], start=True, stop=False)
                pe.matmul(bank[7][:, 2 * NE:3 * NE], ones, work[:, 1, :], start=False, stop=True)\
                    .then_inc(counted, 1)
                pe.wait_ge(parts_ready, l + 1)
                it0 = l * (PAIRS // 2 + 1)
                for quarter, b in enumerate(START_BANKS):
                    if quarter == 3:
                        pe.wait_ge(main["xg_ready"], 4 * it0 + 1)
                    gather(quarter, it0, main, bank[b])
                with pe.Fori(0, PAIRS // 2) as j:
                    for par in range(2):
                        expert_pair(par, j + it0, 2 * j + (l * PAIRS + par), main, landed, freed,
                                    lambda s: j * pair_bytes[s]
                                    + (l * layer_lands[s] + 16 * mixer_uses[s] + pair_bytes[s]))
                pe.wait_ge(main["y_ready"], 2 * (l + 1) * PAIRS + 2)
                pe.wait_ge(main["xg_ready"], 4 * it0 + 4 * (PAIRS // 2 + 1))
                pe.wait_ge(over_ready, l + 1)
                n_over = pe.value_load(overint[0:1, l, CELLS_OVER:CELLS_OVER + 1], min_val=0, max_val=2)
                with pe.If(n_over > 0):
                    S = extra[l]
                    for s in range(RING):
                        pe.nop().then_inc(extra_freed[l][s], 1)
                    pe.nop().then_inc(S["gathered"], 4)
                    with pe.Fori(0, n_over) as j:
                        for par in range(2):
                            expert_pair(par, j, 2 * j + par, S, extra_landed[l], extra_freed[l],
                                        lambda s: j * pair_bytes[s] + pair_bytes[s])
                    pe.wait_ge(S["y_ready"], n_over * 4 + 2)
                with pe.Else():
                    pe.nop()
                for n in range(2):
                    combine(1, n)
                zero_acc(False).then_inc(acc_done, 1)

            def last_block():
                plan = plan2

                def open_bank(name):
                    b, n = plan[name]
                    pe.wait_ge(drained[b], n - 1)
                    return bank[b]

                def done(ins, name):
                    ins.then_inc(filled[plan[name][0]], 1)

                def unit(name, cols):
                    s, n = unit2[name]
                    pe.wait_ge(landed[s], DEPTH * layer_lands[s] + 16 * n)
                    return ring[s][:, :].rearrange("p (k n) -> p k n", n=cols)

                behind = []

                def give_back(ins):
                    if behind:
                        ins.then_inc(freed[unit2[behind.pop()][0]], 1)

                def token_tile(u, t):
                    dst = open_bank(f"{u}{t}")
                    w = unit(u, HALF)
                    for k in range(KD):
                        ins = pe.matmul(dst[:, :], xfT[:, k, t * P:(t + 1) * P], w[:, k, :],
                                        start=(k == 0), stop=(k == KD - 1))
                        if k == 0:
                            give_back(ins)
                    done(ins, f"{u}{t}")
                    if t == 1:
                        behind.append(u)

                def pair_unit(u):
                    w = unit(u, HALF)
                    for half in range(2):
                        name = u + "AB"[half]
                        dst = open_bank(name)
                        for i in range(2):
                            at = (2 * half + i) * P
                            for k in range(KD):
                                ins = pe.matmul(dst[:, i * SEQ:(i + 1) * SEQ], w[:, k, at:at + P], xfT[:, k, :],
                                                start=(k == 0), stop=(k == KD - 1))
                                if k == 0:
                                    give_back(ins)
                        done(ins, name)
                    behind.append(u)

                for u in ("qa", "ka"):
                    for t in range(NT):
                        token_tile(u, t)
                pair_unit("qb")
                pair_unit("kb")
                pe.wait_ge(loaded_second, 4 * 16)
                pe.wait_ge(rel_ready, 1)
                dst = open_bank("rel")
                done(pe.transpose(dst[0:33, 0:S_HEADS], s_rel[0:S_HEADS, :], ident[0:S_HEADS, 0:S_HEADS]), "rel")
                copied(pe, plan, "rel")
                dst = open_bank("f")
                done(pe.matmul(dst[0:S_HEADS, 0:384], s_relT[0:33, :], buckets[0:33, :], start=True, stop=True), "f")
                for u in ("va", "vb"):
                    for t in range(NT):
                        token_tile(u, t)
                pe.wait_ge(s_qk_ready, 1)
                for a, kind in enumerate("qk"):
                    for t in range(NT):
                        dst = open_bank(f"{kind}T{t}")
                        for i in range(S_HEADS // 2):
                            ins = pe.transpose(dst[:, i * P:(i + 1) * P],
                                               s_qk[:, t, a * S_WIDTH + i * P:a * S_WIDTH + (i + 1) * P], ident)
                        done(ins, f"{kind}T{t}")
                copied(pe, plan, "qbA", "qbB", "kbA", "kbB", "va0", "va1", "vb0", "vb1", "qT0", "qT1", "kT0", "kT1")

                def first_stage(h):
                    rows_h = slice(S_DIM * (h % 2), S_DIM * (h % 2 + 1))
                    q, k = s_qkbT[rows_h, 0, h // 2, :], s_qkbT[rows_h, 1, h // 2, :]
                    dst = open_bank(f"z{h}")
                    pe.matmul(dst[:, 0:SEQ], k[:, 0:P], q, start=True, stop=False, skip_group_check=True)
                    done(pe.matmul(dst[:, SEQ:3 * P], k[:, P:], q[:, P:], start=False, stop=False,
                                   skip_group_check=True), f"z{h}")
                    q, k = s_qkaT[rows_h, 0, h // 2, :], s_qkaT[rows_h, 1, h // 2, :]
                    dst = open_bank(f"sc{h}")
                    pe.matmul(dst[:, 0:P], q[:, 0:P], k[:, 0:P], start=True, stop=True)
                    done(pe.matmul(dst[:, P:3 * P], q[:, P:], k, start=True, stop=True), f"sc{h}")

                def second_stage(h):
                    dst = open_bank(f"r{h}")
                    pe.wait_ge(s_log_ready, h + 1)
                    log = s_log[:, h % 2, :]
                    pe.matmul(dst[:, 0:SEQ], const["fromon"], log[:, 0:SEQ], start=False, stop=False,
                              skip_group_check=True)
                    pe.matmul(dst[:, P:SEQ], ones, log[:, SEQ:], start=False, stop=False, skip_group_check=True)
                    done(pe.matmul(dst[:, SEQ:3 * P], const["fromon"], log[:, SEQ:], start=False, stop=True,
                                   skip_group_check=True), f"r{h}")
                    dst = open_bank(f"pT{h}")
                    pe.wait_ge(s_prob_ready, NT * (h + 1))
                    for i in range(3):
                        ins = pe.transpose(dst[:, i * P:(i + 1) * P], s_prob[:, h % 2, i * P:(i + 1) * P], ident)
                    done(ins, f"pT{h}")

                def third_stage(h):
                    c = slice(h * S_DIM, (h + 1) * S_DIM)
                    for a, name, src in ((1, "ob", s_log), (0, "oa", s_probT)):
                        dst = open_bank(f"{name}{h}")
                        if a:
                            pe.wait_ge(s_weight_ready, h + 1)
                        w = src[:, h % 2, :]
                        pe.matmul(dst[:, 0:S_DIM], w[:, 0:P], s_v[:, a, 0, c], start=True, stop=True)
                        pe.matmul(dst[:, S_DIM:P], w[:, P:SEQ], s_v[:, a, 0, c], start=True, stop=False)
                        done(pe.matmul(dst[:, S_DIM:P], w[:, SEQ:], s_v[:, a, 1, c], start=False, stop=True),
                             f"{name}{h}")

                for h in range(S_HEADS + 1):
                    if h < S_HEADS:
                        first_stage(h)
                    front, back = step_tiles(h)
                    for n in front:
                        token_tile(n[:-1], int(n[-1]))
                    if h:
                        second_stage(h - 1)
                    for n in back:
                        token_tile(n[:-1], int(n[-1]))
                    if h:
                        third_stage(h - 1)

                for i in range(4):
                    a, t = i // 2, i % 2
                    pe.wait_ge(s_o_ready, i + 1)
                    dst = open_bank(f"oT{i}")
                    for k in range(4):
                        ins = pe.transpose(dst[:, k * P:(k + 1) * P], s_o[:, a, t, k * P:(k + 1) * P], ident)
                        if k == 0:
                            give_back(ins)
                    done(ins, f"oT{i}")
                copied(pe, plan, *[f"oT{i}" for i in range(4)])
                for t in range(NT):
                    for n in range(2):
                        for a, u in enumerate(("upa", "upb")):
                            name = f"y{'ab'[a]}{t}{n}"
                            dst = open_bank(name)
                            w = unit(u, D)
                            for k in range(4):
                                ins = pe.matmul(dst[:, :], s_oT[:, a, k, t * P:(t + 1) * P],
                                                w[:, k, n * HALF:(n + 1) * HALF], start=(k == 0), stop=(k == 3))
                            done(ins, name)
                for u in range(4):
                    t, half = u // 2, u % 2
                    dst = open_bank(f"yT{u}")
                    pe.wait_ge(s_rows, t + 1)
                    for i in range(4):
                        ins = pe.transpose(dst[:, i * P:(i + 1) * P], xf[:, t, 4 * half + i, :], ident)
                    done(ins, f"yT{u}")
                copied(pe, plan, *[f"yT{u}" for u in range(4)])
                for n in range(2):
                    w = unit(f"out{n}", HALF)
                    for t in range(NT):
                        dst = open_bank(f"out{2 * t + n}")
                        for k in range(KD):
                            ins = pe.matmul(dst[:, :], xfT[:, k, t * P:(t + 1) * P], w[:, k, :],
                                            start=(k == 0), stop=(k == KD - 1))
                        done(ins, f"out{2 * t + n}")

            if second:
                turn(PER * DEPTH)
                last_block()

        @block.scalar
        def _(act):
            step = Chain(act, act_step)

            def copy_quarter(quarter, it, S, src):
                act.wait_ge(S["gathered"], 4 * it + (quarter + 1))
                act.activation(xg[:, 2 * quarter:2 * quarter + 2, :], src[:, :].rearrange("p (k s) -> p k s", k=2),
                               ACT.Copy).then_inc(S["xg_ready"], 1)

            def expert_pair(par, it, q, S):
                act.wait_ge(S["up_done"], q + 1)
                act.activation(silu[:, par, :], bank[5][:, 0:DE], ACT.Silu).then_inc(S["silu_ready"], 1)
                if par == 1:
                    for quarter in range(3):
                        copy_quarter(quarter, it + 1, S, bank[4])
                for n in range(2):
                    act.wait_ge(S["down_done"], 2 * q + (n + 1))
                    act.activation(y[:, par, n, :], bank[5 + n][:, :], ACT.Copy).then_inc(S["y_ready"], 1)
                if par == 1:
                    copy_quarter(3, it + 1, S, bank[4])

            def norm_turn(m):
                for t in range(NT):
                    if m == 0:
                        act.wait_ge(loaded_x[t], 16)
                    else:
                        act.wait_ge(x_tile_ready if t == 0 else x_ready, m)
                    if m or t:
                        act.wait_ge(squares, NT * m + t)
                    act.activation(square, x[:, t, :], ACT.Square, accum_out=stats[:, t:t + 1])\
                       .then_inc(squares, 1)
                for u in range(4 * m, 4 * m + 4):
                    act.wait_ge(xf_turned, u + 1)
                    t, half = u % 4 // 2, u % 2
                    act.activation(xfT[:, 4 * half:4 * half + 4, t * P:(t + 1) * P],
                                   bank[4 + u % 2][:, :].rearrange("p (k s) -> p k s", k=4), ACT.Copy)\
                       .then_inc(xfT_ready, 1)

            def mix(l):
                plan = plans[l]
                hd = slice(0, M_DIM)

                def copy_out(name, dst, src):
                    src_bank = full(act, plan, name)
                    act.activation(dst, src(src_bank), ACT.Copy).then_inc(left(plan, name), 1)

                def token_unit(u, t):
                    c0, c1 = UNIT_COLS[u][0] - A_COLS, UNIT_COLS[u][1] - A_COLS
                    src = full(act, plan, f"u{u}t{t}")
                    if c0 < A_COLS < c1:
                        w = A_COLS - c0
                        step(act.activation(proj_a[:, t, c0:], src[:, 0:w], ACT.Copy))
                        ins = act.activation(proj_b[:, t, 0:c1 - A_COLS], src[:, w:c1 - c0], ACT.Copy)
                    elif c0 < A_COLS:
                        ins = act.activation(proj_a[:, t, c0:c1], src[:, 0:c1 - c0], ACT.Copy)
                    else:
                        ins = act.activation(proj_b[:, t, c0 - A_COLS:c1 - A_COLS], src[:, 0:c1 - c0], ACT.Copy)
                    ins.then_inc(left(plan, f"u{u}t{t}"), 1)

                def heads(name, first):
                    copy_out(name, conv_raw[hd, first:first + 2, 3:],
                             lambda b: b[hd, :].rearrange("p (h s) -> p h s", h=2))

                def latent_q(t):
                    for i, half in enumerate("ab"):
                        copy_out(f"q{t}{half}", qk[:, t, 3 * i:3 * i + 3, :],
                                 lambda b: b[:, 0:3 * QK_DIM].rearrange("p (h d) -> p h d", h=3))

                def latent_kv(t):
                    for i, half in enumerate("ab"):
                        copy_out(f"kv{t}{half}", kv[:, t, 3 * i:3 * i + 3, :],
                                 lambda b: b[:, 0:3 * P].rearrange("p (h d) -> p h d", h=3))

                for t in range(NT):
                    token_unit(3, t)
                for t in range(NT):
                    token_unit(4, t)
                copied(act, plan, "u3t0", "u3t1", "u4t0", "u4t1")
                for i, (at, n) in enumerate(((CQ_AT, Q_RANK), (CKV_AT, KV_RANK))):
                    for t in range(NT):
                        if 4 * l + 2 * i + t:
                            act.wait_ge(latent_sums, 4 * l + 2 * i + t)
                        act.activation(square[:, 0:n], proj_b[:, t, at:at + n], ACT.Square,
                                       accum_out=head_sums[:, 2 * i + t:2 * i + t + 1]).then_inc(latent_sums, 1)
                act.wait_ge(gate_abs, l + 1)
                act.activation(gate_in[:, :, 2, 0:4], gate_in[:, :, 1, 4:8], ACT.Exp).then_inc(gate_exp, 1)
                act.wait_ge(gate_exp, l + 1)
                act.activation(gate_in[:, :, 2, 4:8], gate_in[:, :, 2, 0:4], ACT.Ln, bias=1.0).then_inc(gate_ln, 1)
                for t in range(NT):
                    token_unit(5, t)
                copied(act, plan, "u5t0", "u5t1")
                act.activation(gelu, proj_b[:, :, CU_AT:], ACT.Gelu_apprx_tanh).then_inc(gelu_ready, 1)
                act.wait_ge(latent_sums, 4 * l + 4)
                heads("q01", 0)
                copy_out("cqT", latentT[:, 0:2, :], lambda b: b[:, :].rearrange("p (k s) -> p k s", k=2))
                copy_out("ckvT", latentT[:, 2, :], lambda b: b[:, 0:SEQ])
                heads("q23", 2)
                latent_q(0)
                heads("k01", 4)
                latent_q(1)
                act.wait_ge(latent_ready, NT * (l + 1))
                act.wait_ge(gelu_ready, l + 1)
                latent_kv(0)
                heads("k23", 6)
                latent_kv(1)
                for t in range(NT):
                    act.wait_ge(decay_wanted, NT * l + t + 1)
                    act.activation(decay[:, t, :, :], decay[:, t, :, :], ACT.Exp).then_inc(decay_done, 1)
                act.activation(small_exp, small_exp, ACT.Exp).then_inc(decay_done, 1)
                for i in range(2):
                    act.wait_ge(conv_ready, 2 * l + i + 1)
                    part = conv_out[hd, M_HEADS * i:M_HEADS * (i + 1), :]
                    act.activation(part, part, ACT.Silu).then_inc(conv_act, 1)
                    token_unit(2, i)
                copied(act, plan, "u2t0", "u2t1")
                act.activation(proj_a[:, :, M_WIDTH:], proj_a[:, :, M_WIDTH:], ACT.Sigmoid).then_inc(out_gate, 1)
                copy_out("state", state[hd, :, :],
                         lambda b: b[hd, 0:M_HEADS * (M_DIM + 1)].rearrange("p (h d) -> p h d", h=M_HEADS))
                for i in range(6):
                    copy_out(f"qkT{i}", qkT[0:QK_DIM, 2 * i:2 * i + 2, :],
                             lambda b: b[0:QK_DIM, :].rearrange("p (h s) -> p h s", h=2))
                for h in range(A_HEADS):
                    act.wait_ge(logits_ready, A_HEADS * l + h + 1)
                    for t, c in ((0, slice(0, P)), (1, slice(P, 3 * P))):
                        act.activation(prob[:, h % 2, c], prob[:, h % 2, c], ACT.Exp, bias=soft[:, h, 0, t:t + 1],
                                       accum_out=soft[:, h, 1, t:t + 1]).then_inc(prob_ready, 1)
                    copy_out(f"pT{h}", probT[:, h % 2, :], lambda b: b[:, 0:3 * P])
                for u in range(4):
                    t, half = u // 2, u % 2
                    copy_out(f"yT{u}", xfT[:, 4 * half:4 * half + 4, t * P:(t + 1) * P],
                             lambda b: b[:, :].rearrange("p (k s) -> p k s", k=4))

            act.nop().then_inc(main["y_ready"], 2)
            for l in range(DEPTH):
                if mixer:
                    norm_turn(PER * l)
                    if l == 0:
                        act.wait_ge(angles, 1)
                        act.activation(cos_sin[:, :, :, :], cos_sin[:, :, :, :], ACT.Sin).then_inc(rope_ready, 1)
                    mix(l)
                norm_turn(PER * (l + 1) - 1)
                act.wait_ge(exp_wanted, l + 1)
                act.activation(expout[:, :, 0:7], expin[:, :, 0:7], ACT.Exp).then_inc(exp_done, 1)
                it0 = l * (PAIRS // 2 + 1)
                for quarter, b in enumerate(START_BANKS):
                    copy_quarter(quarter, it0, main, bank[b])
                with act.Fori(0, PAIRS // 2) as j:
                    for par in range(2):
                        expert_pair(par, j + it0, 2 * j + (l * PAIRS + par), main)
                act.wait_ge(over_ready, l + 1)
                n_over = act.value_load(overint[0:1, l, CELLS_OVER:CELLS_OVER + 1], min_val=0, max_val=2)
                with act.If(n_over > 0):
                    S = extra[l]
                    act.nop().then_inc(S["y_ready"], 2)
                    act.nop().then_inc(S["xg_ready"], 4)
                    with act.Fori(0, n_over) as j:
                        for par in range(2):
                            expert_pair(par, j, 2 * j + par, S)
                with act.Else():
                    act.nop()

            def last_block():
                plan = plan2

                def copy_out(name, dst, src, scale=1.0):
                    src_bank = full(act, plan, name)
                    act.activation(dst, src(src_bank), ACT.Copy, scale=scale).then_inc(left(plan, name), 1)

                whole = lambda b: b[:, :]
                for a, u in enumerate(("qa", "ka")):
                    for t in range(NT):
                        copy_out(f"{u}{t}", s_qk[:, t, a * S_WIDTH:(a + 1) * S_WIDTH], whole)
                for a, u in enumerate(("qb", "kb")):
                    for half in range(2):
                        copy_out(u + "AB"[half], s_qkbT[:, a, 2 * half:2 * half + 2, :],
                                 lambda b: b[:, :].rearrange("p (i s) -> p i s", i=2),
                                 scale=1.0 if a else float(S_DIM) ** -0.5)
                for a, u in enumerate(("va", "vb")):
                    for t in range(NT):
                        copy_out(f"{u}{t}", s_v[:, a, t, :], whole)
                for a, kind in enumerate("qk"):
                    for t in range(NT):
                        copy_out(f"{kind}T{t}", s_qkaT[:, a, :, t * P:(t + 1) * P],
                                 lambda b: b[:, :].rearrange("p (i s) -> p i s", i=4))
                steps = [0]

                def in_place(dst, src, func, **kw):
                    steps[0] += 1
                    act.activation(dst, src, func, **kw).then_inc(s_act, 1)
                    act.wait_ge(s_act, steps[0])

                def z_tile(n):
                    if n[0] == "z":
                        copy_out(n, s_z[:, "ab".index(n[1]), int(n[-1]), :], whole)

                for h in range(S_HEADS + 1):
                    front, back = step_tiles(h)
                    if h < S_HEADS:
                        log = s_log[:, h % 2, :]
                        src = full(act, plan, f"z{h}")[:, 0:3 * P]
                        if h >= 2:
                            copied(act, plan, f"ob{h - 2}")
                        in_place(log, src, ACT.Abs)
                        in_place(log, log, ACT.Exp, scale=-1.0)
                        act.activation(log, log, ACT.Ln, bias=1.0).then_inc(s_ln_ready, 1)
                    for n in front:
                        z_tile(n)
                    if h < S_HEADS:
                        act.wait_ge(s_logits_ready, h + 1)
                        for t, c in ((0, slice(0, P)), (1, slice(P, 3 * P))):
                            act.activation(s_prob[:, h % 2, c], s_prob[:, h % 2, c], ACT.Exp,
                                           bias=s_soft[:, h, 0, t:t + 1], accum_out=s_soft[:, h, 1, t:t + 1])\
                               .then_inc(s_prob_ready, 1)
                    if h:
                        g = h - 1
                        copy_out(f"pT{g}", s_probT[:, g % 2, :], lambda b: b[:, 0:3 * P])
                        copied(act, plan, f"r{g}")
                        act.activation(s_log[:, g % 2, :], s_log[:, g % 2, :], ACT.Exp).then_inc(s_weight_ready, 1)
                    for n in back:
                        z_tile(n)
                    if h == 4:
                        copied(act, plan, "za0", "za1", "zb0", "zb1")
                        act.activation(s_z, s_z, ACT.Silu).then_inc(s_silu_ready, 1)
                for i in range(4):
                    a, t = i // 2, i % 2
                    copy_out(f"oT{i}", s_oT[:, a, :, t * P:(t + 1) * P],
                             lambda b: b[:, :].rearrange("p (k s) -> p k s", k=4))
                act.wait_ge(s_gates_in, 1)
                act.activation(s_gates, s_gates, ACT.Sigmoid).then_inc(s_gate_ready, 1)
                for u in range(4):
                    t, half = u // 2, u % 2
                    copy_out(f"yT{u}", xfT[:, 4 * half:4 * half + 4, t * P:(t + 1) * P],
                             lambda b: b[:, :].rearrange("p (k s) -> p k s", k=4))

            if second:
                norm_turn(PER * DEPTH)
                last_block()

        @block.vector
        def _(dve):
            step = Chain(dve, vec_step)

            PLAIN_LINKS, WEIGHTED_LINKS = 2 * NT, 3 * NT + 1
            LOOP_LINKS = PLAIN_LINKS + 2 * WEIGHTED_LINKS
            LAYER_LINKS = PLAIN_LINKS + WEIGHTED_LINKS + PAIRS // 2 * LOOP_LINKS

            def plain_hot(it, S, link):
                for t in range(NT):
                    link(dve.tensor_scalar(hotwork[:, :], slots_gathered[:, :], slot_of[:, 0, t:t + 1], None,
                                           ALU.is_equal))
                    ins = dve.scalar_tensor_tensor(onehot[:, t, :], slots_gathered[:, :], slot_of[:, 1, t:t + 1],
                                                   hotwork[:, :], ALU.is_equal, ALU.add)
                    if t < NT - 1:
                        link(ins)
                ins.then_inc(S["hot_ready"], 1)
                dve.wait_ge(S["hot_ready"], it + 1)
                link(dve.tensor_scalar(slots_gathered[:, :], slots_gathered[:, :], 2.0 * P, None, ALU.add))

            def weighted_hot(par, link):
                w = hotwork[:, 0:P]
                for t in range(NT):
                    link(dve.tensor_scalar(w, slots_weighted[:, :], slot_of[:, 0, t:t + 1], gates[:, 0, t:t + 1],
                                           ALU.is_equal, ALU.mult))
                    link(dve.tensor_scalar(onehot_w[:, par, t, :], slots_weighted[:, :], slot_of[:, 1, t:t + 1],
                                           gates[:, 1, t:t + 1], ALU.is_equal, ALU.mult))
                    link(dve.tensor_tensor(onehot_w[:, par, t, :], onehot_w[:, par, t, :], w, ALU.add))
                link(dve.tensor_scalar(slots_weighted[:, :], slots_weighted[:, :], float(P), None, ALU.add))

            def expert_pair(par, it, q, S, links):
                link = Chain(dve, S["vec"], links)
                if par == 0:
                    dve.wait_ge(S["gathered"], 4 * it + 4)
                    plain_hot(it + 1, S, link)
                weighted_hot(1 - par, link)
                dve.wait_ge(S["silu_ready"], q + 1)
                dve.tensor_tensor(hidden[:, par, :], silu[:, par, :], bank[5][:, DE:2 * DE], ALU.mult)\
                   .then_inc(S["hidden_ready"], 1)
                dve.wait_ge(S["turn_done"], q + 1)
                dve.tensor_copy(turned[:, par, :, :], bank[7][:, :].rearrange("p (c s) -> p c s", c=4))\
                   .then_inc(S["turned_ready"], 1)

            def first_of(dst, src, n, link):
                m = rowmax[:, :]
                mb = rowmax[:, :].unsqueeze(2).broadcast_to([P, NT, n])
                rev = const["rev"][:, 0:n].unsqueeze(1).broadcast_to([P, NT, n])
                link(dve.tensor_reduce(m, src, AX.X, ALU.max))
                link(dve.tensor_tensor(dst, src, mb, ALU.is_equal))
                link(dve.tensor_tensor(dst, dst, rev, ALU.mult))
                link(dve.tensor_reduce(m, dst, AX.X, ALU.max))
                link(dve.tensor_tensor(dst, dst, mb, ALU.is_equal))

            def route(l):
                gl, el = logits[:, :, 0:N_GROUPS], logits[:, :, N_GROUPS:]
                bias = router_bias[:, :].unsqueeze(1).broadcast_to([P, NT, 36])
                gw = [groupwork[:, :, i, :] for i in range(3)]
                rb = lambda n: rowmax[:, :].unsqueeze(2).broadcast_to([P, NT, n])
                dve.wait_ge(logits_done, l + 1)
                step(dve.tensor_copy(logits[:, :, :], bank[6][:, 0:72].rearrange("p (t n) -> p t n", t=NT)))
                step(dve.tensor_tensor(gw[0], gl, bias[:, :, 0:N_GROUPS], ALU.add))
                first_of(gw[1], gw[0], N_GROUPS, step)
                step(dve.tensor_scalar(gw[2], gw[1], -1.0, -NEG, ALU.add, ALU.mult))
                out_of = gw[2].unsqueeze(3).broadcast_to([P, NT, N_GROUPS, PER_GROUP])
                four = "p t (g e) -> p t g e"
                step(dve.tensor_tensor(scores[:, :, :].rearrange(four, g=N_GROUPS), el.rearrange(four, g=N_GROUPS),
                                       out_of, ALU.add))
                step(dve.tensor_tensor(biased, scores[:, :, :], bias[:, :, N_GROUPS:], ALU.add))
                first_of(pick[:, :, 0, :], biased, NE, step)
                step(dve.scalar_tensor_tensor(biased, pick[:, :, 0, :], 4 * NEG, biased, ALU.mult, ALU.add))
                first_of(pick[:, :, 1, :], biased, NE, step)
                dve.tensor_tensor(work[:, :, :], pick[:, :, 0, :], pick[:, :, 1, :], ALU.add).then_inc(picked, 1)
                step(dve.tensor_reduce(rowmax[:, :], gl, AX.X, ALU.max))
                step(dve.tensor_tensor(expin[:, :, 0:N_GROUPS], gl, rb(N_GROUPS), ALU.subtract))
                step(dve.tensor_tensor(gw[2], expin[:, :, 0:N_GROUPS], gw[1], ALU.mult))
                step(dve.tensor_reduce(expin[:, :, 4:5], gw[2], AX.X, ALU.add))
                step(dve.tensor_reduce(rowmax[:, :], scores[:, :, :], AX.X, ALU.max))
                for i in range(2):
                    step(dve.tensor_tensor(scores[:, :, :], pick[:, :, i, :], el, ALU.mult))
                    step(dve.tensor_reduce(expin[:, :, 5 + i:6 + i], scores[:, :, :], AX.X, ALU.add))
                dve.tensor_tensor(expin[:, :, 5:7], expin[:, :, 5:7], rb(2), ALU.subtract).then_inc(exp_wanted, 1)
                dve.wait_ge(counted, l + 1)
                step(dve.tensor_copy(position[:, :, :], bank[7][:, 0:3 * NE].rearrange("p (t e) -> p t e", e=NE)))
                pos = position[:, 0:NT, :]
                step(dve.tensor_scalar(biased, pos, CELL - 0.5, float(2 * SEQ * NE), ALU.is_gt, ALU.mult))
                step(dve.tensor_tensor(biased, biased, pos, ALU.add))
                step(dve.tensor_tensor(biased, biased, const["cell64"].unsqueeze(1).broadcast_to([P, NT, NE]), ALU.add))
                find_slots()

            def find_slots():
                for i in range(2):
                    step(dve.tensor_tensor(scores[:, :, :], pick[:, :, i, :], biased, ALU.mult))
                    step(dve.tensor_reduce(slot_of[:, i, :], scores[:, :, :], AX.X, ALU.add))

            def finish_route(l):
                dve.wait_ge(exp_done, l + 1)
                step(dve.tensor_reduce(expin[:, :, 0:1], expout[:, :, 0:N_GROUPS], AX.X, ALU.add))
                step(dve.tensor_tensor(expin[:, :, 1:2], expout[:, :, 5:6], expout[:, :, 6:7], ALU.add))
                step(dve.tensor_tensor(expin[:, :, 0:1], expin[:, :, 0:1], expin[:, :, 1:2], ALU.mult))
                step(dve.reciprocal(expin[:, :, 0:1], expin[:, :, 0:1]))
                step(dve.tensor_tensor(expin[:, :, 0:1], expin[:, :, 0:1], expout[:, :, 4:5], ALU.mult))
                for i in range(2):
                    step(dve.tensor_tensor(gates[:, i, :], expin[:, :, 0:1].rearrange("p t o -> p (t o)"),
                                           expout[:, :, 5 + i:6 + i].rearrange("p t o -> p (t o)"), ALU.mult))

            def overflow(l):
                count = position[:, NT, :]
                cells, ahead, total = over[:, 0, :], over[:, 1, :], over[:, 2, :]
                step(dve.tensor_scalar(cells, count, CELL + 0.5, None, ALU.is_gt))
                for lim in range(2 * CELL, SEQ, CELL):
                    step(dve.scalar_tensor_tensor(cells, count, lim + 0.5, cells, ALU.is_gt, ALU.add))
                step(dve.tensor_copy(total, cells))
                a, b = total, ahead
                for sh in (1, 2, 4, 8, 16):
                    step(dve.tensor_copy(b, a))
                    step(dve.tensor_tensor(b[:, sh:], a[:, sh:], a[:, 0:NE - sh], ALU.add))
                    a, b = b, a
                total = a
                cidx = const["iota"][:, 0:CELLS_OVER].unsqueeze(2).broadcast_to([P, CELLS_OVER, NE])
                step(dve.tensor_tensor(overlist[:, :, :], total.unsqueeze(1).broadcast_to([P, CELLS_OVER, NE]), cidx,
                                       ALU.is_le))
                step(dve.tensor_reduce(oversum[:, 0:CELLS_OVER], overlist[:, :, :], AX.X, ALU.add))
                step(dve.tensor_scalar(oversum[:, 0:CELLS_OVER], oversum[:, 0:CELLS_OVER], float(NE - 1), None, ALU.min))
                last = total[:, NE - 1:NE]
                step(dve.tensor_scalar(oversum[:, CELLS_OVER:], last, 4.5, None, ALU.is_gt))
                step(dve.scalar_tensor_tensor(oversum[:, CELLS_OVER:], last, 0.5, oversum[:, CELLS_OVER:],
                                              ALU.is_gt, ALU.add))
                dve.tensor_copy(overint[0:1, l, :], oversum[0:1, :]).then_inc(over_ready, 1)
                step(dve.tensor_tensor(b, total, cells, ALU.subtract))
                step(dve.tensor_scalar(b, b, float(CELL), float(CELL * (NE - 1)), ALU.mult, ALU.add))
                step(dve.tensor_tensor(b, b, const["cell64"], ALU.subtract))
                pos = position[:, 0:NT, :]
                step(dve.tensor_scalar(biased, pos, CELL - 0.5, None, ALU.is_gt))
                step(dve.tensor_tensor(biased, biased, b.unsqueeze(1).broadcast_to([P, NT, NE]), ALU.mult))
                step(dve.tensor_tensor(biased, biased, pos, ALU.add))
                step(dve.tensor_tensor(biased, biased, const["cell64"].unsqueeze(1).broadcast_to([P, NT, NE]), ALU.add))
                find_slots()

            def norm(m, by_chunk, gains):
                dve.wait_ge(loaded_gain, 16 * gains)
                for t in range(NT):
                    dve.wait_ge(rstd_ready, NT * m + t + 1)
                    dve.scalar_tensor_tensor(xf[:, t, :, :], x[:, t, :].rearrange(by_chunk, k=KD),
                                             stats[:, 8 + t:9 + t], gain[:, :].rearrange(by_chunk, k=KD),
                                             ALU.mult, ALU.mult).then_inc(xf_ready, 1)

            def rope_tables():
                two_pi = 2.0 * np.pi
                c1 = 6.28125
                c2 = float(np.float32(np.round((two_pi - c1) * 2.0 ** 20) / 2.0 ** 20))
                c3 = two_pi - c1 - c2
                pos = gate_in[:, :, 0, 0:1]
                ang, turns, r = [place(turned_at + 32 * i, NT, 16) for i in range(3)]
                magic = 12582912.0
                dve.wait_ge(loaded_positions, 16)
                step(dve.tensor_copy(pos, positions[:, :].unsqueeze(2)))
                step(dve.tensor_tensor(ang, pos.broadcast_to([P, NT, 16]),
                                       const["inv_freq"].unsqueeze(1).broadcast_to([P, NT, 16]), ALU.mult))
                for i, quarter in ((0, 0.25), (1, 0.0)):
                    step(dve.tensor_scalar(turns, ang, 1.0 / two_pi, quarter, ALU.mult, ALU.add))
                    step(dve.tensor_scalar(turns, turns, magic, None, ALU.add))
                    step(dve.tensor_scalar(turns, turns, -magic, None, ALU.add))
                    step(dve.scalar_tensor_tensor(r, turns, -c1, ang, ALU.mult, ALU.add))
                    step(dve.scalar_tensor_tensor(r, turns, -c2, r, ALU.mult, ALU.add))
                    step(dve.scalar_tensor_tensor(r, turns, -c3, r, ALU.mult, ALU.add))
                    step(dve.tensor_scalar(r, r, quarter * two_pi, 3.1415925, ALU.add, ALU.min))
                    ins = dve.tensor_scalar(cos_sin[:, i, :, :], r, -3.1415925, None, ALU.max)
                    if i == 0:
                        step(ins)
                ins.then_inc(angles, 1)

            def mix(l):
                plan = plans[l]
                hd = slice(0, M_DIM)
                rows = xf[:, :, :, :].rearrange("p t k i -> p t (k i)")

                def spread(ap, *shape):
                    return ap.broadcast_to([P, *shape])

                def rstds(n):
                    dve.wait_ge(head_rstd_ready, 6 * l + n)

                src = full(dve, plan, "conv_rows")
                step(dve.tensor_copy(conv_w[hd, :, :], src[hd, 0:40].rearrange("p (h j) -> p h j", j=5)))
                dve.tensor_copy(cb, src[:, 40:44]).then_inc(left(plan, "conv_rows"), 1)
                src = full(dve, plan, "gate_w")
                dve.tensor_tensor(gate_wT, src[:, :].rearrange("p (g s) -> p g s", g=C_GROUPS),
                                  spread(const["upto"].unsqueeze(1), C_GROUPS, P), ALU.mult)\
                   .then_inc(left(plan, "gate_w"), 1)
                copied(dve, plan, "u3t0", "u3t1")
                z, na = gate_in[:, :, 0, :], gate_in[:, :, 1, :]
                step(dve.tensor_tensor(z, proj_b[:, :, GATE_AT:GATE_AT + 8], spread(gate_bias.unsqueeze(1), NT, 8),
                                       ALU.add))
                step(dve.tensor_scalar(na, z, -1.0, None, ALU.mult))
                dve.tensor_tensor(na, na, z, ALU.min).then_inc(gate_abs, 1)
                copied(dve, plan, "u4t0", "u4t1")
                for t in range(NT):
                    step(dve.tensor_copy(qk[:, t, A_HEADS:, NOPE:],
                                         spread(proj_b[:, t, KR_AT:KR_AT + ROPE].unsqueeze(1), A_HEADS, ROPE)))
                dve.wait_ge(gate_ln, l + 1)
                dve.scalar_tensor_tensor(log_f, z[:, :, 4:8], 0.0, gate_in[:, :, 2, 4:8], ALU.min, ALU.subtract)\
                   .then_inc(log_f_ready, 1)
                rstds(1)
                step(dve.memset(conv_raw[hd, :, 0:3], 0.0))
                for t in range(NT):
                    step(dve.scalar_tensor_tensor(latent[:, t, 0:Q_RANK], proj_b[:, t, CQ_AT:CQ_AT + Q_RANK],
                                                  head_rstd[:, t:t + 1], latent_gain[:, 0:Q_RANK], ALU.mult, ALU.mult))
                    dve.scalar_tensor_tensor(latent[:, t, Q_RANK:], proj_b[:, t, CKV_AT:CKV_AT + KV_RANK],
                                             head_rstd[:, 2 + t:3 + t], latent_gain[:, Q_RANK:], ALU.mult, ALU.mult)\
                       .then_inc(latent_ready, 1)

                def diagonal(v):
                    dve.tensor_tensor(diag, spread(ident.unsqueeze(1), M_HEADS, P), spread(v.unsqueeze(2), M_HEADS, P),
                                      ALU.mult).then_inc(diag_ready, 1)

                def causal_max(name, t):
                    src = full(dve, plan, name)
                    dve.tensor_tensor(masked, src[:, :].rearrange("p (h s) -> p h s", h=M_HEADS),
                                      spread(const["causal"][:, P:].unsqueeze(1), M_HEADS, P), ALU.add)\
                       .then_inc(left(plan, name), 1)
                    copied(dve, plan, name)
                    step(dve.tensor_reduce(run_max[:, t, :], masked, AX.X, ALU.max))

                def decays(t):
                    name = f"mrow{t}"
                    src = full(dve, plan, name)[:, :].rearrange("p (h s) -> p h s", h=M_HEADS)
                    if t == 0:
                        step(dve.tensor_tensor(carry, cum[:, 0, 1, :],
                                               src[:, :, P - 1:P].rearrange("p h o -> p (h o)"), ALU.add))
                    dve.tensor_tensor(decay[:, t, :, :], spread(const["causal_t"].unsqueeze(1), M_HEADS, P), src,
                                      ALU.subtract).then_inc(left(plan, name), 1)
                    copied(dve, plan, name)
                    return dve.tensor_tensor(decay[:, t, :, :], decay[:, t, :, :],
                                             spread(rel[:, t, :].unsqueeze(2), M_HEADS, P), ALU.add)

                def convolve(i):
                    for pair, name in enumerate((("q01", "q23"), ("k01", "k23"))[i]):
                        copied(dve, plan, name)
                        for h in range(M_HEADS * i + 2 * pair, M_HEADS * i + 2 * pair + 2):
                            dst = conv_out[hd, h, :]
                            step(dve.tensor_scalar(dst, conv_raw[hd, h, 3:3 + SEQ], conv_w[hd, h, 3:4],
                                                   conv_w[hd, h, 4:5], ALU.mult, ALU.add))
                            for j in range(3):
                                ins = dve.scalar_tensor_tensor(dst, conv_raw[hd, h, j:j + SEQ], conv_w[hd, h, j:j + 1],
                                                               dst, ALU.mult, ALU.add)
                                if j < 2 or h % M_HEADS < M_HEADS - 1:
                                    step(ins)
                    ins.then_inc(conv_ready, 1)

                src = full(dve, plan, "cum")
                dve.tensor_copy(cum, src[:, 0:16].rearrange("p (t n h) -> p t n h", t=NT, n=2))\
                   .then_inc(left(plan, "cum"), 1)
                copied(dve, plan, "cum")
                step(dve.tensor_tensor(rel, z[:, :, 0:4], cum[:, :, 0, :], ALU.subtract))
                diagonal(rel[:, 0, :])
                causal_max("rrow0", 0)
                step(dve.tensor_scalar(run_max[:, 0, :], run_max[:, 0, :], 0.0, None, ALU.max))
                diagonal(rel[:, 1, :])
                causal_max("rrow1", 1)
                diagonal(run_max[:, 0, :])
                dve.wait_ge(gelu_ready, l + 1)
                gv = gelu[:, :, C_WIDTH:]
                v_square = place(small_at + 772, NT, C_WIDTH)
                v_groups = [gv[:, t, :].rearrange("p (g d) -> p g d", g=C_GROUPS) for t in range(NT)]
                step(dve.tensor_tensor(v_square, gv, gv, ALU.mult))
                dve.tensor_reduce(head_sums[:, 4:12].rearrange("p (t g) -> p t g", t=NT),
                                  v_square.rearrange("p t (g d) -> p t g d", g=C_GROUPS), AX.X, ALU.add)\
                   .then_inc(head_sums_ready, 1)
                rstds(2)
                for t in range(NT):
                    step(dve.tensor_tensor(v_groups[t], v_groups[t],
                                           spread(head_rstd[:, 4 + 4 * t:8 + 4 * t].unsqueeze(2), C_GROUPS, C_DIM),
                                           ALU.mult))
                dve.tensor_tensor(gv, gv, spread(cv_gain.unsqueeze(1), NT, C_WIDTH), ALU.mult)\
                   .then_inc(gate_v_ready, 1)
                convolve(0)
                decays(0).then_inc(decay_wanted, 1)
                step(dve.tensor_tensor(run_max[:, 1, :], run_max[:, 1, :], carry, ALU.max))
                diagonal(run_max[:, 1, :])
                step(dve.tensor_tensor(small_exp[:, 0, :], carry, run_max[:, 1, :], ALU.subtract))
                step(dve.tensor_tensor(small_exp[:, 1:3, :], cum[:, :, 0, :], run_max, ALU.add))
                step(dve.tensor_scalar(small_exp[:, 1:3, :], small_exp[:, 1:3, :], -1.0, None, ALU.mult))
                decays(1).then_inc(decay_wanted, 1)
                convolve(1)
                src = full(dve, plan, "gated")
                out_c = rows[:, :, M_WIDTH + A_WIDTH:]
                for t in range(NT):
                    o = out_c[:, t, :].rearrange("p (g d) -> p g d", g=C_GROUPS)
                    ins = dve.tensor_tensor(o, src[:, t * C_WIDTH:(t + 1) * C_WIDTH].rearrange("p (g d) -> p g d",
                                                                                              g=C_GROUPS),
                                            spread(cb.unsqueeze(2), C_GROUPS, C_DIM), ALU.add)
                    if t == 0:
                        step(ins)
                ins.then_inc(left(plan, "gated"), 1)
                copied(dve, plan, "gated")
                step(dve.tensor_tensor(out_c, out_c, gelu[:, :, 0:C_WIDTH], ALU.mult))
                for t in range(NT):
                    copied(dve, plan, f"q{t}a", f"q{t}b", f"kv{t}a", f"kv{t}b")
                    step(dve.tensor_copy(qk[:, t, A_HEADS:, 0:NOPE], kv[:, t, :, 0:NOPE]))
                    step(dve.tensor_tensor(qk_square, qk[:, t, :, :], qk[:, t, :, :], ALU.mult))
                    ins = dve.tensor_reduce(head_sums[:, 12 + 12 * t:24 + 12 * t], qk_square, AX.X, ALU.add)
                    if t == 0:
                        step(ins)
                ins.then_inc(head_sums_ready, 1)
                scale = float(M_DIM) ** -0.5
                dve.wait_ge(decay_done, 3 * (l + 1))
                keep = carry
                step(dve.tensor_copy(keep, decay[:, 0, :, P - 1:P].rearrange("p h o -> p (h o)")))
                for t in range(NT):
                    src = full(dve, plan, f"st{t}")
                    dve.scalar_tensor_tensor(decay[:, t, :, :], src[:, :].rearrange("p (h s) -> p h s", h=M_HEADS),
                                             scale, decay[:, t, :, :], ALU.mult, ALU.mult)\
                       .then_inc(left(plan, f"st{t}"), 1)
                    copied(dve, plan, f"st{t}")
                    dve.nop().then_inc(pt_ready, 1)
                src = full(dve, plan, "ktok")
                dve.scalar_tensor_tensor(k_weighted, src[:, 0:M_WIDTH].rearrange("p (h d) -> p h d", h=M_HEADS), scale,
                                         spread(keep.unsqueeze(2), M_HEADS, M_DIM), ALU.mult, ALU.mult)\
                   .then_inc(left(plan, "ktok"), 1)
                copied(dve, plan, "ktok")
                dve.nop().then_inc(kw_ready, 1)
                rstds(3)
                if l == 0:
                    dve.wait_ge(rope_ready, 1)
                n = 2 * A_HEADS
                half = ROPE // 2
                for t in range(NT):
                    heads = qk[:, t, :, :]
                    step(dve.tensor_tensor(heads, heads, spread(head_rstd[:, 12 + 12 * t:24 + 12 * t].unsqueeze(2), n,
                                                                QK_DIM), ALU.mult))
                    for i in range(2):
                        part = heads[:, A_HEADS * i:A_HEADS * (i + 1), :]
                        step(dve.tensor_tensor(part, part, spread(qk_gain[:, i, :].unsqueeze(1), A_HEADS, QK_DIM),
                                               ALU.mult))
                    a, b = heads[:, :, NOPE:NOPE + half], heads[:, :, NOPE + half:]
                    c = spread(cos_sin[:, 0, t, :].unsqueeze(1), n, half)
                    si = spread(cos_sin[:, 1, t, :].unsqueeze(1), n, half)
                    w = [rope_work[:, i, :, :] for i in range(4)]
                    step(dve.tensor_tensor(w[0], a, c, ALU.mult))
                    step(dve.tensor_tensor(w[1], b, si, ALU.mult))
                    step(dve.tensor_tensor(w[2], a, si, ALU.mult))
                    step(dve.tensor_tensor(w[3], b, c, ALU.mult))
                    step(dve.tensor_tensor(a, w[0], w[1], ALU.subtract))
                    dve.tensor_tensor(b, w[2], w[3], ALU.add).then_inc(qk_ready, 1)
                by_head = lambda b: b[:, 0:M_HEADS * (M_DIM + 1)].rearrange("p (h d) -> p h d", h=M_HEADS)
                src = by_head(full(dve, plan, "num0"))
                dve.tensor_copy(total[:, 0, :, :], src).then_inc(left(plan, "num0"), 1)
                copied(dve, plan, "num0")
                src = by_head(full(dve, plan, "inter"))
                dve.tensor_tensor(total[:, 1, :, :], src, spread(small_exp[:, 0, :].unsqueeze(2), M_HEADS, M_DIM + 1),
                                  ALU.mult).then_inc(left(plan, "inter"), 1)
                copied(dve, plan, "inter")
                src = by_head(full(dve, plan, "num1"))
                dve.tensor_tensor(total[:, 1, :, :], total[:, 1, :, :], src, ALU.add).then_inc(left(plan, "num1"), 1)
                copied(dve, plan, "num1")
                for t in range(NT):
                    n_q = total[:, t, :, M_DIM:].rearrange("p h o -> p (h o)")
                    d = den[:, t, 0, :]
                    step(dve.tensor_scalar(d, n_q, -1.0, None, ALU.mult))
                    step(dve.tensor_tensor(d, d, n_q, ALU.max))
                    step(dve.tensor_tensor(d, d, small_exp[:, 1 + t, :], ALU.max))
                    step(dve.reciprocal(den[:, t, 1, :], d))
                    step(dve.tensor_tensor(rows[:, t, 0:M_WIDTH].rearrange("p (h d) -> p h d", h=M_HEADS),
                                           total[:, t, :, 0:M_DIM], spread(den[:, t, 1, :].unsqueeze(2), M_HEADS, M_DIM),
                                           ALU.mult))
                dve.wait_ge(out_gate, l + 1)
                step(dve.tensor_tensor(rows[:, :, 0:M_WIDTH], rows[:, :, 0:M_WIDTH], proj_a[:, :, M_WIDTH:], ALU.mult))
                scale = float(QK_DIM) ** -0.5
                m_rows = rows[:, :, 0:M_WIDTH]
                m_square = place(diag_at, NT, M_WIDTH)
                c_square = place(diag_at + NT * M_WIDTH, NT, C_WIDTH)[:, :, :]
                a_square = place(diag_at, A_WIDTH)
                for h in range(A_HEADS):
                    src = full(dve, plan, f"sc{h}")
                    step(dve.scalar_tensor_tensor(prob[:, h % 2, 0:P], src[:, 0:P], scale, const["causal"][:, P:],
                                                  ALU.mult, ALU.add))
                    dve.scalar_tensor_tensor(prob[:, h % 2, P:], src[:, P:3 * P], scale, const["causal"],
                                             ALU.mult, ALU.add).then_inc(left(plan, f"sc{h}"), 1)
                    copied(dve, plan, f"sc{h}")
                    step(dve.tensor_reduce(soft[:, h, 0, 0:1], prob[:, h % 2, 0:P], AX.X, ALU.max))
                    step(dve.tensor_reduce(soft[:, h, 0, 1:2], prob[:, h % 2, P:], AX.X, ALU.max))
                    dve.tensor_scalar(soft[:, h, 0, :], soft[:, h, 0, :], -1.0, None, ALU.mult)\
                       .then_inc(logits_ready, 1)
                    if h == 0:
                        step(dve.tensor_tensor(m_square, m_rows, m_rows, ALU.mult))
                    elif h == 1:
                        step(dve.tensor_reduce(head_sums[:, 0:8].rearrange("p (t h) -> p t h", t=NT),
                                               m_square.rearrange("p t (h d) -> p t h d", h=M_HEADS), AX.X, ALU.add))
                        step(dve.tensor_tensor(c_square, out_c, out_c, ALU.mult))
                    elif h == 2:
                        dve.tensor_reduce(head_sums[:, 8:16].rearrange("p (t h) -> p t h", t=NT),
                                          c_square.rearrange("p t (h d) -> p t h d", h=C_GROUPS), AX.X, ALU.add)\
                           .then_inc(head_sums_ready, 1)
                    elif h == 3:
                        dve.wait_ge(loaded_gain, 16 * (3 * l + 2))
                        rstds(4)
                        for t in range(NT):
                            a = m_rows[:, t, :].rearrange("p (h d) -> p h d", d=M_DIM)
                            step(dve.tensor_tensor(a, a, spread(head_rstd[:, 4 * t:4 * t + 4].unsqueeze(2), M_HEADS,
                                                                M_DIM), ALU.mult))
                    elif h == 4:
                        step(dve.tensor_tensor(m_rows, m_rows, spread(gain[:, 0:M_WIDTH].unsqueeze(1), NT, M_WIDTH),
                                               ALU.mult))
                        for t in range(NT):
                            a = out_c[:, t, :].rearrange("p (h d) -> p h d", d=C_DIM)
                            step(dve.tensor_tensor(a, a, spread(head_rstd[:, 8 + 4 * t:12 + 4 * t].unsqueeze(2),
                                                                C_GROUPS, C_DIM), ALU.mult))
                    else:
                        step(dve.tensor_tensor(out_c, out_c, spread(gain[:, M_WIDTH + A_WIDTH:].unsqueeze(1), NT,
                                                                    C_WIDTH), ALU.mult))
                dve.wait_ge(prob_ready, NT * A_HEADS * (l + 1))
                step(dve.reciprocal(soft[:, :, 1, :], soft[:, :, 1, :]))
                for t in range(NT):
                    src = full(dve, plan, f"o{t}")
                    dve.tensor_tensor(rows[:, t, M_WIDTH:M_WIDTH + A_WIDTH].rearrange("p (h d) -> p h d", h=A_HEADS),
                                      src[:, 0:A_WIDTH].rearrange("p (h d) -> p h d", h=A_HEADS),
                                      spread(soft[:, :, 1, t:t + 1], A_HEADS, V_DIM), ALU.mult)\
                       .then_inc(left(plan, f"o{t}"), 1)
                    copied(dve, plan, f"o{t}")
                for t in range(NT):
                    a = rows[:, t, M_WIDTH:M_WIDTH + A_WIDTH]
                    step(dve.tensor_tensor(a_square, a, a, ALU.mult))
                    dve.tensor_reduce(head_sums[:, 16 + 6 * t:22 + 6 * t],
                                      a_square.rearrange("p (h d) -> p h d", d=V_DIM), AX.X, ALU.add)\
                       .then_inc(head_sums_ready, 1)
                    dve.wait_ge(head_sums_ready, 5 * l + 4 + t)
                for t in range(NT):
                    rstds(5 + t)
                    a = rows[:, t, M_WIDTH:M_WIDTH + A_WIDTH]
                    h = a.rearrange("p (h d) -> p h d", d=V_DIM)
                    step(dve.tensor_tensor(h, h, spread(head_rstd[:, 16 + 6 * t:22 + 6 * t].unsqueeze(2), A_HEADS,
                                                        V_DIM), ALU.mult))
                    dve.tensor_tensor(a, a, gain[:, M_WIDTH:M_WIDTH + A_WIDTH], ALU.mult).then_inc(y_rows, 1)
                for n in range(2):
                    for t in range(NT):
                        name = f"out{2 * t + n}"
                        src = full(dve, plan, name)
                        xs = x[:, t, n * HALF:(n + 1) * HALF]
                        dve.tensor_tensor(xs, xs, src[:, :], ALU.add).then_inc(left(plan, name), 1)
                        copied(dve, plan, name)
                        if (t, n) == (0, 1):
                            dve.nop().then_inc(x_tile_ready, 1)
                dve.nop().then_inc(x_ready, 1)

            dve.wait_ge(loaded_consts, 16)
            for t in range(NT):
                dve.wait_ge(loaded_x[t], 16)
            for l in range(DEPTH):
                if mixer:
                    norm(PER * l, "p (k i) -> p k i", 3 * l + 1)
                    if l == 0:
                        rope_tables()
                    mix(l)
                norm(PER * (l + 1) - 1, "p (i k) -> p k i", 3 * (l + 1) if mixer else l + 1)
                dve.wait_ge(xf_ready, NT * PER * (l + 1))
                step(dve.tensor_copy(xf_parts[0], xf[:, :, :, :]))
                dve.tensor_tensor(xf_rest, xf[:, :, :, :], xf_parts[0], ALU.subtract).then_inc(rest_ready, 1)
                dve.wait_ge(loaded_ffn, ROUTER_LOADS * (l + 1))
                route(l)
                it0 = l * (PAIRS // 2 + 1)
                link = Chain(dve, main["vec"], l * LAYER_LINKS)
                for i in range(2):
                    step(dve.tensor_scalar(slots_gathered[:, i * P:(i + 1) * P], const["iota"], float(i * P), None,
                                           ALU.add))
                plain_hot(it0, main, link)
                finish_route(l)
                step(dve.tensor_copy(slots_weighted[:, :], const["iota"]))
                weighted_hot(0, link)
                overflow(l)
                with dve.Fori(0, PAIRS // 2) as j:
                    for par in range(2):
                        expert_pair(par, j + it0, 2 * j + (l * PAIRS + par), main,
                                    LOOP_LINKS * j + (l * LAYER_LINKS + (1 + par) * (PLAIN_LINKS + WEIGHTED_LINKS)))
                n_over = dve.value_load(overint[0:1, l, CELLS_OVER:CELLS_OVER + 1], min_val=0, max_val=2)
                with dve.If(n_over > 0):
                    S = extra[l]
                    dve.nop().then_inc(S["hot_ready"], 1)
                    dve.wait_ge(main["gathered"], 4 * it0 + 4 * (PAIRS // 2 + 1))
                    with dve.Fori(0, n_over) as j:
                        for par in range(2):
                            expert_pair(par, j, 2 * j + par, S,
                                        LOOP_LINKS * j + par * (PLAIN_LINKS + WEIGHTED_LINKS))
                with dve.Else():
                    dve.nop()
                dve.wait_ge(acc_done, l + 1)
                for t in range(NT):
                    for n in range(2):
                        xs = x[:, t, n * HALF:(n + 1) * HALF]
                        ins = dve.tensor_tensor(xs, xs, bank[2 * t + n][:, :], ALU.add)
                        if (t, n) != (NT - 1, 1):
                            step(ins)
                    if t == 0:
                        dve.nop().then_inc(x_tile_ready, 1)
                ins.then_inc(x_ready, 1)

            def last_block():
                plan = plan2
                rows = xf[:, :, :, :].rearrange("p t k i -> p t (k i)")

                def spread(ap, *shape):
                    return ap.broadcast_to([P, *shape])

                n = 2 * S_HEADS
                for t in range(NT):
                    copied(dve, plan, f"qa{t}", f"ka{t}")
                    step(dve.tensor_tensor(s_square, s_qk[:, t, :], s_qk[:, t, :], ALU.mult))
                    ins = dve.tensor_reduce(s_sums[:, n * t:n * (t + 1)],
                                            s_square.rearrange("p (h d) -> p h d", h=n), AX.X, ALU.add)
                    if t == 0:
                        step(ins)
                ins.then_inc(s_sums_ready, 1)
                dve.wait_ge(loaded_second, 4 * 16)
                dve.memset(s_rel[0:S_HEADS, 32:33], NEG).then_inc(rel_ready, 1)
                src = full(dve, plan, "rel")
                dve.tensor_copy(s_relT[0:33, :], src[0:33, 0:S_HEADS]).then_inc(left(plan, "rel"), 1)
                src = full(dve, plan, "f")
                dve.tensor_copy(s_f[0:S_HEADS, :], src[0:S_HEADS, 0:384]).then_inc(left(plan, "f"), 1)
                copied(dve, plan, "f")
                dve.nop().then_inc(f_ready, 1)
                dve.wait_ge(s_rstd_ready, 1)
                for t in range(NT):
                    heads = s_qk[:, t, :].rearrange("p (h d) -> p h d", h=n)
                    step(dve.tensor_tensor(heads, heads, spread(s_rstd[:, n * t:n * (t + 1)].unsqueeze(2), n, S_DIM),
                                           ALU.mult))
                    for a in range(2):
                        part = heads[:, a * S_HEADS:(a + 1) * S_HEADS, :]
                        step(dve.tensor_tensor(part, part, spread(s_gain[:, a, :].unsqueeze(1), S_HEADS, S_DIM),
                                               ALU.mult))
                dve.nop().then_inc(s_qk_ready, 1)

                def merge_tile(name):
                    if name[0] != "g":
                        return
                    t = int(name[-1])
                    at = "ab".index(name[1]) * D + int(name[2]) * HALF
                    src = full(dve, plan, name)
                    dve.tensor_tensor(s_gates[:, t, at:at + HALF], src[:, :],
                                      xf[:, :, :, :].rearrange("p t k i -> p (t k i)")[:, at:at + HALF], ALU.add)\
                       .then_inc(left(plan, name), 1)

                scale = float(S_DIM) ** -0.5
                dve.wait_ge(bias_loaded, 16)
                dve.wait_ge(loaded_merge_bias, 16)
                for h in range(S_HEADS + 1):
                    front, back = step_tiles(h)
                    if h < S_HEADS:
                        src = full(dve, plan, f"sc{h}")
                        if h >= 2:
                            full(dve, plan, f"pT{h - 2}")
                        p = s_prob[:, h % 2, :]
                        step(dve.scalar_tensor_tensor(p[:, 0:P], src[:, 0:P], scale, s_bias[:, h, P:],
                                                      ALU.mult, ALU.add))
                        dve.scalar_tensor_tensor(p[:, P:], src[:, P:3 * P], scale, s_bias[:, h, :],
                                                 ALU.mult, ALU.add).then_inc(left(plan, f"sc{h}"), 1)
                        copied(dve, plan, f"sc{h}")
                        step(dve.tensor_reduce(s_soft[:, h, 0, 0:1], p[:, 0:P], AX.X, ALU.max))
                        step(dve.tensor_reduce(s_soft[:, h, 0, 1:2], p[:, P:], AX.X, ALU.max))
                        dve.tensor_scalar(s_soft[:, h, 0, :], s_soft[:, h, 0, :], -1.0, None, ALU.mult)\
                           .then_inc(s_logits_ready, 1)
                        dve.wait_ge(s_ln_ready, h + 1)
                        log = s_log[:, h % 2, :]
                        src = full(dve, plan, f"z{h}")
                        dve.scalar_tensor_tensor(log, src[:, 0:3 * P], 0.0, log, ALU.max, ALU.add)\
                           .then_inc(left(plan, f"z{h}"), 1)
                        copied(dve, plan, f"z{h}")
                        step(dve.tensor_tensor(log[:, 0:SEQ], log[:, 0:SEQ], past_neg, ALU.mult))
                        dve.tensor_tensor(log[:, SEQ:], log[:, SEQ:], past_neg[:, 0:P], ALU.mult)\
                           .then_inc(s_log_ready, 1)
                    for name in front:
                        merge_tile(name)
                    if h:
                        g = h - 1
                        log = s_log[:, g % 2, :]
                        src = full(dve, plan, f"r{g}")
                        step(dve.tensor_tensor(log[:, 0:SEQ], src[:, 0:SEQ], past_add, ALU.add))
                        dve.tensor_tensor(log[:, SEQ:], src[:, SEQ:3 * P], past_add[:, 0:P], ALU.add)\
                           .then_inc(left(plan, f"r{g}"), 1)
                    for name in back:
                        merge_tile(name)
                    if h:
                        c = slice(g * S_DIM, (g + 1) * S_DIM)
                        src = full(dve, plan, f"ob{g}")
                        dve.tensor_copy(s_o[:, 1, :, c], src[:, 0:P].rearrange("p (t d) -> p t d", t=NT))\
                           .then_inc(left(plan, f"ob{g}"), 1)
                        step(dve.reciprocal(s_soft[:, g, 1, :], s_soft[:, g, 1, :]))
                        src = full(dve, plan, f"oa{g}")
                        dve.tensor_tensor(s_o[:, 0, :, c], src[:, 0:P].rearrange("p (t d) -> p t d", t=NT),
                                          spread(s_soft[:, g, 1, :].unsqueeze(2), NT, S_DIM), ALU.mult)\
                           .then_inc(left(plan, f"oa{g}"), 1)
                        copied(dve, plan, f"ob{g}", f"oa{g}")
                for name in TILES[4:]:
                    copied(dve, plan, name)
                dve.nop().then_inc(s_gates_in, 1)
                dve.wait_ge(s_silu_ready, 1)
                for a in range(2):
                    for t in range(NT):
                        dve.tensor_tensor(s_o[:, a, t, :], s_o[:, a, t, :], s_z[:, a, t, :], ALU.mult)\
                           .then_inc(s_o_ready, 1)
                dve.wait_ge(s_gate_ready, 1)
                for t in range(NT):
                    for n in range(2):
                        at = n * HALF
                        dst = rows[:, t, at:at + HALF]
                        src = full(dve, plan, f"ya{t}{n}")
                        dve.tensor_tensor(dst, s_gates[:, t, at:at + HALF], src[:, :], ALU.mult)\
                           .then_inc(left(plan, f"ya{t}{n}"), 1)
                        src = full(dve, plan, f"yb{t}{n}")
                        g = s_gates[:, t, D + at:D + at + HALF]
                        dve.tensor_tensor(g, g, src[:, :], ALU.mult).then_inc(left(plan, f"yb{t}{n}"), 1)
                        copied(dve, plan, f"ya{t}{n}", f"yb{t}{n}")
                        ins = dve.tensor_tensor(dst, dst, g, ALU.add)
                        if n == 0:
                            step(ins)
                    ins.then_inc(s_rows, 1)
                for n in range(2):
                    for t in range(NT):
                        name = f"out{2 * t + n}"
                        src = full(dve, plan, name)
                        xs = x[:, t, n * HALF:(n + 1) * HALF]
                        dve.tensor_tensor(xs, xs, src[:, :], ALU.add).then_inc(left(plan, name), 1)
                        copied(dve, plan, name)
                        if (t, n) == (0, 1):
                            dve.nop().then_inc(x_tile_ready, 1)
                dve.nop().then_inc(x_ready, 1)

            if second:
                norm(PER * DEPTH, "p (k i) -> p k i", 3 * DEPTH + 1)
                last_block()


_INS = ["x", "positions", "attn_norm", "w_in", "m_conv_w", "m_conv_b", "m_gate_bias", "a_q_norm", "a_kv_norm",
        "a_w_uq", "a_w_ukv", "a_q_head_norm", "a_k_head_norm", "c_v_norm", "c_w_s", "c_b_s", "mix_out_norm",
        "w_out", "ffn_norm", "w_group", "b_group", "w_expert", "b_expert", "w1", "w3", "w2",
        "norm_w_2", "w_in_2", "merge_gate_b_2", "q_norm_w_2", "k_norm_w_2", "rel_bias_2", "w_up_moba_2",
        "w_up_sb_2", "w_out_2"]
_OUTS = [((1, SEQ, D), "float32")]


def kernel(**inputs):
    import concourse.bacc as _bacc
    from concourse.bass_utils import run_bass_kernel_spmd as _run

    nc = _bacc.Bacc("TRN2", target_bir_lowering=False, num_devices=1)
    arrays = {name: np.ascontiguousarray(inputs[name]) for name in _INS}
    arrays["consts"], arrays["late_consts"] = constant_table()
    io = {name: nc.dram_tensor(f"in_{name}", a.shape, mybir.dt.from_np(a.dtype), kind="ExternalInput").ap()
          for name, a in arrays.items()}
    shape, dtype = _OUTS[0]
    out = nc.dram_tensor("out_0", shape, mybir.dt.from_np(np.dtype(dtype)), kind="ExternalOutput").ap()
    program(nc, io, out)
    r = _run(nc, [{f"in_{name}": a for name, a in arrays.items()}], core_ids=[0])
    return r.results[0]["out_0"]
```
